# Optimizing a Trainium2 kernel written in Bass

```python
import jax, jax.numpy as jnp
from jax import lax
import numpy as np

D_MODEL = 1024
BATCH = 1
SEQ = 256
DEPTH = 2
DEC_BATCH = 8
DEC_SEQ = 8
PAST_LEN = 1024
PAGE_SIZE = 128

N_A = DEPTH // 2
N_B = DEPTH - N_A
GLA_HEADS = 4
GLA_DK = D_MODEL // 2
GLA_DV = D_MODEL
GLA_DKH = GLA_DK // GLA_HEADS
GLA_DVH = GLA_DV // GLA_HEADS
GLA_GATE_RANK = 16
GLA_GATE_TAU = 16.0
GLA_CHUNK = 64
GLA_IN = 2 * GLA_DK + 2 * GLA_DV + GLA_GATE_RANK
FOX_HEADS = 8
FOX_HD = D_MODEL // FOX_HEADS
FOX_DIM = FOX_HEADS * FOX_HD
FOX_BLOCK_Q = 128
FOX_BF_MIN = 2.0
FOX_BF_MAX = 12.0
KV_OUT = 2 * FOX_DIM + FOX_HEADS
N_EXPERTS = 64
TOP_K = 8
N_GROUPS = 8
TOPK_GROUPS = 4
D_EXPERT = 256
D_SHARED = 256
ROUTED_SCALE = 2.5
EXPERT_BLOCK = 128
DEEPNORM_ALPHA = (2 * DEPTH) ** 0.25
DEEPNORM_BETA = (8 * DEPTH) ** -0.25
LN_EPS = 1e-5
RMS_EPS = 1e-6

kernel_name = 'yoco_gla_fox_moe_decoder_step'

def _layer_norm(x, g, b):
    xf = x.astype(jnp.float32)
    xc = xf - jnp.mean(xf, -1, keepdims=True)
    var = jnp.mean(xc * xc, -1, keepdims=True)
    return (xc * lax.rsqrt(var + LN_EPS) * g.astype(jnp.float32) + b.astype(jnp.float32)).astype(x.dtype)

def _gla_chunked(q, k, v, log_a, s0):
    B, T, H, dk = q.shape
    dv = v.shape[-1]
    c = min(GLA_CHUNK, T)
    n = -(-T // c)
    pad = n * c - T

    def blocks(a):
        a = jnp.pad(a, ((0, 0), (0, pad), (0, 0), (0, 0)))
        return a.reshape(B, n, c, H, a.shape[-1]).transpose(1, 0, 3, 2, 4)

    qb, kb, vb, ab = blocks(q), blocks(k), blocks(v), blocks(log_a)
    bcum = jnp.cumsum(ab, axis=3)
    causal = jnp.tril(jnp.ones((c, c), dtype=bool))

    def step(S, inp):
        qc, kc, vc, bc = inp
        b_last = bc[:, :, -1:, :]
        q_dec = qc * jnp.exp(bc)
        k_dec = kc * jnp.exp(-bc)
        inter = jnp.einsum('bhcd,bhde->bhce', q_dec, S)
        att = jnp.where(causal, jnp.einsum('bhcd,bhsd->bhcs', q_dec, k_dec), 0.0)
        intra = jnp.einsum('bhcs,bhse->bhce', att, vc)
        S_new = S * jnp.exp(b_last[:, :, 0, :, None]) + jnp.einsum('bhsd,bhse->bhde', kc * jnp.exp(b_last - bc), vc)
        return S_new, inter + intra

    S_T, o = lax.scan(step, s0, (qb, kb, vb, bcum))
    o = o.transpose(1, 0, 3, 2, 4).reshape(B, n * c, H, dv)[:, :T]
    return o, S_T

def _gla_mixer(u, s0, w_in, w_a2, b_a, norm_g, w_o):
    B, T, _ = u.shape
    p = u @ w_in
    q, k, v, g, a_lr = jnp.split(p, [GLA_DK, 2 * GLA_DK, 2 * GLA_DK + GLA_DV, 2 * GLA_DK + 2 * GLA_DV], axis=-1)
    log_a = jax.nn.log_sigmoid((a_lr @ w_a2 + b_a).astype(jnp.float32)) / GLA_GATE_TAU
    qh = q.astype(jnp.float32).reshape(B, T, GLA_HEADS, GLA_DKH) * (GLA_DKH ** -0.5)
    kh = k.astype(jnp.float32).reshape(B, T, GLA_HEADS, GLA_DKH)
    vh = v.astype(jnp.float32).reshape(B, T, GLA_HEADS, GLA_DVH)
    o, s_T = _gla_chunked(qh, kh, vh, log_a.reshape(B, T, GLA_HEADS, GLA_DKH), s0.astype(jnp.float32))
    o = o * lax.rsqrt(jnp.mean(o * o, -1, keepdims=True) + RMS_EPS) * norm_g.astype(jnp.float32)
    o = o.reshape(B, T, GLA_DV) * jax.nn.silu(g.astype(jnp.float32))
    return o.astype(u.dtype) @ w_o, s_T

def _shared_kv(x, silu_c, kv_w_mod, kv_b_mod, kv_w, fox_b_f):
    B, T, _ = x.shape
    m = (silu_c @ kv_w_mod + kv_b_mod)[:, None, :]
    sh, sc = jnp.split(m, 2, axis=-1)
    p = (x * (1 + sc) + sh) @ kv_w
    k = p[..., :FOX_DIM].reshape(B, T, FOX_HEADS, FOX_HD)
    v = p[..., FOX_DIM:2 * FOX_DIM].reshape(B, T, FOX_HEADS, FOX_HD)
    logf = jax.nn.log_sigmoid(p[..., 2 * FOX_DIM:].astype(jnp.float32) + fox_b_f.astype(jnp.float32))
    return k, v, logf

def _fox_context(k_new, v_new, logf_new, past):
    f_new = jnp.cumsum(logf_new, axis=1)
    if past is None:
        return k_new, v_new, f_new, f_new, 0
    k_past, v_past, logf_past = past
    lf = logf_past.astype(jnp.float32)
    suffix = lax.cumsum(lf, axis=1, reverse=True) - lf
    k_all = jnp.concatenate([k_past.astype(k_new.dtype), k_new], axis=1)
    v_all = jnp.concatenate([v_past.astype(v_new.dtype), v_new], axis=1)
    return k_all, v_all, f_new, jnp.concatenate([-suffix, f_new], axis=1), k_past.shape[1]

def _forgetting_attention(q, k, v, fq, fk, q_off):
    Tq, hd = q.shape[1], q.shape[3]
    scale = hd ** -0.5
    outs = []
    for a in range(0, Tq, FOX_BLOCK_Q):
        b = min(a + FOX_BLOCK_Q, Tq)
        nk = q_off + b
        s = jnp.einsum('bqhd,bkhd->bhqk', q[:, a:b], k[:, :nk], preferred_element_type=jnp.float32) * scale
        s = s + jnp.swapaxes(fq[:, a:b], 1, 2)[..., None] - jnp.swapaxes(fk[:, :nk], 1, 2)[:, :, None, :]
        mask = jnp.arange(nk)[None, :] <= (q_off + jnp.arange(a, b))[:, None]
        p = jax.nn.softmax(jnp.where(mask, s, -jnp.inf), axis=-1)
        outs.append(jnp.einsum('bhqk,bkhd->bqhd', p.astype(v.dtype), v[:, :nk], preferred_element_type=jnp.float32))
    return jnp.concatenate(outs, axis=1)

def _fox_mixer(u, ctx, w_q, w_o):
    k, v, fq, fk, q_off = ctx
    B, T, _ = u.shape
    q = (u @ w_q).reshape(B, T, FOX_HEADS, FOX_HD)
    o = _forgetting_attention(q, k, v, fq, fk, q_off)
    return o.reshape(B, T, FOX_DIM).astype(u.dtype) @ w_o

def _swiglu(x, wg, wu, wd):
    return (jax.nn.silu(x @ wg) * (x @ wu)) @ wd

def _route(xf, w_router, router_bias):
    N = xf.shape[0]
    s = jax.nn.sigmoid((xf @ w_router).astype(jnp.float32))
    sb = s + router_bias.astype(jnp.float32)
    g_score = lax.top_k(sb.reshape(N, N_GROUPS, N_EXPERTS // N_GROUPS), 2)[0].sum(-1)
    _, g_idx = lax.top_k(g_score, TOPK_GROUPS)
    g_mask = (g_idx[..., None] == jnp.arange(N_GROUPS)).any(axis=1)
    e_mask = jnp.repeat(g_mask, N_EXPERTS // N_GROUPS, axis=1)
    _, idx = lax.top_k(jnp.where(e_mask, sb, -jnp.inf), TOP_K)
    w = jnp.take_along_axis(s, idx, axis=-1)
    w = w / jnp.sum(w, -1, keepdims=True) * ROUTED_SCALE
    return idx, w

def _routed_experts(xf, idx, w, w_gate, w_up, w_down):
    N, D = xf.shape
    M = N * TOP_K
    flat_e = idx.reshape(-1)
    order = jnp.argsort(flat_e)
    se = flat_e[order]
    counts = jnp.bincount(flat_e, length=N_EXPERTS)
    padded = (counts + EXPERT_BLOCK - 1) // EXPERT_BLOCK * EXPERT_BLOCK
    pad_end = jnp.cumsum(padded)
    pad_start = pad_end - padded
    grp_start = jnp.cumsum(counts) - counts
    dest = pad_start[se] + jnp.arange(M) - grp_start[se]
    n_blocks = -(-M // EXPERT_BLOCK) + N_EXPERTS
    R = n_blocks * EXPERT_BLOCK
    row_tok = jnp.zeros((R,), jnp.int32).at[dest].set((order // TOP_K).astype(jnp.int32))
    row_w = jnp.zeros((R,), jnp.float32).at[dest].set(w.reshape(-1)[order])
    block_e = jnp.minimum(jnp.searchsorted(pad_end, jnp.arange(n_blocks) * EXPERT_BLOCK, side='right'), N_EXPERTS - 1)

    def block_fn(args):
        toks, e = args
        xb = xf[toks]
        return _swiglu(xb, w_gate[e], w_up[e], w_down[e])

    yb = lax.map(block_fn, (row_tok.reshape(n_blocks, EXPERT_BLOCK), block_e))
    return jax.ops.segment_sum(yb.reshape(R, D) * row_w[:, None], row_tok, num_segments=N)

def _moe(u, router_w, router_bias, w_gate, w_up, w_down, sh_gate, sh_up, sh_down):
    B, T, D = u.shape
    xf = u.reshape(B * T, D)
    idx, w = _route(xf, router_w, router_bias)
    routed = _routed_experts(xf, idx, w, w_gate, w_up, w_down)
    return (routed.astype(u.dtype) + _swiglu(xf, sh_gate, sh_up, sh_down)).reshape(B, T, D)

def _trunk(x, c, gla_s0, past, W):
    silu_c = jax.nn.silu(c.astype(jnp.float32)).astype(x.dtype)
    new_gla = []
    ctx = None
    for l in range(DEPTH):
        mod = (silu_c @ W['ada_w'][l] + W['ada_b'][l])[:, None, :]
        sh_a, sc_a, g_a, sh_m, sc_m, g_m = jnp.split(mod, 6, axis=-1)
        u = x * (1 + sc_a) + sh_a
        if l < N_A:
            out, s_T = _gla_mixer(u, gla_s0[l], W['gla_w_in'][l], W['gla_w_a2'][l], W['gla_b_a'][l],
                                  W['gla_norm_g'][l], W['gla_w_o'][l])
            new_gla.append(s_T)
        else:
            out = _fox_mixer(u, ctx, W['fox_w_q'][l - N_A], W['fox_w_o'][l - N_A])
        x = _layer_norm(DEEPNORM_ALPHA * x + (1 + g_a) * out, W['ln_g'][l, 0], W['ln_b'][l, 0])
        u = x * (1 + sc_m) + sh_m
        y = _moe(u, W['router_w'][l], W['router_bias'][l], W['exp_w_gate'][l], W['exp_w_up'][l],
                 W['exp_w_down'][l], W['sh_w_gate'][l], W['sh_w_up'][l], W['sh_w_down'][l])
        x = _layer_norm(DEEPNORM_ALPHA * x + (1 + g_m) * y, W['ln_g'][l, 1], W['ln_b'][l, 1])
        if l == N_A - 1:
            k_new, v_new, logf_new = _shared_kv(x, silu_c, W['kv_w_mod'], W['kv_b_mod'], W['kv_w'], W['fox_b_f'])
            ctx = _fox_context(k_new, v_new, logf_new, past)
    return x, jnp.stack(new_gla), k_new, v_new, logf_new

def setup_inputs(seed: int = 0) -> dict:
    key = jax.random.key(seed)
    ks = jax.random.split(key, 32)
    f32 = jnp.float32

    def nrm(i, shape, scale=1.0):
        return jax.random.normal(ks[i], shape, f32) * scale

    n_pages = PAST_LEN // PAGE_SIZE
    n_used = DEC_BATCH * n_pages
    n_phys = n_used + max(n_used // 4, 1)
    d = D_MODEL
    head_bias = jnp.linspace(FOX_BF_MIN, FOX_BF_MAX, FOX_HEADS, dtype=f32)
    return {
        'x_prompt': nrm(0, (BATCH, SEQ, d)),
        'x_sample': nrm(1, (DEC_BATCH, DEC_SEQ, d)),
        'c_prompt': nrm(2, (BATCH, d)),
        'c_sample': nrm(3, (DEC_BATCH, d)),
        'state_gla': nrm(4, (N_A, DEC_BATCH, GLA_HEADS, GLA_DKH, GLA_DVH), 0.5),
        'cache_k': nrm(5, (n_phys, PAGE_SIZE, FOX_HEADS, FOX_HD)),
        'cache_v': nrm(6, (n_phys, PAGE_SIZE, FOX_HEADS, FOX_HD)),
        'cache_logf': jax.nn.log_sigmoid(head_bias + nrm(7, (n_phys, PAGE_SIZE, FOX_HEADS), 0.5)),
        'page_table': jax.random.permutation(ks[8], n_phys)[:n_used].reshape(DEC_BATCH, n_pages).astype(jnp.int32),
        'gla_w_in': nrm(9, (N_A, d, GLA_IN), d ** -0.5),
        'gla_w_a2': nrm(10, (N_A, GLA_GATE_RANK, GLA_DK), GLA_GATE_RANK ** -0.5),
        'gla_b_a': nrm(11, (N_A, GLA_DK), 0.1),
        'gla_norm_g': 1.0 + nrm(12, (N_A, GLA_DVH), 0.02),
        'gla_w_o': nrm(13, (N_A, GLA_DV, d), GLA_DV ** -0.5 * DEEPNORM_BETA),
        'kv_w_mod': nrm(14, (d, 2 * d), 0.1 * d ** -0.5),
        'kv_b_mod': nrm(15, (2 * d,), 0.01),
        'kv_w': nrm(16, (d, KV_OUT), d ** -0.5),
        'fox_b_f': head_bias + nrm(17, (FOX_HEADS,), 0.1),
        'fox_w_q': nrm(18, (N_B, d, FOX_DIM), d ** -0.5),
        'fox_w_o': nrm(19, (N_B, FOX_DIM, d), FOX_DIM ** -0.5 * DEEPNORM_BETA),
        'ada_w': nrm(20, (DEPTH, d, 6 * d), 0.1 * d ** -0.5),
        'ada_b': nrm(21, (DEPTH, 6 * d), 0.01),
        'ln_g': 1.0 + nrm(22, (DEPTH, 2, d), 0.02),
        'ln_b': nrm(23, (DEPTH, 2, d), 0.01),
        'router_w': nrm(24, (DEPTH, d, N_EXPERTS), d ** -0.5),
        'router_bias': nrm(25, (DEPTH, N_EXPERTS), 0.01),
        'exp_w_gate': nrm(26, (DEPTH, N_EXPERTS, d, D_EXPERT), d ** -0.5),
        'exp_w_up': nrm(27, (DEPTH, N_EXPERTS, d, D_EXPERT), d ** -0.5),
        'exp_w_down': nrm(28, (DEPTH, N_EXPERTS, D_EXPERT, d), D_EXPERT ** -0.5 * DEEPNORM_BETA),
        'sh_w_gate': nrm(29, (DEPTH, d, D_SHARED), d ** -0.5),
        'sh_w_up': nrm(30, (DEPTH, d, D_SHARED), d ** -0.5),
        'sh_w_down': nrm(31, (DEPTH, D_SHARED, d), D_SHARED ** -0.5 * DEEPNORM_BETA),
    }

def reference(x_prompt, x_sample, c_prompt, c_sample, state_gla, cache_k, cache_v, cache_logf, page_table,
              gla_w_in, gla_w_a2, gla_b_a, gla_norm_g, gla_w_o, kv_w_mod, kv_b_mod, kv_w, fox_b_f,
              fox_w_q, fox_w_o, ada_w, ada_b, ln_g, ln_b, router_w, router_bias,
              exp_w_gate, exp_w_up, exp_w_down, sh_w_gate, sh_w_up, sh_w_down):
    W = dict(gla_w_in=gla_w_in, gla_w_a2=gla_w_a2, gla_b_a=gla_b_a, gla_norm_g=gla_norm_g, gla_w_o=gla_w_o,
             kv_w_mod=kv_w_mod, kv_b_mod=kv_b_mod, kv_w=kv_w, fox_b_f=fox_b_f, fox_w_q=fox_w_q, fox_w_o=fox_w_o,
             ada_w=ada_w, ada_b=ada_b, ln_g=ln_g, ln_b=ln_b, router_w=router_w, router_bias=router_bias,
             exp_w_gate=exp_w_gate, exp_w_up=exp_w_up, exp_w_down=exp_w_down,
             sh_w_gate=sh_w_gate, sh_w_up=sh_w_up, sh_w_down=sh_w_down)
    s0_prompt = jnp.zeros((N_A, x_prompt.shape[0], GLA_HEADS, GLA_DKH, GLA_DVH), jnp.float32)
    y_prompt, gla_prompt, k_prompt, v_prompt, logf_prompt = _trunk(x_prompt, c_prompt, s0_prompt, None, W)
    db, n_pages = page_table.shape
    past_len = n_pages * PAGE_SIZE
    past = (cache_k[page_table].reshape(db, past_len, FOX_HEADS, FOX_HD),
            cache_v[page_table].reshape(db, past_len, FOX_HEADS, FOX_HD),
            cache_logf[page_table].reshape(db, past_len, FOX_HEADS))
    y_sample, gla_sample, k_sample, v_sample, logf_sample = _trunk(x_sample, c_sample, state_gla, past, W)
    return (y_prompt, y_sample, gla_prompt, gla_sample, k_prompt, v_prompt, logf_prompt, k_sample, v_sample, logf_sample)


_drawn_inputs = setup_inputs


def setup_inputs(seed=0):
    import zlib

    import numpy as np

    out = dict(_drawn_inputs(seed))
    spreads = {}
    factors = {'kv_b_mod': 3.894}
    for name, (base, spread) in spreads.items():
        noise = np.random.default_rng([zlib.crc32(name.encode()), seed]).standard_normal(out[name].shape)
        drawn = base * np.exp(spread * noise) if base else spread * noise
        out[name] = __import__('jax').numpy.asarray(drawn.astype(out[name].dtype))
    for name, factor in factors.items():
        out[name] = (out[name] * factor).astype(out[name].dtype)
    return out
```

```python
from contextlib import ExitStack

import concourse.bass as bass
import numpy as np
from concourse import mybir

F32 = mybir.dt.float32
I32 = mybir.dt.int32
ALU = mybir.AluOpType
ACT = mybir.ActivationFunctionType
AX = mybir.AxisListType.X
ds = bass.ds

P = 128
D = 1024
KT = D // P
SEQ, DB, DT = 256, 8, 8
TOK = SEQ + DB * DT
TILES = [(0, 128), (128, 128), (256, 64)]
ST = 2
GH, GK, GV, RANK, CHUNK = 4, 128, 256, 16, 64
GD = GH * GK
TAU = 16.0
FH, HD = 8, 128
PAGES, PAGE = 8, 128
PAST = PAGES * PAGE
CTX = PAST + DT
NE, TOPK, NG, TOPG, FE = 64, 8, 8, 4, 256
CAP = 64
BLOCKS = TOK // CAP
OVER = (TOK * TOPK) // (CAP + 1)
ALPHA = 4.0 ** 0.25
LN_EPS, RMS_EPS = 1e-5, 1e-6
ROUTED = 2.5
NOBODY = 1 << 20
NEG = -1e30
ADA_N = 28
W_IN_N = 3072
UNIT = 2048
UNITS = 9

MOD_CHUNK = {("shift_a", 0): 0, ("scale_a", 0): 2, ("gate_a", 0): 4, ("shift_m", 0): 6, ("scale_m", 0): 8,
             ("gate_m", 0): 10, ("shift_a", 1): 12, ("scale_a", 1): 14, ("gate_a", 1): 16, ("shift_m", 1): 18,
             ("scale_m", 1): 20, ("gate_m", 1): 22, ("shift_kv", 1): 24, ("scale_kv", 1): 26}


class BankRing:

    def __init__(self, sem, name, banks, jobs):
        self.banks = banks
        self.at = {job: n for n, job in enumerate(jobs)}
        assert len(self.at) == len(jobs)
        self.full = [sem(f"{name}_full{b}") for b in banks]
        self.free = [sem(f"{name}_free{b}") for b in banks]

    def bank(self, job):
        return self.banks[self.at[job] % len(self.banks)]

    def wait_free(self, eng, job):
        n, k = divmod(self.at[job], len(self.banks))
        if n:
            eng.wait_ge(self.free[k], n)

    def wait_full(self, eng, job):
        n, k = divmod(self.at[job], len(self.banks))
        eng.wait_ge(self.full[k], n + 1)

    def is_full(self, job):
        return self.full[self.at[job] % len(self.banks)]

    def is_free(self, job):
        return self.free[self.at[job] % len(self.banks)]

    def wait_freed(self, eng, job):
        n, k = divmod(self.at[job], len(self.banks))
        eng.wait_ge(self.free[k], n + 1)

    def wait_drained(self, eng, job):
        last = self.at[job]
        for k in range(len(self.banks)):
            n = (last - k) // len(self.banks) + 1
            if n > 0:
                eng.wait_ge(self.free[k], n)


class Steps:

    def __init__(self, eng, sem):
        self.eng, self.sem, self.base, self.n = eng, sem, 0, 0

    def do(self, ins):
        ins.then_inc(self.sem, 1)
        self.n += 1

    def settle(self):
        self.eng.wait_ge(self.sem, self.base + self.n)

    def run(self, ins):
        self.do(ins)
        self.settle()


class WeightRing:

    def __init__(self):
        self.pos, self.loads, self.owner, self.items = 0, [0] * UNITS, [None] * UNITS, {}

    def take(self, key, units, freed_by, loads=1):
        if self.pos + units > UNITS:
            self.pos = 0
        u = self.pos
        self.pos = (u + units) % UNITS
        waits = {}
        for k in range(u, u + units):
            if self.owner[k] is not None:
                s, n = self.owner[k]
                waits[s.name] = (s, max(n, waits.get(s.name, (s, 0))[1]))
            self.owner[k] = freed_by
        self.loads[u] += loads
        self.items[key] = (u, self.loads[u], list(waits.values()))

    def align(self):
        self.pos = 0


SMALL_LOADS = 6
Y_STORED = [[(l + 1) * len(range(s, NE, 3)) for s in range(3)] for l in range(2)]
KV_SLOTS = [((j, t), 3 * j + t if j < 2 else (6 + j - 2 if t == 2 else None)) for j in range(4) for t in range(3)]
FOX_STEPS = 6


INPUTS = ["x_prompt", "x_sample", "c_prompt", "c_sample", "state_gla", "cache_k", "cache_v", "cache_logf",
          "page_table", "gla_w_in", "gla_w_a2", "gla_b_a", "gla_norm_g", "gla_w_o", "kv_w_mod", "kv_b_mod",
          "kv_w", "fox_b_f", "fox_w_q", "fox_w_o", "ada_w", "ada_b", "ln_g", "ln_b", "router_w", "router_bias",
          "exp_w_gate", "exp_w_up", "exp_w_down", "sh_w_gate", "sh_w_up", "sh_w_down"]
OUTPUTS = [("y_prompt", (1, SEQ, D)), ("y_sample", (DB, DT, D)), ("gla_prompt", (1, 1, GH, GK, GV)),
           ("gla_sample", (1, DB, GH, GK, GV)), ("k_prompt", (1, SEQ, FH, HD)), ("v_prompt", (1, SEQ, FH, HD)),
           ("logf_prompt", (1, SEQ, FH)), ("k_sample", (DB, DT, FH, HD)), ("v_sample", (DB, DT, FH, HD)),
           ("logf_sample", (DB, DT, FH))]


def hybrid_trunk_step(nc, W, O):
    ctx = ExitStack()
    sems = {}

    def sem(name):
        if name not in sems:
            sems[name] = ctx.enter_context(nc.semaphore(name))
        return sems[name]

    def sb(name, shape, dt=F32):
        return ctx.enter_context(nc.sbuf_tensor(name, shape, dt))

    def scratch(name, shape, dt=F32):
        return nc.dram_tensor(name, shape, dt)

    def dram(ap, offset, dims):
        return bass.AP(tensor=ap.tensor, offset=offset, ap=dims)

    with ctx:
        mod_d = scratch("mod_d", [ADA_N * P, P])[:, :]
        u_d = scratch("u_d", [TOK * 2, 512])[:, :]
        places_d = scratch("places_d", [NE * TOK, 1], I32)[:, :]
        pair_d = scratch("pair_d", [TOK * TOPK * 2, 512])[:, :]
        bias_d = scratch("bias_d", [FH * DB, CTX])[:, :]
        fq_d = scratch("fq_d", [DB * DT, FH])[:, :]
        og_d = scratch("og_d", [2 * DB * P, HD])[:, :]

        ring = sb("ring", [P, UNITS, UNIT])
        x = sb("x", [P, 3, D])
        u = sb("u", [P, 3, D])
        uT = sb("uT", [P, KT, TOK])
        mscale = sb("mscale", [P, 2, D])
        mshift = sb("mshift", [P, 2, D])
        mgate = sb("mgate", [P, 2, D])
        ln = sb("ln", [P, 2, D])
        work = sb("work", [P, 12200])
        ident = sb("ident", [P, P])
        ones = sb("ones", [P, P])
        upto = sb("upto", [P, P])
        before = sb("before", [P, P])
        upto64 = sb("upto64", [P, P])
        same64 = sb("same64", [P, P])
        upto8 = sb("upto8", [64, 64])
        same8 = sb("same8", [64, 64])
        group64 = sb("group64", [P, 2])
        group8 = sb("group8", [64, 8])
        causal = sb("causal", [P, P])
        causal8 = sb("causal8", [P, DT])
        tri8 = sb("tri8", [P, 8, 8])
        place0 = sb("place0", [P, NE])
        pair_id = sb("pair_id", [P, 3, TOPK], I32)
        half_id = sb("half_id", [P, 1])
        ov_code = sb("ov_code", [1, (BLOCKS - 1) * NE])
        cT = sb("cT", [P, KT, 32])
        ada_bias = sb("ada_bias", [P, 4, P])
        ada_out = sb("ada_out", [P, 4, P])
        w_small = sb("w_small", [P, KT, 64])
        w_a2 = sb("w_a2", [RANK, GD])
        b_a = sb("b_a", [P, GD])
        norm_g = sb("norm_g", [P, GV])
        r_bias = sb("r_bias", [P, NE])
        b_f = sb("b_f", [P, FH])
        pages = sb("pages", [1, DB * PAGES], I32)
        page_col = sb("page_col", [DB * PAGES, 1], I32)
        alrT = sb("alrT", [RANK, TOK])
        w8 = sb("w8", [P, 3, TOPK])
        ov_idx = sb("ov_idx", [1, OVER + 1], I32)
        ov_e = sb("ov_e", [1, OVER + 1], I32)
        eps = sb("eps", [P, 2])
        stat = sb("stat", [P, 64])

        psum = [ctx.enter_context(nc.psum_tensor(f"bank{i}", [P, 512], F32)) for i in range(8)]

        cursor = [0]

        def carve(n, *shape):
            v = work[:, cursor[0]:cursor[0] + n]
            cursor[0] += n
            assert cursor[0] <= 12200, cursor[0]
            if len(shape) == 2:
                return v.rearrange("p (a b) -> p a b", a=shape[0], b=shape[1])
            if len(shape) == 3:
                return v.rearrange("p (a b c) -> p a b c", a=shape[0], b=shape[1], c=shape[2])
            return v

        cursor[0] = 0
        q = carve(3 * GD, 3, GD)
        k = carve(3 * GD, 3, GD)
        gs = carve(3 * D, 3, D)
        la = carve(3 * GD, 3, GD)
        qz_all = carve(GH * 576)
        qz64 = qz_all[:, 0:GH * 384].rearrange("p (h n) -> p h n", h=GH)
        qz8 = qz_all[:, :].rearrange("p (h n) -> p h n", h=GH)
        s_in = carve(2 * D, 2, D)
        lf_pages = la
        later = gs[:, 0, :]
        s_out = ln
        s_p = mscale[:, 0, :]
        att = mscale[:, 1, 0:GD].rearrange("p (h t) -> p h t", h=GH)
        egT = mscale[:, 1, GD:GD + 32].rearrange("p (h g) -> p h g", h=GH)
        e_cum = mshift[:, 0, 0:GD]
        e_end = mshift[:, 0, GD:2 * GD]
        kd = mshift[:, 1, 0:GD]
        qdT = mshift[:, 1, GD:2 * GD].rearrange("p (h t) -> p h t", h=GH)
        kdT = mgate[:, 0, 0:GD].rearrange("p (h t) -> p h t", h=GH)
        kem = mgate[:, 0, GD:2 * GD]
        cum_sb = mgate[:, 1, 0:GD]
        z_neg = mgate[:, 1, GD:2 * GD]
        v = u
        cursor[0] = 0
        ysh = carve(3 * D, 3, D)
        moe_end = cursor[0]
        xg = carve(3 * 512, 3, 512)
        xT = carve(3 * 512, 3, 512)
        y_sb = carve(3 * 512, 3, 512)
        sil = carve(3 * P, 3, P)
        hs = carve(3 * P, 3, P)
        hT = carve(3 * P, 3, P)
        h_sh = carve(FE)
        hT_sh = carve(2 * P, 2, P)
        xidx = carve(BLOCKS * NE).bitcast(I32)
        yidx = carve(BLOCKS * NE).bitcast(I32)
        xi = carve(4).bitcast(I32)
        yi = carve(4).bitcast(I32)
        score = carve(NE)
        route = carve(10 * NE, 10, NE)
        sel = carve(3 * NE, 3, NE)
        wgt = carve(3 * NE, 3, NE)
        eq3 = mscale[:, 0, 0:TOPK * NE].rearrange("p (k e) -> p k e", k=TOPK)
        place8 = carve(3 * TOPK, 3, TOPK)
        place_i = carve(3 * TOPK, 3, TOPK).bitcast(I32)
        tab_i = mshift[0:NE, 1, 0:TOK].bitcast(I32)
        tab2 = mshift[0:NE, 0, 0:BLOCKS * P].rearrange("p (b h r) -> p b h r", b=BLOCKS, h=2)
        ov_row = mshift[0:1, 1, 512:512 + 4 * NE]
        cnt = carve(NE)
        ov_top = carve(OVER + 1)
        ov_gate = mscale
        ov_up = mshift
        ov_down = u[:, 0:2, :]
        cursor[0] = moe_end
        y_pairs = carve(2 * TOPK * 512, 2, TOPK, 512)
        cursor[0] = 0
        kTp = carve(FH * SEQ, FH, SEQ)
        kTs = carve(FH * 64, FH, 64)
        qT = carve(FH * TOK, FH, TOK)
        vp = carve(2 * D, 2, D)
        kt_sb = carve(2 * PAST, 2, PAST)
        pT = carve(PAGES * P, PAGES, P)
        pTn = carve(P)
        qz = carve(2 * P, 2, 4, 32)
        kn = carve(2 * 32, 2, 4, DT)
        vn = carve(2 * 512, 2, 512)
        og = carve(2 * P, 2, P)
        f_p = carve(2 * FH, 2, FH)
        lf = carve(3 * FH, 3, FH)
        lf_t = carve(3 * FH, 3, FH)
        lf_m = carve(3 * FH, 3, FH)
        f_s = carve(FH)
        nf_s = carve(FH)
        fqc = carve(2 * DB)
        fT = mgate[0:FH, 0, 0:SEQ]
        selneg = mgate[0:FH, 1, :].rearrange("p (h t) -> p h t", h=FH)
        p_sc = kt_sb[:, 0, 0:512].rearrange("p (a b) -> p a b", a=2)
        p_T = kt_sb[:, 1, 0:512].rearrange("p (a b c) -> p a b c", a=2, b=2)
        key_bias = [m[:, :, :].rearrange("p a b -> p (a b)")[:, 0:CTX] for m in (mscale, mshift)]
        sc = ln[:, :, :].rearrange("p a b -> p (a b)")[:, 0:CTX]
        kv_rows = kt_sb[:, :, :].rearrange("p a (b n) -> p (a b) n", n=512)

        def tile_rows(t):
            return TILES[t][1]

        def ring_pair(unit):
            return ring[:, unit:unit + 2, :].rearrange("p a (c n) -> p (a c) n", n=512)

        def state_of(t):
            return (upto64, same64, group64, 2) if t < ST else (upto8, same8, group8, 8)

        moe_pe = ["router_full"] * 3 + ["rank_full"] * 3
        moe_act = ["sigmoid_ready"] * 3 + ["sh_silu_ready"] * 3
        moe_dve = ["chosen", "route_done"] * 3 + ["over_ready", "tab2_ready", "index_ready"]
        events = {
            "pe_event": ["c_turned", "alr_full"] + ["z_full"] * 3
            + ["dec_full", "qdT_full", "kdT_full", "att_full", "upd_full", "o_full", "upd_full"] * 2
            + ["dec_full", "qdT_full", "kdT_full", "att_full"] + ["upd_full"] * (DB - 1) + ["o_full", "upd_full"]
            + moe_pe + ["lf_full", "f_full", "fT_full", "ps_full"] + ["ps_full", "p_turned", "po_full"] * (2 * FH - 1)
            + ["p_turned", "po_full"] + moe_pe,
            "act_event": ["c_silu", "cT_ready", "alrT_ready"] + ["z_log_ready"] * 3
            + ["e_ready", "e_end_ready", "qdT_ready", "rms_ready"] * 3 + moe_act + ["lf_log_ready", "p_exp_ready"]
            + ["p_exp_ready", "p_T_ready"] * (2 * FH - 1) + ["p_T_ready"] + moe_act,
            "dve_event": ["ada_added"] * ADA_N + ["z_neg_ready", "la_ready"] * 3
            + ["end_gap_ready", "qd_ready", "kd_ready", "ke_ready", "kdT_ready", "att_ready",
               "prompt_state_ready", "prompt_state_ready"] * 2
            + ["end_gap_ready", "qd_ready", "kd_ready", "ke_ready", "kdT_ready", "att_ready"]
            + ["kem_ready", "sup_ready"] * DB + moe_dve + ["lf_neg_ready", "lf_ready", "f_ready", "fT_ready", "p_max_ready"]
            + ["p_max_ready", "o_prompt_done"] * (2 * FH - 1) + ["o_prompt_done"] + moe_dve,
        }
        counts, owner_of = {}, {}
        for s_name, order in events.items():
            for n, e_name in enumerate(order):
                counts.setdefault(e_name, []).append(n + 1)
                owner_of[e_name] = s_name
        signalled = {s_name: 0 for s_name in events}

        def wait(eng, event, n):
            eng.wait_ge(sem(owner_of[event]), counts[event][n - 1])

        def signal(event):
            s_name = owner_of[event]
            assert events[s_name][signalled[s_name]] == event, (event, signalled[s_name])
            signalled[s_name] += 1
            return sem(s_name)

        plan_jobs = [("suf", n) for n in range(2)]
        plan_jobs += [("w_in", j, t) for j in range(W_IN_N // 512) for t in range(3)]
        plan_jobs += [("gla_wo", j, t) for j in range(2) for t in range(3)]
        plan_jobs += [("sh_gu", 0, t) for t in range(3)] + [("sh_d", 0, j, t) for t in range(3) for j in range(2)]
        plan_jobs += [("kv", j, t) for j in range(4) for t in range(3)] + [("w_q", h) for h in range(FH)]
        plan_jobs += [("fox_wo", j, t) for j in range(2) for t in range(3)]
        plan_jobs += [("sh_gu", 1, t) for t in range(3)] + [("sh_d", 1, j, t) for t in range(3) for j in range(2)]
        lin = BankRing(sem, "lin", [0, 1, 2], plan_jobs)
        stages = ["gla", "gla_o", "moe0", "kv", "fox", "fox_o", "moe1"]
        turn_jobs = [("lf",)]
        for s in stages:
            turn_jobs += [(s, t, half) for t in range(3) for half in range(2)]
            if s in ("moe0", "moe1"):
                turn_jobs += [("h_sh", int(s[-1]), t) for t in range(3)] + [("places", int(s[-1]))]
            if s == "kv":
                turn_jobs += [("kT", j, t) for j in range(2) for t in range(3)]
        turn = BankRing(sem, "turn", [3, 4], turn_jobs)
        adas = BankRing(sem, "ada", [5, 6], range(ADA_N))

        def last_use(ring_of_banks, job):
            n, b = divmod(ring_of_banks.at[job], len(ring_of_banks.banks))
            return (ring_of_banks.full[b], n + 1)

        wr = WeightRing()
        h_full, y_full = sem("h_full"), sem("y_full")
        kt_full, fo_full = sem("kt_full"), sem("fo_full")

        def plan():
            ada = 0
            for _ in range(4):
                wr.take(("ada", ada), 2, last_use(adas, ada))
                ada += 1
            for j in range(W_IN_N // 512):
                wr.take(("w_in", j), 2, last_use(lin, ("w_in", j, 2)))
                for _ in range(4):
                    wr.take(("ada", ada), 2, last_use(adas, ada))
                    ada += 1
            for j in range(2):
                wr.take(("gla_wo", j), 2, last_use(lin, ("gla_wo", j, 2)))

            def moe(l):
                wr.take(("sh_gu", l), 2, last_use(lin, ("sh_gu", l, 2)), loads=2)
                wr.take(("sh_d", l), 1, last_use(lin, ("sh_d", l, 1, 2)))
                wr.align()
                for e in range(NE):
                    wr.take(("gate", l, e), 1, (h_full, NE * l + e + 1))
                    wr.take(("up", l, e), 1, (h_full, NE * l + e + 1))
                    wr.take(("down", l, e), 1, (y_full, NE * l + e + 1))

            moe(0)
            for j in range(4):
                wr.take(("kv", j), 2, last_use(lin, ("kv", j, 2)))
            for j in range(2):
                wr.take(("w_q", j), 2, last_use(lin, ("w_q", 4 * j + 3)))
            wr.align()
            for g in range(2 * DB):
                if g % 2 == 0:
                    wr.align()
                wr.take(("fox_k", g), 2, (kt_full, 8 * g + 8), loads=PAGES)
                wr.take(("fox_v", g), 2, (fo_full, g + 1), loads=PAGES)
            for j in range(2):
                wr.take(("fox_wo", j), 2, last_use(lin, ("fox_wo", j, 2)))
            moe(1)

        plan()
        unit_full = [sem(f"unit_full{n}") for n in range(UNITS)]

        def weights_landed(eng, key):
            unit, fills, _ = wr.items[key]
            eng.wait_ge(unit_full[unit], 16 * fills)
            return unit

        def mod_wait(eng, chunk):
            eng.wait_ge(sem(f"ada_stored{chunk % 4}"), 16 * (chunk // 4 + 1))

        mods = ["gla", "moe0", "kv", "fox", "moe1"]
        gates = ["gate_a0", "gate_m0", "gate_a1", "gate_m1"]
        NSUB = 4

        block = ctx.enter_context(nc.Block())

        @block.sync
        def _(sp):
            def w_chunk(ap, j):
                return ap.rearrange("(p c) n -> p c n", c=KT)[:, :, j * 512:(j + 1) * 512]

            def free_units(key):
                for s, n in wr.items[key][2]:
                    sp.wait_ge(s, n)
                return wr.items[key][0]

            def load_ada(n):
                unit = free_units(("ada", n))
                w = W["ada_w"][n // 12] if n < 24 else W["kv_w_mod"]
                b = W["ada_b"][n // 12] if n < 24 else W["kv_b_mod"]
                j = n % 12
                sp.dma_start(ring_pair(unit), w_chunk(w, j)).then_inc(unit_full[unit], 16)
                if n >= 4:
                    adas.wait_drained(sp, n - 4)
                off = b.offset + j * 512
                sp.dma_start(ada_bias[:, n % 4, :],
                             dram(b, off, [[P, 4], [0, 32], [1, P]])).then_inc(sem(f"ada_bias{n % 4}"), 16)

            def load_linear(key, ap, j):
                unit = free_units(key)
                sp.dma_start(ring_pair(unit), w_chunk(ap, j)).then_inc(unit_full[unit], 16)

            def load_shared(l):
                unit = free_units(("sh_gu", l))
                for n, w in enumerate((W["sh_w_gate"], W["sh_w_up"])):
                    sp.dma_start(ring_pair(unit)[:, :, n * FE:(n + 1) * FE],
                                 w[l].rearrange("(p c) n -> p c n", c=KT)).then_inc(unit_full[unit], 16)
                unit = free_units(("sh_d", l))
                sp.dma_start(ring[:, unit, :].rearrange("p (f n) -> p f n", f=2),
                             W["sh_w_down"][l].rearrange("(f p) n -> p f n", f=2)).then_inc(unit_full[unit], 16)

            def load_expert(l, e, s):
                for n, name in enumerate(("exp_w_gate", "exp_w_up")):
                    w = W[name][l, ds(e, 1)].rearrange("o (h p j) n -> p (o h) (j n)", h=2, j=4)
                    sp.dma_start(ring[:, 3 * s + n, :].rearrange("p (h m) -> p h m", h=2), w)\
                      .then_inc(unit_full[3 * s + n], 16)

            def load_down(l, e, s):
                w = W["exp_w_down"][l, ds(e, 1)].rearrange("o (f p) n -> p (o f) n", f=2)
                sp.dma_start(ring[:, 3 * s + 2, :].rearrange("p (f n) -> p f n", f=2), w)\
                  .then_inc(unit_full[3 * s + 2], 16)

            def load_experts(l):
                for e in range(3):
                    free_units(("gate", l, e))
                    free_units(("up", l, e))
                    load_expert(l, e, e)
                    free_units(("down", l, e))
                    load_down(l, e, e)
                base = l * NE

                def steady(e, s):
                    sp.wait_ge(h_full, e + (base - 2))
                    load_expert(l, e, s)
                    sp.wait_ge(y_full, e + (base - 2))
                    load_down(l, e, s)

                with sp.Fori(1, NE // 3) as i:
                    for s in range(3):
                        steady(i * 3 + s, s)
                steady(NE - 1, 0)

            def load_pages(g, b, s, first):
                page = [sp.value_load(pages[0:1, ds(b * PAGES + j, 1)], min_val=0,
                                      max_val=W["cache_k"].shape[0] - 1) for j in range(PAGES)]
                for kind, cache, at, freed in (("fox_k", W["cache_k"], 4 * s, (kt_full, g * 8 - 8)),
                                               ("fox_v", W["cache_v"], 4 * s + 2, (fo_full, g - 1))):
                    if first:
                        free_units((kind, g))
                    else:
                        sp.wait_ge(*freed)
                    for j in range(PAGES):
                        rows = cache[ds(page[j], 1)].rearrange("o r h d -> (o r) (h d)")
                        sp.dma_start(ring_pair(at)[:, j, :], rows[:, s * 512:(s + 1) * 512])\
                          .then_inc(unit_full[at], 16)

            for n in range(4):
                load_ada(n)
            n = 4
            for j in range(W_IN_N // 512):
                load_linear(("w_in", j), W["gla_w_in"][0], j)
                for _ in range(4):
                    load_ada(n)
                    n += 1
            for j in range(2):
                load_linear(("gla_wo", j), W["gla_w_o"][0], j)
            load_shared(0)
            load_experts(0)
            for j in range(4):
                load_linear(("kv", j), W["kv_w"], j)
            for j in range(2):
                load_linear(("w_q", j), W["fox_w_q"][0], j)
            sp.wait_ge(sem("small_loaded"), 16 * SMALL_LOADS)
            for s in range(2):
                load_pages(s, 0, s, True)
            with sp.Fori(1, DB) as b:
                for s in range(2):
                    load_pages(b * 2 + s, b, s, False)
            for j in range(2):
                load_linear(("fox_wo", j), W["fox_w_o"][0], j)
            load_shared(1)
            load_experts(1)

        @block.gpsimd
        def _(pool):
            run = Steps(pool, sem("pool_step"))

            def triangle(out, compare, base, pattern, cm, fill=0.0):
                run.run(pool.affine_select(out=out, in_=out, pattern=pattern, compare_op=compare, fill=fill,
                                           base=base, channel_multiplier=cm))

            run.do(pool.memset(cT[:, :, :], 0.0))
            run.do(pool.memset(ident[:, :], 1.0))
            run.settle()
            triangle(ident[:, :], ALU.is_equal, 0, [[-1, P]], 1)
            sem_const = sem("consts_ready")
            pool.nop().then_inc(sem_const, 1)
            pool.wait_ge(sem("page_col_loaded"), 16)
            pool.indirect_dma_start(
                out=mgate[0:DB * PAGES, 0, :], out_offset=None,
                in_=W["cache_logf"].rearrange("n r h -> n (r h)"),
                in_offset=bass.IndirectOffsetOnAxis(ap=page_col[:, 0:1], axis=0)).then_inc(sem("lf_loaded"), 16)
            pool.wait_ge(sem("lf_loaded"), 16)
            for m in (upto, before, upto64, same64, upto8, same8, later, ones, group64, group8):
                run.do(pool.memset(m[:, :], 1.0))
            run.do(pool.memset(causal[:, :], 0.0))
            run.do(pool.memset(eps[:, 0:1], LN_EPS))
            run.do(pool.memset(eps[:, 1:2], RMS_EPS))
            run.do(pool.memset(causal8[:, :], 0.0))
            run.do(pool.memset(tri8[:, :, :], 1.0))
            run.do(pool.memset(qz_all[:, :], 0.0))
            run.settle()
            triangle(upto[:, :], ALU.is_ge, 0, [[1, P]], -1)
            triangle(before[:, :], ALU.is_ge, -1, [[1, P]], -1)
            triangle(later[:, 7 * P:], ALU.is_ge, -1, [[-1, P]], 1)
            for m, w in ((same64, 64), (upto64, 64), (same8, 8), (upto8, 8)):
                size = m.shape[1] // w
                blocks = m[:, :].rearrange("p (b c) -> p b c", c=w)
                triangle(blocks, ALU.is_ge, 0, [[-w, size], [0, w]], 1)
                triangle(blocks, ALU.is_ge, w - 1, [[w, size], [0, w]], -1)
            triangle(upto64[:, :], ALU.is_ge, 0, [[1, P]], -1)
            triangle(upto8[:, :], ALU.is_ge, 0, [[1, 64]], -1)
            for m, w in ((group64, 64), (group8, 8)):
                size = m.shape[1]
                triangle(m[:, :], ALU.is_ge, 0, [[-w, size]], 1)
                triangle(m[:, :], ALU.is_ge, w - 1, [[w, size]], -1)
            triangle(causal[:, :], ALU.is_ge, 0, [[-1, P]], 1, NEG)
            for i in range(4):
                triangle(causal8[32 * i:32 * i + 32, :], ALU.is_ge, 0, [[-1, DT]], 1, NEG)
            triangle(tri8[:, :, :], ALU.is_ge, -1, [[1, 8], [-1, 8]], 0)
            run.do(pool.iota(place0[:, :].bitcast(I32), pattern=[[TOK, NE]], base=1, channel_multiplier=0))
            run.do(pool.iota(pair_id[:, :, :], pattern=[[P * TOPK, 3], [1, TOPK]], base=0,
                             channel_multiplier=TOPK))
            run.run(pool.memset(half_id[:, :], 0.0))
            triangle(half_id[:, :], ALU.is_ge, 63, [[0, 1]], -1, 1.0)
            run.do(pool.iota(ov_code[:, :].bitcast(I32), pattern=[[-1, (BLOCKS - 1) * NE]], base=1000 - NE,
                             channel_multiplier=0))
            run.settle()
            run.do(pool.tensor_copy(place0[:, :], place0[:, :].bitcast(I32)))
            run.do(pool.tensor_copy(ov_code[:, :], ov_code[:, :].bitcast(I32)))
            run.settle()
            pool.nop().then_inc(sem_const, 1)

            wait(pool, "o_full", 2)
            pool.memset(qz_all[:, :], 0.0).then_inc(sem("qz_cleared"), 1)

            def dispatch(l):
                pool.wait_ge(sem("u_ready"), 3 * (stages.index(f"moe{l}") + 1))
                run.run(pool.memset(tab_i, NOBODY))
                pool.dma_start(places_d.rearrange("(e r) o -> e (r o)", e=NE), tab_i)\
                    .then_inc(sem("places_blank"), 16)
                pool.wait_ge(sem("places_blank"), 16 * (l + 1))
                wait(pool, "route_done", 3 * (l + 1))
                for t in range(3):
                    r = tile_rows(t)
                    for j in range(TOPK):
                        pool.indirect_dma_start(
                            out=places_d, out_offset=bass.IndirectOffsetOnAxis(ap=place_i[0:r, t, j:j + 1], axis=0),
                            in_=pair_id[0:r, t, j:j + 1], in_offset=None).then_inc(sem("places_stored"), 16)

            def gather(s, landed):
                pool.sem_inc(sem("pool_passed"), 1)
                pool.indirect_dma_start(
                    out=xg[:, s, :], out_offset=None, in_=u_d,
                    in_offset=bass.IndirectOffsetOnAxis(ap=xi[:, s:s + 1], axis=0),
                    bounds_check=2 * TOK - 1, oob_is_err=False).then_inc(landed, 16)

            def scatter(s, stored):
                pool.sem_inc(sem("pool_passed"), 1)
                pool.indirect_dma_start(
                    out=pair_d, out_offset=bass.IndirectOffsetOnAxis(ap=yi[:, s:s + 1], axis=0),
                    in_=y_sb[:, s, :], in_offset=None,
                    bounds_check=2 * TOK * TOPK - 1, oob_is_err=False).then_inc(stored, 16)

            def experts(l):
                base = l * NE
                wait(pool, "index_ready", l + 1)
                for t in range(3):
                    pool.wait_ge(sem(f"u_stored{t}"), 16 * (l + 1))

                def one(e, s, first=False, last=False):
                    if not last:
                        if not first:
                            pool.wait_ge(sem("xT_full"), e + base)
                        pool.wait_ge(sem("xi_ready"), e + (base + 3))
                        gather((s + 2) % 3, sem(f"xg_full{(s + 2) % 3}"))
                    if not first:
                        pool.wait_ge(sem("yi_ready"), e + base)
                        scatter((s + 2) % 3, sem(f"y_stored{(s + 2) % 3}"))

                pool.wait_ge(sem("xi_ready"), base + 2)
                for e in range(2):
                    gather(e, sem(f"xg_full{e}"))
                for e in range(3):
                    one(e, e, first=(e == 0))
                with pool.Fori(1, 20) as i:
                    for s in range(3):
                        one(i * 3 + s, s)
                for e in range(60, 64):
                    one(e, e % 3, last=(e >= 62))
                pool.wait_ge(sem("yi_ready"), base + NE)
                scatter(0, sem("y_stored0"))

            def overflow(l):
                done = sem(f"pool_over{l}")
                wait(pool, "over_ready", l + 1)
                for s in range(3):
                    pool.wait_ge(sem(f"y_stored{s}"), 16 * Y_STORED[l][s])
                any_ = pool.value_load(ov_idx[0:1, 0:1], min_val=0, max_val=1023)
                with pool.If(any_ < 512):
                    with pool.Fori(0, OVER) as j:
                        col = pool.value_load(ov_idx[0:1, ds(j, 1)], min_val=0, max_val=1023)
                        with pool.If(col < 512):
                            col = pool.value_load(ov_idx[0:1, ds(j, 1)], min_val=0, max_val=BLOCKS * NE - 1)
                            pool.tensor_copy(xi[:, 0:1], xidx[:, ds(col, 1)]).then_inc(done, 1)
                            pool.tensor_copy(yi[:, 0:1], yidx[:, ds(col, 1)]).then_inc(done, 1)
                            pool.wait_ge(done, j * 2 + 2)
                            pool.sem_inc(sem("pool_passed"), 1)
                            pool.indirect_dma_start(
                                out=xg[:, 0, :], out_offset=None, in_=u_d,
                                in_offset=bass.IndirectOffsetOnAxis(ap=xi[:, 0:1], axis=0),
                                bounds_check=2 * TOK - 1, oob_is_err=False).then_inc(sem(f"over_xg{l}"), 16)
                            pool.wait_ge(sem(f"act_over{l}"), j * 2 + 2)
                            pool.sem_inc(sem("pool_passed"), 1)
                            pool.indirect_dma_start(
                                out=pair_d, out_offset=bass.IndirectOffsetOnAxis(ap=yi[:, 0:1], axis=0),
                                in_=y_sb[:, 0, :], in_offset=None,
                                bounds_check=2 * TOK * TOPK - 1, oob_is_err=False)\
                                .then_inc(sem(f"over_stored{l}"), 16)
                            pool.wait_ge(sem(f"over_stored{l}"), j * 16 + 16)
                        with pool.Else():
                            pool.nop()
                        pool.nop()
                    pool.nop()
                with pool.Else():
                    pool.nop()
                pool.nop().then_inc(sem("pairs_stored"), 1)

            dispatch(0)
            experts(0)
            overflow(0)

            pool.wait_ge(sem("ln_done"), 3 * 2)
            run.run(pool.memset(selneg, -1.0))
            triangle(selneg, ALU.is_equal, 0, [[-1, FH], [0, P]], 1)
            run.do(pool.memset(qz[:, :, :, :], 0.0))
            run.do(pool.memset(fqc, 0.0))
            run.settle()
            pool.nop().then_inc(sem("fox_cleared"), 1)
            pool.wait_ge(sem("u_ready"), 3 * (stages.index("fox") + 1))
            for kb in key_bias:
                run.do(pool.memset(kb, 0.0))
            run.settle()
            pool.wait_ge(sem("bias_stored"), 16 * (1 + DB))
            pool.wait_ge(sem("v_stored"), 16 * 8)
            for n in (2, 3):
                pool.wait_ge(sem(f"kv_out{n}"), 32)
            for i in range(4):
                for s in range(2):
                    pool.dma_start(fqc[32 * i:32 * i + DT, s::2],
                                   dram(fq_d, 4 * s + i, [[FH, DT], [DT * FH, DB]]),
                                   allow_slow_non_contiguous=True).then_inc(sem("fqc_loaded"), 16)

            def fetch(b, s):
                for i in range(4):
                    row = bias_d[ds((s * 4 + i) * DB + b, 1), :]
                    pool.dma_start(key_bias[s][32 * i:32 * i + DT, :], row.to_broadcast([DT, CTX])).then_inc(sem(f"fetched{s}"), 16)
                pool.dma_start(vn[0:DT, s, :], O["v_sample"][ds(b, 1)].rearrange("o t h d -> (o t) (h d)")
                               [:, s * 512:(s + 1) * 512]).then_inc(sem(f"fetched{s}"), 16)

            def put(g, b, s):
                pool.wait_ge(sem("og_ready"), g)
                pool.dma_start(og_d[ds((b * 2 + s) * P, P), :], og[:, s, :]).then_inc(sem(f"og_stored{s}"), 16)

            for s in range(2):
                fetch(0, s)
            with pool.Fori(1, DB) as b:
                for s in range(2):
                    put(b * 2 + (s - 1), b - 1, s)
                    fetch(b, s)
            for s in range(2):
                put(2 * DB - 1 + s, DB - 1, s)
            dispatch(1)
            experts(1)
            overflow(1)

        SI = {s: n for n, s in enumerate(stages)}

        def u_ready(eng, stage, t):
            eng.wait_ge(sem("u_ready"), 3 * SI[stage] + t + 1)

        @block.scalar
        def _(act):
            run = Steps(act, sem("act_step"))
            small = sem("small_loaded")
            row = lambda ap, n: dram(ap, ap.offset, [[0, P], [1, n]])

            act.dma_start(ln[0:1, 0, :], W["c_prompt"]).then_inc(sem("c_loaded"), 16)
            act.dma_start(ln[1:9, 0, :], W["c_sample"]).then_inc(sem("c_loaded"), 16)
            act.dma_start(page_col[:, :], W["page_table"].rearrange("b (n o) -> (b n) o", o=1))\
               .then_inc(sem("page_col_loaded"), 16)
            for t in range(2):
                act.dma_start(x[:, t, :], W["x_prompt"][0, t * P:(t + 1) * P, :]).then_inc(sem("x_loaded"), 16)
            act.dma_start(x[0:64, 2, :], W["x_sample"].rearrange("b t d -> (b t) d")).then_inc(sem("x_loaded"), 16)
            act.dma_start(w_small[:, :, 0:RANK], W["gla_w_in"][0].rearrange("(p c) n -> p c n", c=KT)
                          [:, :, W_IN_N:W_IN_N + RANK]).then_inc(small, 16)
            act.dma_start(w_a2[:, :], W["gla_w_a2"][0]).then_inc(small, 16)
            act.dma_start(b_a[:, :], row(W["gla_b_a"], GD)).then_inc(small, 16)
            act.dma_start(norm_g[:, :], row(W["gla_norm_g"], GV)).then_inc(small, 16)
            act.dma_start(b_f[:, :], row(W["fox_b_f"], FH)).then_inc(small, 16)
            act.dma_start(pages[:, :], W["page_table"].rearrange("(o b) n -> o (b n)", o=1)).then_inc(small, 16)

            def load_mod(n, dst, name, l, landed):
                c = MOD_CHUNK[(name, l)]
                mod_wait(act, c)
                mod_wait(act, c + 1)
                act.dma_start(dst[:, 0, :].rearrange("p (k c) -> p k c", c=P),
                              dram(mod_d, c * P * P, [[0, P], [32 * P, 8], [1, P]])).then_inc(landed, 16)
                for b in range(DB):
                    act.dma_start(dst[b * DT:(b + 1) * DT, 1, :].rearrange("p (k c) -> p k c", c=P),
                                  dram(mod_d, c * P * P + (1 + b) * P, [[0, DT], [32 * P, 8], [1, P]]))\
                       .then_inc(landed, 16)

            def load_modulation(n, l, which):
                load_mod(n, mscale, f"scale_{which}", l, sem("mod_loaded"))
                load_mod(n, mshift, f"shift_{which}", l, sem("mod_loaded"))

            def load_gate(n):
                l, sub = divmod(n, 2)
                load_mod(n, mgate, "gate_" + "am"[sub], l, sem("gate_loaded"))
                for i, w in enumerate((W["ln_g"], W["ln_b"])):
                    act.dma_start(ln[:, i, :], row(w[l, sub], D)).then_inc(sem("gate_loaded"), 16)

            def turned(stage):
                for t, (t0, r) in enumerate(TILES):
                    for half in range(2):
                        job = (stage, t, half)
                        turn.wait_full(act, job)
                        act.copy(uT[:, 4 * half:4 * half + 4, t0:t0 + r],
                                 psum[turn.bank(job)][:, :].rearrange("p (c n) -> p c n", c=4)[:, :, 0:r])\
                           .then_inc(turn.is_free(job), 1)

            def store_ada(n):
                wait(act, "ada_added", n + 1)
                act.dma_start(mod_d[n * P:(n + 1) * P, :], ada_out[:, n % 4, :]).then_inc(sem(f"ada_stored{n % 4}"), 16)

            def std(n):
                for t in range(3):
                    r = tile_rows(t)
                    act.wait_ge(sem("var_ready"), 3 * n + t + 1)
                    act.activation(stat[0:r, 47:48], stat[0:r, 45:46], ACT.Sqrt, bias=eps[0:r, 0:1])\
                       .then_inc(sem("std_ready"), 1)

            act.wait_ge(sem("c_loaded"), 32)
            act.activation(ln[0:9, 1, :], ln[0:9, 0, :], ACT.Silu).then_inc(signal("c_silu"), 1)
            wait(act, "c_turned", 1)
            act.copy(cT[:, :, 0:9], psum[7][:, 0:KT * 16].rearrange("p (c n) -> p c n", c=KT)[:, :, 0:9])\
               .then_inc(signal("cT_ready"), 1)
            for n in range(4):
                store_ada(n)
            load_modulation(0, 0, "a")
            turn.wait_full(act, ("lf",))
            act.copy(lf_pages[:, 0, :].rearrange("p (j h b) -> p h b j", j=PAGES, h=FH),
                     psum[turn.bank(("lf",))][:, :].rearrange("p (h b j) -> p h b j", h=FH, b=DB))\
               .then_inc(turn.is_free(("lf",)), 1)
            for n in range(2):
                lin.wait_full(act, ("suf", n))
                act.copy(mgate[0:64, 1, n * 512:(n + 1) * 512], psum[lin.bank(("suf", n))][0:64, :])\
                   .then_inc(lin.is_free(("suf", n)), 1)
            lin.wait_drained(act, ("suf", 1))
            act.dma_start(bias_d[:, 0:PAST], mgate[0:64, 1, :]).then_inc(sem("bias_stored"), 16)
            turned("gla")
            wait(act, "alr_full", 1)
            act.copy(alrT[:, :], psum[7][0:RANK, 0:TOK]).then_inc(signal("alrT_ready"), 1)
            act.dma_start(w_small[:, :, :], W["router_w"][0].rearrange("(p c) n -> p c n", c=KT))\
               .then_inc(sem("router_loaded"), 16)
            act.dma_start(r_bias[:, :], row(W["router_bias"][0], NE)).then_inc(sem("router_loaded"), 16)
            n = 4
            for j in range(W_IN_N // 512):
                for t in range(3):
                    r = tile_rows(t)
                    job = ("w_in", j, t)
                    lin.wait_full(act, job)
                    src = psum[lin.bank(job)][0:r, :]
                    if j == 0:
                        ins = act.activation(q[0:r, t, :], src, ACT.Copy, scale=GK ** -0.5)
                    elif j == 1:
                        ins = act.copy(k[0:r, t, :], src)
                    elif j < 4:
                        ins = act.copy(v[0:r, t, (j - 2) * 512:(j - 1) * 512], src)
                    else:
                        ins = act.activation(gs[0:r, t, (j - 4) * 512:(j - 3) * 512], src, ACT.Silu)
                    ins.then_inc(lin.is_free(job), 1)
                for _ in range(4):
                    store_ada(n)
                    n += 1
            for t in range(3):
                r = tile_rows(t)
                wait(act, "z_neg_ready", t + 1)
                run.run(act.activation(z_neg[0:r, :], z_neg[0:r, :], ACT.Exp))
                act.activation(z_neg[0:r, :], z_neg[0:r, :], ACT.Ln, bias=ones[0:r, 0:1]).then_inc(signal("z_log_ready"), 1)

            def load_state(b):
                if b >= 2:
                    wait(act, "sup_ready", b - 1)
                act.dma_start(s_in[:, b % 2, :].rearrange("p (h e) -> p h e", h=GH),
                              W["state_gla"][0, b].rearrange("h d e -> d h e")).then_inc(sem(f"state_loaded{b % 2}"), 16)

            for b in range(2):
                load_state(b)
            for t in range(3):
                r = tile_rows(t)
                groups = state_of(t)[3]
                wait(act, "dec_full", t + 1)
                run.do(act.copy(cum_sb[0:r, :], psum[0][0:r, :]))
                run.do(act.activation(e_cum[0:r, :], psum[0][0:r, :], ACT.Exp))
                run.do(act.activation(kd[0:r, :], psum[0][0:r, :], ACT.Exp, scale=-1.0))
                act.activation(egT[:, :, 0:groups], psum[2][:, 0:GH * groups].rearrange("p (h g) -> p h g", h=GH),
                               ACT.Exp).then_inc(signal("e_ready"), 1)
                run.settle()
                wait(act, "end_gap_ready", t + 1)
                act.activation(e_end[0:r, :], e_end[0:r, :], ACT.Exp).then_inc(signal("e_end_ready"), 1)
                wait(act, "qdT_full", t + 1)
                bank3 = psum[3][:, :].rearrange("p (h n) -> p h n", h=GH)
                run.do(act.copy(qdT[:, :, 0:r], bank3[:, :, 0:r]))
                if t < ST:
                    diag = qz64.rearrange("p h (g s) -> p h g s", s=192)[:, :, :, 0:64]
                    src = bank3.rearrange("p h (g j) -> p h g j", g=2)
                else:
                    act.wait_ge(sem("qz_cleared"), 1)
                    diag = qz8.rearrange("p h (g s) -> p h g s", s=72)[:, :, :, 0:8]
                    src = bank3[:, :, 0:64].rearrange("p h (g j) -> p h g j", g=8)
                run.settle()
                act.copy(diag, src).then_inc(signal("qdT_ready"), 1)
                if t == ST:
                    for b in range(DB):
                        if b >= 2:
                            load_state(b)
                        wait(act, "sup_ready", b + 1)
                        act.dma_start(O["gla_sample"][0, b].rearrange("h d e -> d h e"),
                                      s_out[:, b % 2, :].rearrange("p (h e) -> p h e", h=GH))\
                           .then_inc(sem(f"state_stored{b % 2}"), 16)
                if t == 1:
                    wait(act, "prompt_state_ready", 4)
                    act.dma_start(O["gla_prompt"][0, 0].rearrange("h d e -> d h e"),
                                  s_p.rearrange("p (h e) -> p h e", h=GH)).then_inc(sem("gla_stored"), 16)
                wait(act, "o_full", t + 1)
                for h in range(GH):
                    ins = act.activation(e_cum[0:r, 0:GV], psum[6 + h // 2][0:r, (h % 2) * GV:(h % 2 + 1) * GV],
                                         ACT.Square, accum_out=stat[0:r, h:h + 1])
                    run.run(ins)
                act.activation(stat[0:r, 48:52], stat[0:r, 0:4], ACT.Sqrt, scale=1.0 / GV, bias=eps[0:r, 1:2])\
                   .then_inc(signal("rms_ready"), 1)
            for b in range(2):
                act.wait_ge(sem(f"state_stored{b}"), 64)
            act.wait_ge(sem("gla_stored"), 16)
            u_ready(act, "gla_o", 2)
            load_gate(0)
            load_modulation(1, 0, "m")
            turned("gla_o")
            std(0)

            def moe_front(l):
                stage = f"moe{l}"
                for t in range(3):
                    t0, r = TILES[t]
                    u_ready(act, stage, t)
                    act.dma_start(u_d[2 * t0:2 * (t0 + r), :].rearrange("(p a) n -> p a n", a=2),
                                  u[0:r, t, :].rearrange("p (a n) -> p a n", a=2)).then_inc(sem(f"u_stored{t}"), 16)
                turned(stage)
                for t in range(3):
                    r = tile_rows(t)
                    wait(act, "router_full", 3 * l + t + 1)
                    if 3 * l + t:
                        wait(act, "route_done", 3 * l + t)
                    act.activation(route[0:r, 0, :], psum[5 + t][0:r, 0:NE], ACT.Sigmoid).then_inc(signal("sigmoid_ready"), 1)
                for t in range(3):
                    r = tile_rows(t)
                    lin.wait_full(act, ("sh_gu", l, t))
                    if t:
                        turn.wait_full(act, ("h_sh", l, t - 1))
                    act.activation(h_sh[0:r, :], psum[lin.bank(("sh_gu", l, t))][0:r, 0:FE], ACT.Silu)\
                       .then_inc(signal("sh_silu_ready"), 1)
                    if t:
                        shared_down(l, t - 1)
                    turn.wait_full(act, ("h_sh", l, t))
                    act.copy(hT_sh[:, :, 0:r], psum[turn.bank(("h_sh", l, t))][:, 0:2 * P]
                             .rearrange("p (f n) -> p f n", f=2)[:, :, 0:r]).then_inc(turn.is_free(("h_sh", l, t)), 1)
                shared_down(l, 2)
                act.wait_ge(sem("places_stored"), 16 * 24 * (l + 1))
                act.dma_start(tab_i, places_d.rearrange("(e r) o -> e (r o)", e=NE)).then_inc(sem("places_loaded"), 16)

            def shared_down(l, t):
                r = tile_rows(t)
                for j in range(2):
                    job = ("sh_d", l, j, t)
                    lin.wait_full(act, job)
                    act.copy(ysh[0:r, t, j * 512:(j + 1) * 512], psum[lin.bank(job)][0:r, :]).then_inc(lin.is_free(job), 1)

            def experts(l):
                base = l * NE

                def y_out(e, s, n_stored):
                    act.wait_ge(y_full, e + (base + 1))
                    if n_stored is not None:
                        act.wait_ge(sem(f"y_stored{s}"), n_stored)
                    act.copy(y_sb[:, s, :], psum[3 + s][:, :]).then_inc(sem("y_ready"), 1)

                def one(e, s, i, first=False):
                    act.wait_ge(h_full, e + (base + 1))
                    act.activation(sil[:, s, :], psum[s][:, 0:P], ACT.Silu).then_inc(sem("sil_ready"), 1)
                    if not first:
                        y_out(e - 1, (s + 2) % 3, stored_before(e - 1, (s + 2) % 3, i))

                before_l = [Y_STORED[l - 1][s] if l else 0 for s in range(3)]

                def stored_before(e, s, i):
                    n = (i if s < 2 else i - 1) if not isinstance(e, int) else e // 3
                    n = n + before_l[s]
                    return None if isinstance(n, int) and n == 0 else n * 16

                for e in range(3):
                    one(e, e, 0, first=(e == 0))
                with act.Fori(1, 20) as i:
                    for s in range(3):
                        one(i * 3 + s, s, i)
                for e in range(60, 64):
                    one(e, e % 3, 0)
                y_out(NE - 1, 0, stored_before(NE - 1, 0, 0))

            def overflow(l):
                done = sem(f"act_over{l}")
                wait(act, "over_ready", l + 1)
                any_ = act.value_load(ov_idx[0:1, 0:1], min_val=0, max_val=1023)
                with act.If(any_ < 512):
                    with act.Fori(0, OVER) as j:
                        col = act.value_load(ov_idx[0:1, ds(j, 1)], min_val=0, max_val=1023)
                        with act.If(col < 512):
                            e = act.value_load(ov_e[0:1, ds(j, 1)], min_val=0, max_val=NE - 1)
                            for name, dst in (("exp_w_gate", ov_gate), ("exp_w_up", ov_up)):
                                act.dma_start(dst[:, :, :], W[name][l, ds(e, 1)].rearrange(
                                    "o (h p j) n -> p (o h) (j n)", h=2, j=4)).then_inc(sem(f"over_w{l}"), 16)
                            act.dma_start(ov_down, W["exp_w_down"][l, ds(e, 1)].rearrange(
                                "o (f p) n -> p (o f) n", f=2)).then_inc(sem(f"over_w{l}"), 16)
                            act.wait_ge(sem(f"over_pe{l}"), j * 4 + 2)
                            act.activation(sil[:, 0, :], psum[0][:, 0:P], ACT.Silu).then_inc(done, 1)
                            act.wait_ge(sem(f"over_pe{l}"), j * 4 + 4)
                            act.copy(y_sb[:, 0, :], psum[3][:, :]).then_inc(sem(f"act_over{l}"), 1)
                            act.wait_ge(sem(f"over_stored{l}"), j * 16 + 16)
                            act.sem_inc(sem("act_passed"), 1)
                        with act.Else():
                            act.nop()
                        act.nop()
                    act.nop()
                with act.Else():
                    act.nop()
                act.nop()

            def load_pairs(l):
                act.wait_ge(sem("pairs_stored"), l + 1)
                for n in range(6):
                    t, half = divmod(n, 2)
                    t0, r = TILES[t]
                    if n >= 2:
                        act.wait_ge(sem("pairs_used"), 6 * l + n - 1)
                    act.dma_start(y_pairs[0:r, n % 2, :, :],
                                  dram(pair_d, t0 * TOPK * D + half * 512, [[TOPK * D, r], [D, TOPK], [1, 512]]))\
                       .then_inc(sem(f"pairs_loaded{n % 2}"), 16)

            moe_front(0)
            act.wait_ge(sem("ln_done"), 3)
            load_gate(1)
            experts(0)
            overflow(0)
            load_pairs(0)
            std(1)
            load_modulation(2, 1, "kv")
            act.dma_start(w_small[:, :, 0:FH], W["kv_w"].rearrange("(p c) n -> p c n", c=KT)[:, :, 2 * D:2 * D + FH])\
               .then_inc(sem("router_loaded"), 16)
            turned("kv")
            for (j, t), slot in KV_SLOTS:
                t0, r = TILES[t]
                job = ("kv", j, t)
                lin.wait_full(act, job)
                if slot is None:
                    dst = vp[0:r, t, (j - 2) * 512:(j - 1) * 512]
                else:
                    if slot >= 4:
                        n_before = (slot - 4) // 4 + 1
                        act.wait_ge(sem(f"kv_out{slot % 4}"), 16 * n_before)
                        if slot - 4 < 6:
                            turn.wait_full(act, ("kT",) + KV_SLOTS[slot - 4][0])
                    dst = kv_rows[0:r, slot % 4, :]
                act.copy(dst, psum[lin.bank(job)][0:r, :]).then_inc(lin.is_free(job), 1)
                lin.wait_freed(act, job)
                out = O[("k" if j < 2 else "v") + ("_prompt" if t < ST else "_sample")]\
                    .rearrange("b t h d -> (b t) (h d)")
                at = t0 if t < ST else 0
                done = sem("v_stored") if slot is None else sem(f"kv_out{slot % 4}")
                act.dma_start(out[at:at + r, (j % 2) * 512:(j % 2 + 1) * 512], dst).then_inc(done, 16)
            wait(act, "lf_neg_ready", 1)
            run.run(act.activation(lf_t[:, :, :], lf_t[:, :, :], ACT.Exp))
            act.activation(lf_t[:, :, :], lf_t[:, :, :], ACT.Ln, bias=ones[:, 0:1]).then_inc(signal("lf_log_ready"), 1)
            wait(act, "lf_ready", 1)
            for t in range(2):
                act.dma_start(O["logf_prompt"][0, t * P:(t + 1) * P, :], lf[:, t, :]).then_inc(sem("v_stored"), 16)
            act.dma_start(O["logf_sample"].rearrange("b t h -> (b t) h"), lf[0:64, 2, :]).then_inc(sem("v_stored"), 16)
            wait(act, "f_ready", 1)
            act.dma_start(fq_d, f_s[0:64, :]).then_inc(sem("v_stored"), 16)
            for b in range(DB):
                act.dma_start(dram(bias_d, b * CTX + PAST, [[1, DT], [DB * CTX, FH]]), nf_s[b * DT:(b + 1) * DT, :],
                              allow_slow_non_contiguous=True)\
                   .then_inc(sem("bias_stored"), 16)
            u_ready(act, "kv", 2)
            load_modulation(3, 1, "a")
            turned("fox")
            for h in range(FH):
                lin.wait_full(act, ("w_q", h))
                act.activation(qT[:, h, :], psum[lin.bank(("w_q", h))][:, 0:TOK], ACT.Copy, scale=HD ** -0.5)\
                   .then_inc(lin.is_free(("w_q", h)), 1)
            for n in range(2 * FH + 1):
                if n < 2 * FH:
                    nk = P * (n % 2 + 1)
                    wait(act, "p_max_ready", n + 1)
                    act.activation(p_sc[:, n % 2, 0:nk], p_sc[:, n % 2, 0:nk], ACT.Exp,
                                   bias=stat[:, 8 + n % 2:9 + n % 2],
                                   accum_out=stat[:, 10 + n % 2:11 + n % 2]).then_inc(signal("p_exp_ready"), 1)
                if n >= 1:
                    m = n - 1
                    wait(act, "p_turned", m + 1)
                    if m >= 2:
                        wait(act, "po_full", m - 1)
                    act.copy(p_T[:, m % 2, 0:m % 2 + 1, :], psum[5 + m % 2][:, 0:P * (m % 2 + 1)]
                             .rearrange("p (a n) -> p a n", n=P)).then_inc(signal("p_T_ready"), 1)
            wait(act, "po_full", 2 * FH)

            def keys_turned(g, i):
                act.wait_ge(kt_full, g * 8 + (2 * i + 1))
                if i >= 2:
                    act.wait_ge(sem("s_full"), g * 4 + (i - 1))
                act.copy(kt_sb[:, i % 2, 0:512], psum[0][:, :]).then_inc(sem("kt_act"), 1)

            def probs_turned(g):
                act.wait_ge(sem("pt_full"), g * 3 + 1)
                act.copy(pT[:, 0:4, :].rearrange("p a b -> p (a b)"), psum[5][:, :]).then_inc(sem("pt_act"), 1)

            def fox_group(g, s, first=False):
                keys_turned(g, 0)
                keys_turned(g, 1)
                if not first:
                    probs_turned(g - 1)
                keys_turned(g, 2)
                keys_turned(g, 3)
                act.wait_ge(sem("max_ready"), g + 1)
                act.activation(sc, sc, ACT.Exp, bias=stat[:, 16:17], accum_out=stat[:, 18 + s:19 + s])\
                   .then_inc(sem("exp_ready"), 1)

            for s in range(2):
                fox_group(s, s, first=(s == 0))
            with act.Fori(1, DB) as b:
                for s in range(2):
                    fox_group(b * 2 + s, s)
            probs_turned(2 * DB - 1)
            for s in range(2):
                act.wait_ge(sem(f"og_stored{s}"), 16 * DB)
            wait(act, "o_prompt_done", 2 * FH)
            for b in range(DB):
                act.dma_start(u[b * DT:(b + 1) * DT, ST, :].rearrange("p (k n) -> p k n", n=HD),
                              dram(og_d, b * 2 * P * HD, [[HD, DT], [32 * HD, FH], [1, HD]])).then_inc(sem("og_loaded"), 16)
            load_gate(2)
            load_modulation(4, 1, "m")
            act.dma_start(w_small[:, :, :], W["router_w"][1].rearrange("(p c) n -> p c n", c=KT))\
               .then_inc(sem("router_loaded"), 16)
            act.dma_start(r_bias[:, :], row(W["router_bias"][1], NE)).then_inc(sem("router_loaded"), 16)
            turned("fox_o")
            std(2)
            moe_front(1)
            act.wait_ge(sem("ln_done"), 9)
            load_gate(3)
            experts(1)
            overflow(1)
            load_pairs(1)
            std(3)
            act.wait_ge(sem("ln_done"), 12)
            for t in range(2):
                act.dma_start(O["y_prompt"][0, t * P:(t + 1) * P, :], x[:, t, :]).then_inc(sem("y_out"), 16)
            act.dma_start(O["y_sample"].rearrange("b t d -> (b t) d"), x[0:64, 2, :]).then_inc(sem("y_out"), 16)
            act.wait_ge(sem("y_out"), 48)
            act.wait_ge(sem("v_stored"), 16 * (4 + 3 + 1))
            for n in range(4):
                act.wait_ge(sem(f"kv_out{n}"), 32)

        @block.vector
        def _(dve):
            run = Steps(dve, sem("dve_step"))
            stt, tt, ts = dve.scalar_tensor_tensor, dve.tensor_tensor, dve.tensor_scalar

            def side(m, t):
                return m[0:tile_rows(t), 0 if t < ST else 1, :]

            def add_ada(n):
                adas.wait_full(dve, n)
                dve.wait_ge(sem(f"ada_bias{n % 4}"), 16 * (n // 4 + 1))
                if n >= 4:
                    mod_wait(dve, n - 4)
                tt(ada_out[:, n % 4, :], psum[adas.bank(n)][:, 0:P], ada_bias[:, n % 4, :], ALU.add)\
                    .then_inc(adas.is_free(n), 1)
                adas.wait_freed(dve, n)
                dve.nop().then_inc(signal("ada_added"), 1)

            def modulate(n, stage):
                dve.wait_ge(sem("mod_loaded"), 16 * 18 * (n + 1))
                for t in range(3):
                    r = tile_rows(t)
                    run.run(stt(u[0:r, t, :], side(mscale, t), 1.0, x[0:r, t, :], ALU.add, ALU.mult))
                    tt(u[0:r, t, :], u[0:r, t, :], side(mshift, t), ALU.add).then_inc(sem("u_ready"), 1)

            def norm_tile(n, t):
                r = tile_rows(t)
                xt = x[0:r, t, :]
                st, mv, rstd = stat[0:r, 32:44], stat[0:r, 44:46], stat[0:r, 46:47]
                for h in range(2):
                    run.do(dve.bn_stats(st[:, 6 * h:6 * h + 6], xt[:, h * 512:(h + 1) * 512]))
                run.settle()
                dve.bn_aggr(mv, st).then_inc(sem("var_ready"), 1)
                dve.wait_ge(sem("var_ready"), 3 * n + t + 1)
                run.do(stt(xt, xt, mv[:, 0:1], ln[0:r, 0, :], ALU.subtract, ALU.mult))
                dve.wait_ge(sem("std_ready"), 3 * n + t + 1)
                run.run(dve.reciprocal(rstd, stat[0:r, 47:48]))
                stt(xt, xt, rstd, ln[0:r, 1, :], ALU.mult, ALU.add).then_inc(sem("ln_done"), 1)

            def residual(n, name):
                dve.wait_ge(sem("gate_loaded"), 16 * 11 * (n + 1))
                for j in range(2):
                    for t in range(3):
                        r = tile_rows(t)
                        cols = slice(j * 512, (j + 1) * 512)
                        job = (name, j, t)
                        lin.wait_full(dve, job)
                        stt(u[0:r, t, cols], side(mgate, t)[:, cols], 1.0, psum[lin.bank(job)][0:r, :],
                            ALU.add, ALU.mult).then_inc(lin.is_free(job), 1)
                lin.wait_drained(dve, (name, 1, 2))
                for t in range(3):
                    r = tile_rows(t)
                    run.run(stt(x[0:r, t, :], x[0:r, t, :], ALPHA, u[0:r, t, :], ALU.mult, ALU.add))
                    norm_tile(n, t)

            dve.wait_ge(sem("consts_ready"), 1)
            for n in range(4):
                add_ada(n)
            dve.wait_ge(sem("x_loaded"), 48)
            modulate(0, "gla")
            n = 4
            for j in range(W_IN_N // 512):
                for _ in range(4):
                    add_ada(n)
                    n += 1

            dve.wait_ge(sem("small_loaded"), 16 * SMALL_LOADS)
            dve.wait_ge(sem("consts_ready"), 2)
            for t in range(3):
                r = tile_rows(t)
                wait(dve, "z_full", t + 1)
                z = la[0:r, t, :]
                run.run(tt(z, psum[5 + t][0:r, :], b_a[0:r, :], ALU.add))
                stt(z_neg[0:r, :], z, -1.0, z, ALU.mult, ALU.min).then_inc(signal("z_neg_ready"), 1)
                wait(dve, "z_log_ready", t + 1)
                run.run(stt(z, z, 0.0, z_neg[0:r, :], ALU.min, ALU.subtract))
                ts(z, z, 1.0 / TAU, None, ALU.mult).then_inc(signal("la_ready"), 1)
            for t in range(3):
                r = tile_rows(t)
                mask, _, _, groups = state_of(t)
                wait(dve, "e_ready", t + 1)
                tt(e_end[0:r, :], psum[1][0:r, :], cum_sb[0:r, :], ALU.subtract).then_inc(signal("end_gap_ready"), 1)
                tt(q[0:r, t, :], q[0:r, t, :], e_cum[0:r, :], ALU.mult).then_inc(signal("qd_ready"), 1)
                tt(kd[0:r, :], k[0:r, t, :], kd[0:r, :], ALU.mult).then_inc(signal("kd_ready"), 1)
                wait(dve, "e_end_ready", t + 1)
                wait(dve, "kd_ready", t + 1)
                tt(k[0:r, t, :], k[0:r, t, :], e_end[0:r, :], ALU.mult).then_inc(signal("ke_ready"), 1)
                wait(dve, "kdT_full", t + 1)
                dve.tensor_copy(kdT[:, :, 0:r], psum[4][:, :].rearrange("p (h n) -> p h n", h=GH)[:, :, 0:r])\
                   .then_inc(signal("kdT_ready"), 1)
                wait(dve, "att_full", t + 1)
                tt(att[0:r, :, 0:r], psum[5][0:r, :].rearrange("p (h n) -> p h n", h=GH)[:, :, 0:r],
                   mask[0:r, 0:r].unsqueeze(1).to_broadcast([r, GH, r]), ALU.mult).then_inc(signal("att_ready"), 1)

                def state_step(new, old, g):
                    for h in range(GH):
                        part = slice(h * GV, (h + 1) * GV)
                        upd = psum[h // 2][:, (h % 2) * GV:(h % 2 + 1) * GV]
                        if old is None:
                            run.do(dve.tensor_copy(new[:, part], upd))
                        else:
                            run.do(stt(new[:, part], old[:, part], egT[:, h, g:g + 1], upd, ALU.mult, ALU.add))
                    run.settle()

                if t < ST:
                    for g in range(2):
                        c = 2 * t + g
                        wait(dve, "upd_full", c + 1)
                        state_step(s_p, s_p if c else None, g)
                        dve.nop().then_inc(signal("prompt_state_ready"), 1)
                else:
                    for b in range(DB):
                        if b:
                            wait(dve, "upd_full", 4 + b)
                        ts(kem[0:r, :], k[0:r, t, :], group8[:, b:b + 1], None, ALU.mult).then_inc(signal("kem_ready"), 1)
                        wait(dve, "upd_full", 5 + b)
                        dve.wait_ge(sem(f"state_loaded{b % 2}"), 16 * (b // 2 + 1))
                        if b >= 2:
                            dve.wait_ge(sem(f"state_stored{b % 2}"), 16 * (b // 2))
                        state_step(s_out[:, b % 2, :], s_in[:, b % 2, :], b)
                        dve.nop().then_inc(signal("sup_ready"), 1)
                wait(dve, "rms_ready", t + 1)
                run.run(dve.reciprocal(stat[0:r, 4:8], stat[0:r, 48:52]))
                for h in range(GH):
                    run.do(stt(u[0:r, t, h * GV:(h + 1) * GV], psum[6 + h // 2][0:r, (h % 2) * GV:(h % 2 + 1) * GV],
                               stat[0:r, 4 + h:5 + h], norm_g[0:r, :], ALU.mult, ALU.mult))
                run.settle()
                tt(u[0:r, t, :], u[0:r, t, :], gs[0:r, t, :], ALU.mult).then_inc(sem("u_ready"), 1)
            residual(0, "gla_wo")

            def choose(l, t):
                r = tile_rows(t)
                R = route[0:r, :, :]
                s, sb_, rep, msk = R[:, 0, :], R[:, 1, :], R[:, 2, :], R[:, 3, :]
                grp = lambda a: a.rearrange("p (g e) -> p g e", g=NG)
                top, two, eqs = R[:, 4, :], R[:, 5, 0:NG], R[:, 6, :]
                rank8, best = R[:, 5, NG:2 * NG], R[:, 5, 16:24]
                wait(dve, "sigmoid_ready", 3 * l + t + 1)
                run.run(tt(sb_, s, r_bias[0:r, :], ALU.add))
                for g in range(NG):
                    run.do(dve.max(out=top[:, g * 8:g * 8 + 8], in_=sb_[:, g * 8:g * 8 + 8]))
                run.settle()
                run.run(tt(two, grp(top)[:, :, 0], grp(top)[:, :, 1], ALU.add))
                mine = two.unsqueeze(2).to_broadcast([r, NG, NG])
                other = two.unsqueeze(1).to_broadcast([r, NG, NG])
                run.do(tt(grp(rep), other, mine, ALU.is_gt))
                run.do(tt(grp(eqs), other, mine, ALU.is_equal))
                run.settle()
                run.run(tt(grp(eqs), grp(eqs), tri8[0:r, :, :], ALU.mult))
                run.run(tt(rep, rep, eqs, ALU.add))
                run.run(dve.tensor_reduce(rank8, grp(rep), AX, ALU.add))
                run.run(ts(rank8, rank8, float(TOPG) - 0.5, NEG, ALU.is_gt, ALU.mult))
                run.run(tt(grp(msk), grp(sb_), rank8.unsqueeze(2).to_broadcast([r, NG, 8]), ALU.add))
                run.run(dve.max(out=best, in_=msk))
                run.run(dve.match_replace(out=rep, in_to_replace=best, in_values=msk, imm_value=4 * NEG))
                run.run(tt(sel[0:r, t, :], rep, msk, ALU.not_equal))
                w = wgt[0:r, t, :]
                run.run(tt(w, s, sel[0:r, t, :], ALU.mult))
                run.run(dve.tensor_reduce(R[:, 5, 24:25], w, AX, ALU.add))
                run.run(dve.reciprocal(R[:, 5, 25:26], R[:, 5, 24:25]))
                ts(w, w, R[:, 5, 25:26], ROUTED, ALU.mult, ALU.mult).then_inc(signal("chosen"), 1)

            def place(l, t):
                r = tile_rows(t)
                wait(dve, "rank_full", 3 * l + t + 1)
                pl = route[0:r, 7, :]
                run.run(tt(pl, psum[5 + t][0:r, 0:NE], place0[0:r, :], ALU.add))
                run.run(tt(pl, pl, sel[0:r, t, :], ALU.mult))
                run.run(dve.max(out=place8[0:r, t, :], in_=pl))
                e3 = eq3[0:r, :, :]
                run.run(tt(e3, pl.unsqueeze(1).to_broadcast([r, TOPK, NE]),
                           place8[0:r, t, :].unsqueeze(2).to_broadcast([r, TOPK, NE]), ALU.is_equal))
                run.run(tt(e3, e3, wgt[0:r, t, :].unsqueeze(1).to_broadcast([r, TOPK, NE]), ALU.mult))
                run.run(dve.tensor_reduce(w8[0:r, t, :], e3, AX, ALU.add))
                ts(place_i[0:r, t, :], place8[0:r, t, :], 1.0, None, ALU.subtract).then_inc(signal("route_done"), 1)

            def moe_front(l):
                modulate(1 + 3 * l, f"moe{l}")
                dve.wait_ge(sem("router_loaded"), 16 * (2 + 3 * l))
                for t in range(3):
                    choose(l, t)
                    place(l, t)
                for t in range(3):
                    r = tile_rows(t)
                    wait(dve, "sh_silu_ready", 3 * l + t + 1)
                    tt(h_sh[0:r, :], h_sh[0:r, :], psum[lin.bank(("sh_gu", l, t))][0:r, FE:2 * FE], ALU.mult)\
                        .then_inc(lin.is_free(("sh_gu", l, t)), 1)
                for b in range(1, BLOCKS):
                    run.do(ts(ov_row[:, (b - 1) * NE:b * NE], psum[7][0:1, NE:2 * NE], float(CAP * b), None, ALU.is_gt))
                run.settle()
                run.run(tt(ov_row, ov_row, ov_code[:, :], ALU.mult))
                for n in range((OVER + 1) // 8):
                    run.run(dve.max(out=ov_top[0:1, 8 * n:8 * n + 8], in_=ov_row))
                    run.run(dve.match_replace(out=ov_row, in_to_replace=ov_top[0:1, 8 * n:8 * n + 8],
                                              in_values=ov_row, imm_value=0.0))
                run.run(ts(ov_idx[0:1, :], ov_top[0:1, :], -1.0, 1000.0, ALU.mult, ALU.add))
                ts(ov_e[0:1, :], ov_idx[0:1, :], NE - 1, None, ALU.bitwise_and).then_inc(signal("over_ready"), 1)
                dve.wait_ge(sem("places_loaded"), 16 * (l + 1))
                for h in range(2):
                    run.do(dve.tensor_copy(tab2[:, :, h, :], tab_i.rearrange("e (b r) -> e b r", b=BLOCKS)))
                run.settle()
                dve.nop().then_inc(signal("tab2_ready"), 1)
                job = ("places", l)
                turn.wait_full(dve, job)
                run.run(dve.tensor_copy(yidx, psum[turn.bank(job)][:, 0:BLOCKS * NE]))
                run.run(ts(xidx, yidx, 3, None, ALU.arith_shift_right))
                run.do(ts(xidx, xidx, 2.0, half_id[:, 0:1], ALU.mult, ALU.add))
                ts(yidx, yidx, 2.0, half_id[:, 0:1], ALU.mult, ALU.add).then_inc(turn.is_free(job), 1)
                run.settle()
                turn.wait_freed(dve, job)
                run.run(dve.memset(xg[:, :, :], 0.0))
                dve.nop().then_inc(signal("index_ready"), 1)

            def experts(l):
                base = l * NE

                def rows_turned(e, s):
                    dve.wait_ge(sem("xT_full"), e + (base + 1))
                    dve.tensor_copy(xT[:, s, :], psum[3 + s][:, :]).then_inc(sem("xT_ready"), 1)

                def rows_wanted(e, s):
                    dve.tensor_copy(xi[:, s:s + 1], xidx[:, ds(e, 1)]).then_inc(sem("xi_ready"), 1)

                def rows_returned(e, s):
                    dve.wait_ge(sem("y_ready"), e + (base + 1))
                    dve.tensor_copy(yi[:, s:s + 1], yidx[:, ds(e, 1)]).then_inc(sem("yi_ready"), 1)

                def one(e, s, first=False, fetch=True, turn_next=True):
                    dve.wait_ge(sem("sil_ready"), e + (base + 1))
                    if fetch:
                        rows_wanted(e + 2, (s + 2) % 3)
                    tt(hs[:, s, :], sil[:, s, :], psum[s][:, P:2 * P], ALU.mult).then_inc(sem("h_ready"), 1)
                    if turn_next:
                        rows_turned(e + 1, (s + 1) % 3)
                    dve.wait_ge(sem("hT_full"), e + (base + 1))
                    dve.tensor_copy(hT[:, s, :], psum[s][:, 2 * P:3 * P]).then_inc(sem("hT_ready"), 1)
                    if not first:
                        rows_returned(e - 1, (s + 2) % 3)

                for e in range(2):
                    rows_wanted(e, e)
                rows_turned(0, 0)
                for e in range(3):
                    one(e, e, first=(e == 0))
                with dve.Fori(1, 20) as i:
                    for s in range(3):
                        one(i * 3 + s, s)
                for e in range(60, 64):
                    one(e, e % 3, fetch=(e < 62), turn_next=(e < 63))
                rows_returned(NE - 1, 0)

            def overflow(l):
                wait(dve, "over_ready", l + 1)
                any_ = dve.value_load(ov_idx[0:1, 0:1], min_val=0, max_val=1023)
                with dve.If(any_ < 512):
                    with dve.Fori(0, OVER) as j:
                        col = dve.value_load(ov_idx[0:1, ds(j, 1)], min_val=0, max_val=1023)
                        with dve.If(col < 512):
                            dve.wait_ge(sem(f"over_pe{l}"), j * 4 + 1)
                            dve.tensor_copy(xT[:, 0, :], psum[3][:, :]).then_inc(sem(f"over_dve{l}"), 1)
                            dve.wait_ge(sem(f"act_over{l}"), j * 2 + 1)
                            tt(hs[:, 0, :], sil[:, 0, :], psum[0][:, P:2 * P], ALU.mult)\
                                .then_inc(sem(f"over_dve{l}"), 1)
                            dve.wait_ge(sem(f"over_pe{l}"), j * 4 + 3)
                            dve.tensor_copy(hT[:, 0, :], psum[0][:, 2 * P:3 * P]).then_inc(sem(f"over_dve{l}"), 1)
                        with dve.Else():
                            dve.nop()
                        dve.nop()
                    dve.nop()
                with dve.Else():
                    dve.nop()

            def combine(l):
                for n in range(6):
                    t, half = divmod(n, 2)
                    r = tile_rows(t)
                    dve.wait_ge(sem(f"pairs_loaded{n % 2}"), 16 * (3 * l + n // 2 + 1))
                    y = ysh[0:r, t, half * 512:(half + 1) * 512]
                    for j in range(TOPK):
                        ins = stt(y, y_pairs[0:r, n % 2, j, :], w8[0:r, t, j:j + 1], y, ALU.mult, ALU.add)
                        if j < TOPK - 1:
                            run.run(ins)
                    ins.then_inc(sem("pairs_used"), 1)
                dve.wait_ge(sem("pairs_used"), 6 * (l + 1))
                dve.wait_ge(sem("gate_loaded"), 16 * 11 * (2 * l + 2))
                for t in range(3):
                    r = tile_rows(t)
                    run.run(stt(u[0:r, t, :], side(mgate, t), 1.0, ysh[0:r, t, :], ALU.add, ALU.mult))
                    run.run(stt(x[0:r, t, :], x[0:r, t, :], ALPHA, u[0:r, t, :], ALU.mult, ALU.add))
                    norm_tile(2 * l + 1, t)

            moe_front(0)
            experts(0)
            overflow(0)
            combine(0)

            dve.wait_ge(sem("ln_done"), 6)
            modulate(2, "kv")
            for j in range(2):
                for t in range(3):
                    t0, r = TILES[t]
                    job = ("kT", j, t)
                    turn.wait_full(dve, job)
                    src = psum[turn.bank(job)][:, :].rearrange("p (h n) -> p h n", h=4)[:, :, 0:r]
                    dst = kTp[:, 4 * j:4 * j + 4, t0:t0 + r] if t < ST else kTs[:, 4 * j:4 * j + 4, :]
                    dve.tensor_copy(dst, src).then_inc(turn.is_free(job), 1)
            turn.wait_drained(dve, ("kT", 1, 2))
            wait(dve, "lf_full", 1)
            run.do(dve.memset(lf[:, :, :], 0.0))
            run.do(dve.memset(lf_t[:, :, :], 0.0))
            run.settle()
            for t in range(3):
                r = tile_rows(t)
                run.do(tt(lf[0:r, t, :], psum[5 + t][0:r, 0:FH], b_f[0:r, :], ALU.add))
            run.settle()
            stt(lf_t[:, :, :], lf[:, :, :], -1.0, lf[:, :, :], ALU.mult, ALU.min).then_inc(signal("lf_neg_ready"), 1)
            wait(dve, "lf_log_ready", 1)
            stt(lf[:, :, :], lf[:, :, :], 0.0, lf_t[:, :, :], ALU.min, ALU.subtract).then_inc(signal("lf_ready"), 1)
            wait(dve, "f_full", 1)
            run.do(dve.tensor_copy(f_p[:, 0, :], psum[5][:, 64:64 + FH]))
            run.do(dve.tensor_copy(f_p[:, 1, :], psum[6][:, 64:64 + FH]))
            run.do(ts(nf_s[0:64, :], psum[7][0:64, 64:64 + FH], -1.0, None, ALU.mult))
            run.do(dve.tensor_copy(f_s[0:64, :], psum[7][0:64, 64:64 + FH]))
            run.settle()
            dve.nop().then_inc(signal("f_ready"), 1)
            wait(dve, "fT_full", 1)
            dve.tensor_copy(fT, psum[7][0:FH, 0:SEQ]).then_inc(signal("fT_ready"), 1)
            modulate(3, "fox")

            dve.wait_ge(sem("consts_ready"), 2)

            def p_out(m):
                h, qt = divmod(m, 2)
                wait(dve, "po_full", m + 1)
                run.run(dve.reciprocal(stat[:, 12:13], stat[:, 10 + m % 2:11 + m % 2]))
                ts(u[:, qt, h * HD:(h + 1) * HD], psum[7][:, 0:HD], stat[:, 12:13], None, ALU.mult)\
                    .then_inc(signal("o_prompt_done"), 1)

            for n in range(2 * FH):
                h, qt = divmod(n, 2)
                wait(dve, "ps_full", n + 1)
                if n >= 2:
                    wait(dve, "p_turned", n - 1)
                s, bank = p_sc[:, n % 2, :], psum[2 + n % 2]
                run.do(stt(s[:, qt * P:(qt + 1) * P], bank[:, qt * P:(qt + 1) * P], f_p[:, qt, h:h + 1], causal[:, :],
                           ALU.add, ALU.add))
                if qt:
                    run.do(ts(s[:, 0:P], bank[:, 0:P], f_p[:, qt, h:h + 1], None, ALU.add))
                run.settle()
                dve.tensor_reduce(stat[:, 8 + n % 2:9 + n % 2], s[:, 0:P * (qt + 1)], AX, ALU.max, negate=True)\
                   .then_inc(signal("p_max_ready"), 1)
                if n >= 1:
                    p_out(n - 1)
            p_out(2 * FH - 1)

            dve.wait_ge(sem("fox_cleared"), 1)
            dve.wait_ge(sem("fqc_loaded"), 128)

            def prepare(b, s):
                run.do(dve.tensor_copy(qz[:, s, :, 0:DT], qT[:, 4 * s:4 * s + 4, ds(b * DT + SEQ, DT)]))
                dve.tensor_copy(kn[:, s, :, :], kTs[:, 4 * s:4 * s + 4, ds(b * DT, DT)]).then_inc(sem("kn_ready"), 1)

            def keys_turned(g, i):
                dve.wait_ge(kt_full, g * 8 + (2 * i + 2))
                if i >= 2:
                    dve.wait_ge(sem("s_full"), g * 4 + (i - 1))
                dve.tensor_copy(kt_sb[:, i % 2, 512:1024], psum[1][:, :]).then_inc(sem("kt_dve"), 1)

            def group_out(g, s):
                dve.wait_ge(fo_full, g + 1)
                run.run(dve.reciprocal(stat[:, 20 + s:21 + s], stat[:, 18 + s:19 + s]))
                ts(og[:, s, :], psum[7][:, 256:256 + HD], stat[:, 20 + s:21 + s], None, ALU.mult)\
                    .then_inc(sem("og_ready"), 1)

            def probs_turned(g):
                dve.wait_ge(sem("pt_full"), g * 3 + 3)
                run.do(dve.tensor_copy(pTn[0:DT, :], psum[7][0:DT, 0:P]))
                dve.tensor_copy(pT[:, 4:8, :].rearrange("p a b -> p (a b)"), psum[6][:, :]).then_inc(sem("pt_dve"), 1)

            def fox_group(g, b, s, stored, first=False):
                prepare(b, s)
                keys_turned(g, 0)
                keys_turned(g, 1)
                if not first:
                    probs_turned(g - 1)
                keys_turned(g, 2)
                if not first:
                    if stored is not None:
                        dve.wait_ge(sem(f"og_stored{1 - s}"), stored)
                    group_out(g - 1, 1 - s)
                keys_turned(g, 3)
                dve.wait_ge(sem("s_full"), g * 4 + 4)
                dve.wait_ge(sem(f"fetched{s}"), b * 80 + 80)
                run.run(tt(key_bias[s][:, PAST:], key_bias[s][:, PAST:], causal8[:, :], ALU.add))
                run.do(stt(sc[:, 0:512], psum[2][:, :], fqc[:, ds(g, 1)], key_bias[s][:, 0:512], ALU.add, ALU.add))
                run.do(stt(sc[:, 512:1024], psum[3][:, :], fqc[:, ds(g, 1)], key_bias[s][:, 512:1024], ALU.add, ALU.add))
                stt(sc[:, PAST:], psum[4][:, 0:DT], fqc[:, ds(g, 1)], key_bias[s][:, PAST:], ALU.add, ALU.add)\
                    .then_inc(sem("sc_ready"), 1)
                run.settle()
                dve.wait_ge(sem("sc_ready"), g + 1)
                dve.tensor_reduce(stat[:, 16:17], sc, AX, ALU.max, negate=True).then_inc(sem("max_ready"), 1)

            fox_group(0, 0, 0, None, first=True)
            fox_group(1, 0, 1, None)
            fox_group(2, 1, 0, None)
            fox_group(3, 1, 1, 16)
            per, start = FOX_STEPS, run.n
            with dve.Fori(2, DB) as b:
                run.base, run.n = b * (2 * per) + (start - 4 * per), 0
                for s in range(2):
                    fox_group(b * 2 + s, b, s, (b + (s - 1)) * 16)
                assert run.n == 2 * per, run.n
            run.base, run.n = start + (DB - 2) * 2 * per, 0
            probs_turned(2 * DB - 1)
            dve.wait_ge(sem("og_stored1"), 16 * (DB - 1))
            group_out(2 * DB - 1, 1)
            wait(dve, "o_prompt_done", 2 * FH)
            for _ in range(2):
                dve.nop().then_inc(sem("u_ready"), 1)
            dve.wait_ge(sem("og_loaded"), 16 * DB)
            dve.nop().then_inc(sem("u_ready"), 1)
            residual(2, "fox_wo")
            moe_front(1)
            experts(1)
            overflow(1)
            combine(1)

        @block.tensor
        def _(pe):
            mm = pe.matmul

            def turn_stage(stage):
                for t, (t0, r) in enumerate(TILES):
                    u_ready(pe, stage, t)
                    for half in range(2):
                        job = (stage, t, half)
                        turn.wait_free(pe, job)
                        for i in range(4):
                            c = 4 * half + i
                            ins = pe.transpose(psum[turn.bank(job)][:, i * P:i * P + r],
                                               u[0:r, t, c:D:KT], ident[0:r, 0:r])
                        ins.then_inc(turn.is_full(job), 1)
                turn.wait_drained(pe, (stage, 2, 1))

            def product(job, t, unit):
                t0, r = TILES[t]
                lin.wait_free(pe, job)
                for c in range(KT):
                    ins = mm(psum[lin.bank(job)][0:r, :], uT[:, c, t0:t0 + r], ring_pair(unit)[:, c, :],
                             start=(c == 0), stop=(c == KT - 1))
                ins.then_inc(lin.is_full(job), 1)

            def linear(name, j):
                unit = weights_landed(pe, (name, j))
                for t in range(3):
                    product((name, j, t), t, unit)

            def ada(n):
                unit = weights_landed(pe, ("ada", n))
                adas.wait_free(pe, n)
                for c in range(KT):
                    for i in range(4):
                        ins = mm(psum[adas.bank(n)][32 * i:32 * i + 32, 0:P], cT[:, c, :],
                                 ring_pair(unit)[:, c, i * P:(i + 1) * P], start=(c == 0), stop=(c == KT - 1),
                                 tile_position=(0, 32 * i), skip_group_check=True)
                ins.then_inc(adas.is_full(n), 1)

            pe.wait_ge(sem("consts_ready"), 1)
            wait(pe, "c_silu", 1)
            for c in range(KT):
                ins = pe.transpose(psum[7][:, c * 16:c * 16 + 9], ln[0:9, 1, c:D:KT], ident[0:9, 0:9])
            ins.then_inc(signal("c_turned"), 1)
            wait(pe, "cT_ready", 1)
            for n in range(4):
                ada(n)
            pe.wait_ge(sem("lf_loaded"), 16)
            for h in range(FH):
                ins = pe.transpose(psum[turn.bank(("lf",))][:, h * 64:(h + 1) * 64], mgate[0:64, 0, h:D:FH],
                                   ident[0:64, 0:64])
            ins.then_inc(turn.is_full(("lf",)), 1)
            turn.wait_freed(pe, ("lf",))
            pe.wait_ge(sem("consts_ready"), 2)
            for n in range(2):
                lin.wait_free(pe, ("suf", n))
                for page in range(PAGES - 1, 4 * n - 1, -1):
                    width = min(512, (page + 1) * P - n * 512)
                    first = (PAGES - 1 - page) * P + n * 512
                    ins = mm(psum[lin.bank(("suf", n))][0:64, 0:width], lf_pages[:, 0, page * 64:(page + 1) * 64],
                             later[:, first:first + width], start=(page == PAGES - 1), stop=(page == 4 * n),
                             skip_group_check=True)
                ins.then_inc(lin.is_full(("suf", n)), 1)
            turn_stage("gla")
            pe.wait_ge(sem("small_loaded"), 16 * SMALL_LOADS)
            for c in range(KT):
                ins = mm(psum[7][0:RANK, 0:TOK], w_small[:, c, 0:RANK], uT[:, c, :], start=(c == 0), stop=(c == KT - 1))
            ins.then_inc(signal("alr_full"), 1)
            n = 4
            for j in range(W_IN_N // 512):
                linear("w_in", j)
                for _ in range(4):
                    ada(n)
                    n += 1

            wait(pe, "alrT_ready", 1)
            adas.wait_drained(pe, ADA_N - 1)
            for t, (t0, r) in enumerate(TILES):
                mm(psum[5 + t][0:r, :], alrT[:, t0:t0 + r], w_a2[:, :], start=True, stop=True)\
                    .then_inc(signal("z_full"), 1)
            lin.wait_drained(pe, ("w_in", 5, 2))
            for t, (t0, r) in enumerate(TILES):
                mask, same, group, groups = state_of(t)
                wait(pe, "la_ready", 3 if t == 0 else t + 1)
                if t:
                    u_ready(pe, "gla_o", t - 1)
                mm(psum[0][0:r, :], mask[0:r, 0:r], la[0:r, t, :], start=True, stop=True)
                mm(psum[1][0:r, :], same[0:r, 0:r], la[0:r, t, :], start=True, stop=True)
                for h in range(GH):
                    ins = mm(psum[2][:, h * groups:(h + 1) * groups], la[0:r, t, h * GK:(h + 1) * GK], group[0:r, :],
                             start=True, stop=True)
                ins.then_inc(signal("dec_full"), 1)
                wait(pe, "qd_ready", t + 1)
                for h in range(GH):
                    ins = pe.transpose(psum[3][:, h * P:h * P + r], q[0:r, t, h * GK:(h + 1) * GK], ident[0:r, 0:r])
                ins.then_inc(signal("qdT_full"), 1)
                wait(pe, "kd_ready", t + 1)
                for h in range(GH):
                    ins = pe.transpose(psum[4][:, h * P:h * P + r], kd[0:r, h * GK:(h + 1) * GK], ident[0:r, 0:r])
                ins.then_inc(signal("kdT_full"), 1)
                wait(pe, "qdT_ready", t + 1)
                wait(pe, "kdT_ready", t + 1)
                for h in range(GH):
                    ins = mm(psum[5][0:r, h * P:h * P + r], kdT[:, h, 0:r], qdT[:, h, 0:r], start=True, stop=True)
                ins.then_inc(signal("att_full"), 1)
                wait(pe, "att_ready", t + 1)
                wait(pe, "ke_ready", t + 1)

                def o_part(h, lhsT, rhs, start=False, stop=False):
                    return mm(psum[6 + h // 2][0:r, (h % 2) * GV:(h % 2 + 1) * GV], lhsT, rhs,
                              start=start and h % 2 == 0, stop=stop, skip_group_check=True)

                def update(h, lhsT, rhs):
                    return mm(psum[h // 2][:, (h % 2) * GV:(h % 2 + 1) * GV], lhsT, rhs, start=True, stop=True)

                for h in range(GH):
                    o_part(h, att[0:r, h, 0:r], v[0:r, t, h * GV:(h + 1) * GV], start=True)
                if t < ST:
                    for g in range(2):
                        c = 2 * t + g
                        if c:
                            wait(pe, "prompt_state_ready", c)
                            for h in range(GH):
                                ins = o_part(h, qz64[:, h, g * P:(g + 1) * P], s_p[:, h * GV:(h + 1) * GV], stop=(g == 1))
                            if g:
                                ins.then_inc(signal("o_full"), 1)
                        rows = slice(64 * g, 64 * g + 64)
                        for h in range(GH):
                            ins = update(h, k[rows, t, h * GK:(h + 1) * GK], v[rows, t, h * GV:(h + 1) * GV])
                        ins.then_inc(signal("upd_full"), 1)
                else:
                    for b in range(DB):
                        wait(pe, "kem_ready", b + 1)
                        pe.wait_ge(sem(f"state_loaded{b % 2}"), 16 * (b // 2 + 1))
                        for h in range(GH):
                            ins = o_part(h, qz8[:, h, b * 64:(b + 1) * 64], s_in[:, b % 2, h * GV:(h + 1) * GV],
                                         stop=(b == DB - 1))
                        if b == DB - 1:
                            ins.then_inc(signal("o_full"), 1)
                        if b:
                            wait(pe, "sup_ready", b)
                        for h in range(GH):
                            ins = update(h, kem[0:64, h * GK:(h + 1) * GK], v[0:64, t, h * GV:(h + 1) * GV])
                        ins.then_inc(signal("upd_full"), 1)
            turn_stage("gla_o")
            for j in range(2):
                linear("gla_wo", j)

            def moe_front(l):
                stage = f"moe{l}"
                turn_stage(stage)
                pe.wait_ge(sem("router_loaded"), 16 * (2 + 3 * l))
                for t, (t0, r) in enumerate(TILES):
                    for c in range(KT):
                        ins = mm(psum[5 + t][0:r, 0:NE], uT[:, c, t0:t0 + r], w_small[:, c, :],
                                 start=(c == 0), stop=(c == KT - 1))
                    ins.then_inc(signal("router_full"), 1)
                unit = weights_landed(pe, ("sh_gu", l))
                for t in range(3):
                    product(("sh_gu", l, t), t, unit)
                for t, (t0, r) in enumerate(TILES):
                    wait(pe, "chosen", 3 * l + t + 1)
                    if t == ST:
                        for s in range(3):
                            rs = tile_rows(s)
                            mm(psum[7][:, NE:2 * NE], ones[0:rs, :], sel[0:rs, s, :], start=(s == 0), stop=(s == 2))
                    for s in range(t):
                        mm(psum[5 + t][0:r, 0:NE], ones[:, 0:r], sel[:, s, :], start=(s == 0), stop=False)
                    mm(psum[5 + t][0:r, 0:NE], before[0:r, 0:r], sel[0:r, t, :], start=(t == 0), stop=True)\
                        .then_inc(signal("rank_full"), 1)
                unit = weights_landed(pe, ("sh_d", l))
                for t, (t0, r) in enumerate(TILES):
                    lin.wait_freed(pe, ("sh_gu", l, t))
                    job = ("h_sh", l, t)
                    turn.wait_free(pe, job)
                    for f in range(2):
                        ins = pe.transpose(psum[turn.bank(job)][:, f * P:f * P + r], h_sh[0:r, f * P:(f + 1) * P],
                                           ident[0:r, 0:r])
                    ins.then_inc(turn.is_full(job), 1)
                    turn.wait_freed(pe, job)
                    for j in range(2):
                        job = ("sh_d", l, j, t)
                        lin.wait_free(pe, job)
                        for f in range(2):
                            ins = mm(psum[lin.bank(job)][0:r, :], hT_sh[:, f, 0:r],
                                     ring[:, unit, f * D + j * 512:f * D + (j + 1) * 512], start=(f == 0), stop=(f == 1))
                        ins.then_inc(lin.is_full(job), 1)
                wait(pe, "tab2_ready", l + 1)
                job = ("places", l)
                turn.wait_free(pe, job)
                for b in range(BLOCKS):
                    ins = pe.transpose(psum[turn.bank(job)][:, b * NE:(b + 1) * NE],
                                       tab2[:, b, :, :].rearrange("e h r -> e (h r)"), ident[0:NE, 0:NE])
                ins.then_inc(turn.is_full(job), 1)
                turn.wait_drained(pe, job)
                lin.wait_drained(pe, ("sh_d", l, 1, 2))

            def turn_rows(s, event):
                for j in range(4):
                    ins = pe.transpose(psum[3 + s][:, j * P:(j + 1) * P], xg[:, s, j:512:4], ident[:, :])
                ins.then_inc(event, 1)

            def gate_up(s, gu, event):
                for kk in range(KT):
                    half, j = divmod(kk, 4)
                    for c in range(2):
                        ins = mm(psum[s][64 * c:64 * c + 64, 0:2 * P].rearrange("p (a n) -> p a n", a=2),
                                 xT[:, s, j * P + 64 * half:j * P + 64 * half + 64],
                                 gu[:, kk, :, c * P:(c + 1) * P], start=(kk == 0), stop=(kk == KT - 1),
                                 skip_group_check=True)
                ins.then_inc(event, 1)

            def turn_hidden(s, event):
                pe.transpose(psum[s][:, 2 * P:3 * P], hs[:, s, :], ident[:, :]).then_inc(event, 1)

            def down(s, w, event):
                for f in range(2):
                    for c in range(2):
                        ins = mm(psum[3 + s][64 * c:64 * c + 64, :], hT[:, s, 64 * f:64 * f + 64],
                                 w[:, f, c * 512:(c + 1) * 512], start=(f == 0), stop=(f == 1),
                                 skip_group_check=True)
                ins.then_inc(event, 1)

            def experts(l):
                base = l * NE
                loads = [wr.items[("gate", l, s)][1] for s in range(3)] , [wr.items[("up", l, s)][1] for s in range(3)], \
                        [wr.items[("down", l, s)][1] for s in range(3)]

                def rows(e, s, i, fresh=False):
                    pe.wait_ge(sem(f"xg_full{s}"), (i + (Y_STORED[l - 1][s] if l else 0) + 1) * 16)
                    if not fresh:
                        pe.wait_ge(sem("y_ready"), e + (base - 2))
                    turn_rows(s, sem("xT_full"))

                def one(e, s, i, first=False, fresh=False, last=False):
                    pe.wait_ge(sem("xT_ready"), e + (base + 1))
                    for n in range(2):
                        pe.wait_ge(unit_full[3 * s + n], (i + loads[n][s]) * 16)
                    gu = ring[:, 3 * s:3 * s + 2, :].rearrange("p a (k n) -> p k a n", n=FE)
                    gate_up(s, gu, h_full)
                    if not last:
                        s1 = (s + 1) % 3
                        rows(e + 1, s1, i + (s + 1) // 3, fresh=fresh)
                    if not first:
                        s0 = (s + 2) % 3
                        i0 = i if s else i - 1
                        pe.wait_ge(unit_full[3 * s0 + 2], (i0 + loads[2][s0]) * 16)
                        pe.wait_ge(sem("hT_ready"), e + base)
                        down(s0, ring[:, 3 * s0 + 2, :].rearrange("p (f n) -> p f n", f=2), y_full)
                    pe.wait_ge(sem("h_ready"), e + (base + 1))
                    turn_hidden(s, sem("hT_full"))

                wait(pe, "index_ready", l + 1)
                rows(0, 0, 0, fresh=True)
                for e in range(3):
                    one(e, e, 0, first=(e == 0), fresh=(e < 2))
                with pe.Fori(1, NE // 3) as i:
                    for s in range(3):
                        one(i * 3 + s, s, i)
                one(NE - 1, 0, NE // 3, last=True)
                pe.wait_ge(unit_full[2], (NE // 3 + loads[2][0]) * 16)
                pe.wait_ge(sem("hT_ready"), base + NE)
                down(0, ring[:, 2, :].rearrange("p (f n) -> p f n", f=2), y_full)

            def overflow(l):
                wait(pe, "over_ready", l + 1)
                any_ = pe.value_load(ov_idx[0:1, 0:1], min_val=0, max_val=1023)
                with pe.If(any_ < 512):
                    with pe.Fori(0, OVER) as j:
                        col = pe.value_load(ov_idx[0:1, ds(j, 1)], min_val=0, max_val=1023)
                        with pe.If(col < 512):
                            pe.wait_ge(sem(f"over_xg{l}"), j * 16 + 16)
                            pe.wait_ge(sem("y_ready"), NE * (l + 1))
                            turn_rows(0, sem(f"over_pe{l}"))
                            pe.wait_ge(sem(f"over_dve{l}"), j * 3 + 1)
                            pe.wait_ge(sem(f"over_w{l}"), j * 48 + 48)
                            for kk in range(KT):
                                half, jj = divmod(kk, 4)
                                for c in range(2):
                                    for a, w in enumerate((ov_gate, ov_up)):
                                        ins = mm(psum[0][64 * c:64 * c + 64, a * P:(a + 1) * P],
                                                 xT[:, 0, jj * P + 64 * half:jj * P + 64 * half + 64],
                                                 w[:, :, :].rearrange("p a (k n) -> p (a k) n", n=FE)
                                                 [:, kk, c * P:(c + 1) * P], start=(kk == 0 and a == 0),
                                                 stop=(kk == KT - 1), skip_group_check=True)
                            ins.then_inc(sem(f"over_pe{l}"), 1)
                            pe.wait_ge(sem(f"over_dve{l}"), j * 3 + 2)
                            turn_hidden(0, sem(f"over_pe{l}"))
                            pe.wait_ge(sem(f"over_dve{l}"), j * 3 + 3)
                            down(0, ov_down, sem(f"over_pe{l}"))
                        with pe.Else():
                            pe.nop()
                        pe.nop()
                    pe.nop()
                with pe.Else():
                    pe.nop()

            moe_front(0)
            experts(0)
            overflow(0)

            turn_stage("kv")
            pe.wait_ge(sem("router_loaded"), 48)
            for t, (t0, r) in enumerate(TILES):
                for c in range(KT):
                    ins = mm(psum[5 + t][0:r, 0:FH], uT[:, c, t0:t0 + r], w_small[:, c, 0:FH],
                             start=(c == 0), stop=(c == KT - 1))
            ins.then_inc(signal("lf_full"), 1)
            for j in range(4):
                unit = weights_landed(pe, ("kv", j))
                for t in range(3):
                    product(("kv", j, t), t, unit)
                    if j < 2:
                        slot = (3 * j + t) % 4
                        r = tile_rows(t)
                        lin.wait_freed(pe, ("kv", j, t))
                        job = ("kT", j, t)
                        turn.wait_free(pe, job)
                        for i in range(4):
                            ins = pe.transpose(psum[turn.bank(job)][:, i * P:i * P + r],
                                               kv_rows[0:r, slot, i * P:(i + 1) * P], ident[0:r, 0:r])
                        ins.then_inc(turn.is_full(job), 1)
            wait(pe, "lf_ready", 1)
            mm(psum[5][:, 64:64 + FH], upto[:, :], lf[:, 0, :], start=True, stop=True)
            mm(psum[6][:, 64:64 + FH], ones[:, :], lf[:, 0, :], start=True, stop=False)
            mm(psum[6][:, 64:64 + FH], upto[:, :], lf[:, 1, :], start=False, stop=True)
            mm(psum[7][0:64, 64:64 + FH], upto8[:, :], lf[0:64, 2, :], start=True, stop=True).then_inc(signal("f_full"), 1)
            wait(pe, "f_ready", 1)
            for t in range(2):
                ins = pe.transpose(psum[7][0:FH, t * P:(t + 1) * P], f_p[:, t, :], ident[:, :])
            ins.then_inc(signal("fT_full"), 1)
            turn_stage("fox")
            for h in range(FH):
                j, i = divmod(h, 4)
                unit = weights_landed(pe, ("w_q", j))
                job = ("w_q", h)
                lin.wait_free(pe, job)
                for c in range(KT):
                    ins = mm(psum[lin.bank(job)][:, 0:TOK], ring_pair(unit)[:, c, i * P:(i + 1) * P], uT[:, c, :],
                             start=(c == 0), stop=(c == KT - 1))
                ins.then_inc(lin.is_full(job), 1)
            lin.wait_drained(pe, ("w_q", 7))

            wait(pe, "fT_ready", 1)
            pe.wait_ge(sem("fox_cleared"), 1)
            turn.wait_drained(pe, ("kT", 1, 2))

            def p_rest(m):
                h, qt = divmod(m, 2)
                wait(pe, "p_exp_ready", m + 1)
                for a in range(qt + 1):
                    ins = pe.transpose(psum[5 + m % 2][:, a * P:(a + 1) * P], p_sc[:, m % 2, a * P:(a + 1) * P], ident[:, :])
                ins.then_inc(signal("p_turned"), 1)
                wait(pe, "p_T_ready", m + 1)
                if m:
                    wait(pe, "o_prompt_done", m)
                for a in range(qt + 1):
                    ins = mm(psum[7][:, 0:HD], p_T[:, m % 2, a, :], vp[:, a, h * HD:(h + 1) * HD],
                             start=(a == 0), stop=(a == qt))
                ins.then_inc(signal("po_full"), 1)

            for n in range(2 * FH):
                h, qt = divmod(n, 2)
                nk = P * (qt + 1)
                if n >= 2:
                    wait(pe, "p_max_ready", n - 1)
                mm(psum[2 + n % 2][:, 0:nk], qT[:, h, qt * P:(qt + 1) * P], kTp[:, h, 0:nk], start=True, stop=False)
                mm(psum[2 + n % 2][:, 0:nk], selneg[:, h, :], fT[:, 0:nk], start=False, stop=True)\
                    .then_inc(signal("ps_full"), 1)
                if n >= 1:
                    p_rest(n - 1)
            p_rest(2 * FH - 1)
            wait(pe, "o_prompt_done", 2 * FH)

            k_loads = [wr.items[("fox_k", s)][1] for s in range(2)]
            v_loads = [wr.items[("fox_v", s)][1] for s in range(2)]

            def turn_keys(g, i, s, b):
                if i == 0:
                    pe.wait_ge(unit_full[4 * s], (b * PAGES + k_loads[s]) * 16)
                for n in range(2):
                    if isinstance(g, bass.RuntimeValue) or g or i:
                        pe.wait_ge(sem(("kt_act", "kt_dve")[n]), g * 4 + i)
                    for a in range(4):
                        ins = pe.transpose(psum[n][:, a * P:(a + 1) * P],
                                           ring_pair(4 * s)[:, 4 * n + a, i * P:(i + 1) * P], ident[:, :])
                    ins.then_inc(kt_full, 1)

            def head_scores(g, i, s):
                pe.wait_ge(sem("kt_act"), g * 4 + (i + 1))
                pe.wait_ge(sem("kt_dve"), g * 4 + (i + 1))
                if i == 0:
                    pe.wait_ge(sem("kn_ready"), g + 1)
                    if isinstance(g, bass.RuntimeValue) or g:
                        pe.wait_ge(sem("sc_ready"), g)
                for n in range(2):
                    mm(psum[2 + n][32 * i:32 * i + 32, :], qz[:, s, i, :], kt_sb[:, i % 2, n * 512:(n + 1) * 512],
                       start=True, stop=True, tile_position=(0, 32 * i))
                mm(psum[4][32 * i:32 * i + 32, 0:DT], qz[:, s, i, :], kn[:, s, i, :], start=True, stop=True,
                   tile_position=(0, 32 * i)).then_inc(sem("s_full"), 1)

            def turn_probs(g):
                pe.wait_ge(sem("exp_ready"), g + 1)
                for n in range(2):
                    for a in range(4):
                        ins = pe.transpose(psum[5 + n][:, a * P:(a + 1) * P],
                                           sc[:, (4 * n + a) * P:(4 * n + a + 1) * P], ident[:, :])
                    ins.then_inc(sem("pt_full"), 1)
                if isinstance(g, bass.RuntimeValue) or g:
                    pe.wait_ge(sem("og_ready"), g)
                pe.transpose(psum[7][0:DT, 0:P], sc[:, PAST:CTX], ident[:, :]).then_inc(sem("pt_full"), 1)

            def values(g, s, b):
                pe.wait_ge(unit_full[4 * s + 2], (b * PAGES + v_loads[s]) * 16)
                pe.wait_ge(sem("pt_act"), g + 1)
                pe.wait_ge(sem("pt_dve"), g + 1)
                for a in range(PAGES):
                    for i in range(4):
                        mm(psum[7][32 * i:32 * i + 32, 256:256 + HD], pT[:, a, 32 * i:32 * i + 32],
                           ring_pair(4 * s + 2)[:, a, i * P:(i + 1) * P], start=(a == 0), stop=False,
                           tile_position=(0, 32 * i), skip_group_check=True)
                for i in range(4):
                    ins = mm(psum[7][32 * i:32 * i + 32, 256:256 + HD], pTn[0:DT, 32 * i:32 * i + 32],
                             vn[0:DT, s, i * P:(i + 1) * P], start=False, stop=True,
                             tile_position=(0, 32 * i), skip_group_check=True)
                ins.then_inc(fo_full, 1)

            def fox_group(g, s, b, b0, first=False):
                turn_keys(g, 0, s, b)
                turn_keys(g, 1, s, b)
                if not first:
                    turn_probs(g - 1)
                head_scores(g, 0, s)
                turn_keys(g, 2, s, b)
                if not first:
                    values(g - 1, 1 - s, b0)
                head_scores(g, 1, s)
                turn_keys(g, 3, s, b)
                head_scores(g, 2, s)
                head_scores(g, 3, s)

            fox_group(0, 0, 0, 0, first=True)
            fox_group(1, 1, 0, 0)
            with pe.Fori(1, DB) as b:
                for s in range(2):
                    fox_group(b * 2 + s, s, b, b + (s - 1))
            turn_probs(2 * DB - 1)
            values(2 * DB - 1, 1, DB - 1)

            turn_stage("fox_o")
            for j in range(2):
                linear("fox_wo", j)
            moe_front(1)
            experts(1)
            overflow(1)


def kernel(**inputs):
    import concourse.bacc as bacc
    from concourse.bass_utils import run_bass_kernel_spmd

    nc = bacc.Bacc("TRN2", target_bir_lowering=False, num_devices=1)
    arrays, w, o = {}, {}, {}
    for name in INPUTS:
        a = np.ascontiguousarray(inputs[name])
        arrays[f"in_{name}"] = a
        w[name] = nc.dram_tensor(f"in_{name}", a.shape, mybir.dt.from_np(a.dtype), kind="ExternalInput").ap()
    for name, shape in OUTPUTS:
        o[name] = nc.dram_tensor(f"out_{name}", shape, F32, kind="ExternalOutput").ap()
    hybrid_trunk_step(nc, w, o)
    r = run_bass_kernel_spmd(nc, [arrays], core_ids=[0])
    return tuple(r.results[0][f"out_{name}"] for name, _ in OUTPUTS)
```

```python
from contextlib import ExitStack

import concourse.bass as bass
import numpy as np
from concourse import mybir

F32 = mybir.dt.float32
I32 = mybir.dt.int32
ALU = mybir.AluOpType
ACT = mybir.ActivationFunctionType
AX = mybir.AxisListType.X
ds = bass.ds

P = 128
D = 1024
KT = D // P
SEQ, DB, DT = 256, 8, 8
TOK = SEQ + DB * DT
TILES = [(0, 128), (128, 128), (256, 64)]
ST = 2
GH, GK, GV, RANK, CHUNK = 4, 128, 256, 16, 64
GD = GH * GK
TAU = 16.0
FH, HD = 8, 128
PAGES, PAGE = 8, 128
PAST = PAGES * PAGE
CTX = PAST + DT
NE, TOPK, NG, TOPG, FE = 64, 8, 8, 4, 256
CAP = 64
BLOCKS = TOK // CAP
OVER = (TOK * TOPK) // (CAP + 1)
OVER_GROUPS = OVER // 8 + 1
OVER_LIST = 8 * (OVER_GROUPS + 1)
ALPHA = 4.0 ** 0.25
LN_EPS, RMS_EPS = 1e-5, 1e-6
ROUTED = 2.5
NOBODY = 1 << 20
NEG = -1e30
ADA_N = 28
W_IN_N = 3072
FIRST_ADA = 10
ADA_AFTER = [3] * 6
UNIT = 2048
UNITS = 9

MOD_CHUNK = {("shift_a", 0): 0, ("scale_a", 0): 2, ("gate_a", 0): 4, ("shift_m", 0): 6, ("scale_m", 0): 8,
             ("gate_m", 0): 10, ("shift_a", 1): 12, ("scale_a", 1): 14, ("gate_a", 1): 16, ("shift_m", 1): 18,
             ("scale_m", 1): 20, ("gate_m", 1): 22, ("shift_kv", 1): 24, ("scale_kv", 1): 26}


class BankRing:

    def __init__(self, sem, name, banks, jobs):
        self.banks = banks
        self.at = {job: n for n, job in enumerate(jobs)}
        assert len(self.at) == len(jobs)
        self.full = [sem(f"{name}_full{b}") for b in banks]
        self.free = [sem(f"{name}_free{b}") for b in banks]

    def bank(self, job):
        return self.banks[self.at[job] % len(self.banks)]

    def wait_free(self, eng, job):
        n, k = divmod(self.at[job], len(self.banks))
        if n:
            eng.wait_ge(self.free[k], n)

    def wait_full(self, eng, job):
        n, k = divmod(self.at[job], len(self.banks))
        eng.wait_ge(self.full[k], n + 1)

    def is_full(self, job):
        return self.full[self.at[job] % len(self.banks)]

    def is_free(self, job):
        return self.free[self.at[job] % len(self.banks)]

    def wait_freed(self, eng, job):
        n, k = divmod(self.at[job], len(self.banks))
        eng.wait_ge(self.free[k], n + 1)

    def wait_drained(self, eng, job):
        last = self.at[job]
        for k in range(len(self.banks)):
            n = (last - k) // len(self.banks) + 1
            if n > 0:
                eng.wait_ge(self.free[k], n)


class Steps:

    def __init__(self, eng, sem):
        self.eng, self.sem, self.base, self.n = eng, sem, 0, 0

    def do(self, ins):
        ins.then_inc(self.sem, 1)
        self.n += 1

    def settle(self):
        self.eng.wait_ge(self.sem, self.base + self.n)

    def run(self, ins):
        self.do(ins)
        self.settle()


class WeightRing:

    def __init__(self):
        self.pos, self.loads, self.owner, self.items = 0, [0] * UNITS, [None] * UNITS, {}

    def take(self, key, units, freed_by, loads=1):
        if self.pos + units > UNITS:
            self.pos = 0
        u = self.pos
        self.pos = (u + units) % UNITS
        waits = {}
        for k in range(u, u + units):
            if self.owner[k] is not None:
                s, n = self.owner[k]
                waits[s.name] = (s, max(n, waits.get(s.name, (s, 0))[1]))
            self.owner[k] = freed_by
        self.loads[u] += loads
        self.items[key] = (u, self.loads[u], list(waits.values()))

    def at(self, unit):
        self.pos = unit


SMALL_LOADS = 6
Y_STORED = [[(l + 1) * len(range(s, NE, 3)) for s in range(3)] for l in range(2)]
KV_SLOTS = [((j, t), 3 * j + t if j < 2 else (6 + j - 2 if t == 2 else None)) for j in range(4) for t in range(3)]
FOX_STEPS = 6


INPUTS = ["x_prompt", "x_sample", "c_prompt", "c_sample", "state_gla", "cache_k", "cache_v", "cache_logf",
          "page_table", "gla_w_in", "gla_w_a2", "gla_b_a", "gla_norm_g", "gla_w_o", "kv_w_mod", "kv_b_mod",
          "kv_w", "fox_b_f", "fox_w_q", "fox_w_o", "ada_w", "ada_b", "ln_g", "ln_b", "router_w", "router_bias",
          "exp_w_gate", "exp_w_up", "exp_w_down", "sh_w_gate", "sh_w_up", "sh_w_down"]
OUTPUTS = [("y_prompt", (1, SEQ, D)), ("y_sample", (DB, DT, D)), ("gla_prompt", (1, 1, GH, GK, GV)),
           ("gla_sample", (1, DB, GH, GK, GV)), ("k_prompt", (1, SEQ, FH, HD)), ("v_prompt", (1, SEQ, FH, HD)),
           ("logf_prompt", (1, SEQ, FH)), ("k_sample", (DB, DT, FH, HD)), ("v_sample", (DB, DT, FH, HD)),
           ("logf_sample", (DB, DT, FH))]


def hybrid_trunk_step(nc, W, O):
    ctx = ExitStack()
    sems = {}

    def sem(name):
        if name not in sems:
            sems[name] = ctx.enter_context(nc.semaphore(name))
        return sems[name]

    def sb(name, shape, dt=F32):
        return ctx.enter_context(nc.sbuf_tensor(name, shape, dt))

    def scratch(name, shape, dt=F32):
        return nc.dram_tensor(name, shape, dt)

    def dram(ap, offset, dims):
        return bass.AP(tensor=ap.tensor, offset=offset, ap=dims)

    with ctx:
        mod_d = scratch("mod_d", [ADA_N // 2 * 32, D])[:, :]
        u_d = scratch("u_d", [TOK * 2, 512])[:, :]
        places_d = scratch("places_d", [NE * TOK, 1], I32)[:, :]
        pair_d = scratch("pair_d", [TOK * TOPK * 2, 512])[:, :]
        bias_d = scratch("bias_d", [FH * DB, CTX])[:, :]
        fq_d = scratch("fq_d", [DB * DT, FH])[:, :]
        og_d = scratch("og_d", [2 * DB * P, HD])[:, :]

        ring = sb("ring", [P, UNITS, UNIT])
        x = sb("x", [P, 3, D])
        u = sb("u", [P, 3, D])
        uT = sb("uT", [P, KT, TOK])
        mscale = sb("mscale", [P, 2, D])
        mshift = sb("mshift", [P, 2, D])
        mgate = sb("mgate", [P, 2, D])
        ln = sb("ln", [P, 2, D])
        work = sb("work", [P, 12200])
        ident = sb("ident", [P, P])
        ones = sb("ones", [P, P])
        upto = sb("upto", [P, P])
        before = sb("before", [P, P])
        upto64 = sb("upto64", [P, P])
        same64 = sb("same64", [P, P])
        upto8 = sb("upto8", [64, 64])
        same8 = sb("same8", [64, 64])
        group64 = sb("group64", [P, 2])
        group8 = sb("group8", [64, 8])
        causal = sb("causal", [P, P])
        causal8 = sb("causal8", [P, DT])
        tri8 = sb("tri8", [P, 8, 8])
        place0 = sb("place0", [P, NE])
        pair_id = sb("pair_id", [P, 3, TOPK], I32)
        half_id = sb("half_id", [P, 1])
        ov_code = sb("ov_code", [1, (BLOCKS - 1) * NE])
        cT = sb("cT", [P, KT, 32])
        ada_bias = sb("ada_bias", [P, 4, P])
        ada_out = sb("ada_out", [P, 4, P])
        w_small = sb("w_small", [P, KT, 64])
        w_a2 = sb("w_a2", [RANK, GD])
        b_a = sb("b_a", [P, GD])
        norm_g = sb("norm_g", [P, GV])
        r_bias = sb("r_bias", [P, NE])
        b_f = sb("b_f", [P, FH])
        pages = sb("pages", [1, DB * PAGES], I32)
        page_col = sb("page_col", [DB * PAGES, 1], I32)
        alrT = sb("alrT", [RANK, TOK])
        w8 = sb("w8", [P, 3, TOPK])
        ov_idx = sb("ov_idx", [1, OVER_LIST], I32)
        ov_e = sb("ov_e", [1, OVER_LIST], I32)
        eps = sb("eps", [P, 2])
        stat = sb("stat", [P, 64])

        psum = [ctx.enter_context(nc.psum_tensor(f"bank{i}", [P, 512], F32)) for i in range(8)]

        cursor = [0]

        def carve(n, *shape):
            v = work[:, cursor[0]:cursor[0] + n]
            cursor[0] += n
            assert cursor[0] <= 12200, cursor[0]
            if len(shape) == 2:
                return v.rearrange("p (a b) -> p a b", a=shape[0], b=shape[1])
            if len(shape) == 3:
                return v.rearrange("p (a b c) -> p a b c", a=shape[0], b=shape[1], c=shape[2])
            return v

        cursor[0] = 0
        q = carve(3 * GD, 3, GD)
        k = carve(3 * GD, 3, GD)
        gs = carve(3 * D, 3, D)
        la = carve(3 * GD, 3, GD)
        qz_all = carve(GH * 576)
        qz64 = qz_all[:, 0:GH * 384].rearrange("p (h n) -> p h n", h=GH)
        qz8 = qz_all[:, :].rearrange("p (h n) -> p h n", h=GH)
        s_in = carve(2 * D, 2, D)
        lf_pages = la
        later = gs[:, 0, :]
        s_out = ln
        s_p = mscale[:, 0, :]
        att = mscale[:, 1, 0:GD].rearrange("p (h t) -> p h t", h=GH)
        egT = mscale[:, 1, GD:GD + 32].rearrange("p (h g) -> p h g", h=GH)
        e_cum = mshift[:, 0, 0:GD]
        e_end = mshift[:, 0, GD:2 * GD]
        kd = mshift[:, 1, 0:GD]
        qdT = mshift[:, 1, GD:2 * GD].rearrange("p (h t) -> p h t", h=GH)
        kdT = mgate[:, 0, 0:GD].rearrange("p (h t) -> p h t", h=GH)
        kem = [mgate[:, 0, GD:2 * GD], kd]
        cum_sb = mgate[:, 1, 0:GD]
        z_neg = mgate[:, 1, GD:2 * GD]
        v = u
        cursor[0] = 0
        ysh = carve(3 * D, 3, D)
        moe_end = cursor[0]
        xg = carve(3 * 512, 3, 512)
        xT = carve(3 * 512, 3, 512)
        y_sb = carve(3 * 512, 3, 512)
        sil = carve(3 * P, 3, P)
        hs = carve(3 * P, 3, P)
        hT = carve(3 * P, 3, P)
        h_sh = carve(FE)
        hT_sh = carve(2 * P, 2, P)
        xidx = carve(BLOCKS * NE).bitcast(I32)
        yidx = carve(BLOCKS * NE).bitcast(I32)
        xi = carve(4).bitcast(I32)
        yi = carve(4).bitcast(I32)
        score = carve(NE)
        route = carve(10 * NE, 10, NE)
        sel = carve(3 * NE, 3, NE)
        wgt = carve(3 * NE, 3, NE)
        eq3 = mscale[:, 0, 0:TOPK * NE].rearrange("p (k e) -> p k e", k=TOPK)
        place8 = carve(3 * TOPK, 3, TOPK)
        place_i = carve(3 * TOPK, 3, TOPK).bitcast(I32)
        tab_i = mshift[0:NE, 1, 0:TOK].bitcast(I32)
        tab2 = mshift[0:NE, 0, 0:BLOCKS * P].rearrange("p (b h r) -> p b h r", b=BLOCKS, h=2)
        ov_row = mshift[0:1, 1, 512:512 + 4 * NE]
        cnt = carve(NE)
        ov_top = carve(OVER_LIST)
        ov_gate = mscale
        ov_up = mshift
        ov_down = u[:, 0:2, :]
        cursor[0] = moe_end
        y_pairs = carve(2 * TOPK * 512, 2, TOPK, 512)
        diag = uT[:, :, :].rearrange("p c n -> p (c n)")
        diag = [diag[0:r, t * TOPK * P:t * TOPK * P + TOPK * r].rearrange("p (k n) -> p k n", k=TOPK)
                for t, (_, r) in enumerate(TILES)]
        cursor[0] = 0
        kTp = carve(FH * SEQ, FH, SEQ)
        kTs = carve(FH * 64, FH, 64)
        qT = carve(FH * TOK, FH, TOK)
        vp = carve(2 * D, 2, D)
        kt_sb = carve(2 * PAST, 2, PAST)
        pT = carve(PAGES * P, PAGES, P)
        pTn = carve(P)
        qz = carve(2 * P, 2, 4, 32)
        kn = carve(2 * 32, 2, 4, DT)
        vn = carve(2 * 512, 2, 512)
        og = carve(2 * P, 2, P)
        f_p = carve(2 * FH, 2, FH)
        lf = carve(3 * FH, 3, FH)
        lf_t = carve(3 * FH, 3, FH)
        lf_m = carve(3 * FH, 3, FH)
        f_s = carve(FH)
        nf_s = carve(FH)
        fqc = carve(2 * DB)
        fT = mgate[0:FH, 0, 0:SEQ]
        selneg = mgate[0:FH, 1, :].rearrange("p (h t) -> p h t", h=FH)
        p_sc = kt_sb[:, 0, :].rearrange("p (a b) -> p a b", a=4)
        p_T = kt_sb[:, 1, :].rearrange("p (a b c) -> p a b c", a=4, b=2)
        key_bias = [m[:, :, :].rearrange("p a b -> p (a b)")[:, 0:CTX] for m in (mscale, mshift)]
        sc = ln[:, :, :].rearrange("p a b -> p (a b)")[:, 0:CTX]
        kv_rows = kt_sb[:, :, :].rearrange("p a (b n) -> p (a b) n", n=512)

        def tile_rows(t):
            return TILES[t][1]

        def ring_pair(unit):
            return ring[:, unit:unit + 2, :].rearrange("p a (c n) -> p (a c) n", n=512)

        def state_of(t):
            return (upto64, same64, group64, 2) if t < ST else (upto8, same8, group8, 8)

        moe_pe = ["router_full"] * 3 + ["rank_full"] * 3
        moe_act = ["sigmoid_ready"] * 3 + ["sh_silu_ready"] * 3
        moe_dve = ["chosen", "chosen", "route_done", "chosen", "route_done", "route_done",
                   "over_ready", "tab2_ready", "index_ready", "diag_ready"]
        events = {
            "pe_event": ["c_turned", "alr_full"] + ["z_full"] * 3
            + ["dec_full", "qdT_full", "kdT_full", "att_full", "upd_full", "o_full", "upd_full"] * 2
            + ["dec_full", "qdT_full", "kdT_full", "att_full"] + ["upd_full"] * (DB - 1) + ["o_full", "upd_full"]
            + moe_pe + ["lf_full", "f_full", "fT_full"] + ["ps_full"] * 3 + ["p_turned"]
            + ["ps_full", "p_turned", "po_full"] * (2 * FH - 3) + ["p_turned", "po_full"] * 2 + ["po_full"] + moe_pe,
            "act_event": ["c_silu", "cT_ready", "alrT_ready"] + ["z_log_ready"] * 3
            + ["e_ready", "e_end_ready", "qdT_ready", "rms_ready"] * 3 + moe_act + ["lf_log_ready"] + ["p_exp_ready"] * 2
            + ["p_exp_ready", "p_T_ready"] * (2 * FH - 2) + ["p_T_ready"] * 2 + moe_act,
            "dve_event": ["ada_added"] * (FIRST_ADA + ADA_AFTER[0])
            + sum([["ada_added"] * ADA_AFTER[j] + ["z_neg_ready", "la_ready"] for j in (1, 2, 3)], [])
            + ["ada_added"] * (ADA_AFTER[4] + ADA_AFTER[5])
            + ["end_gap_ready", "qd_ready", "kd_ready", "ke_ready", "kdT_ready", "att_ready",
               "prompt_state_ready", "prompt_state_ready"] * 2
            + ["end_gap_ready", "qd_ready", "kd_ready", "ke_ready", "kdT_ready", "att_ready"]
            + ["kem_ready"] + ["kem_ready", "sup_ready"] * (DB - 1) + ["sup_ready"] + moe_dve + ["lf_neg_ready", "lf_ready", "f_ready", "fT_ready"]
            + ["p_max_ready"] * 3 + ["p_max_ready", "o_prompt_done"] * (2 * FH - 3) + ["o_prompt_done"] * 3 + moe_dve,
        }
        counts, owner_of = {}, {}
        for s_name, order in events.items():
            for n, e_name in enumerate(order):
                counts.setdefault(e_name, []).append(n + 1)
                owner_of[e_name] = s_name
        signalled = {s_name: 0 for s_name in events}

        def wait(eng, event, n):
            eng.wait_ge(sem(owner_of[event]), counts[event][n - 1])

        def signal(event):
            s_name = owner_of[event]
            assert events[s_name][signalled[s_name]] == event, (event, signalled[s_name])
            signalled[s_name] += 1
            return sem(s_name)

        plan_jobs = [("suf", n) for n in range(2)]
        plan_jobs += [("w_in", j, t) for j in range(W_IN_N // 512) for t in range(3)]
        plan_jobs += [("gla_wo", j, t) for t in range(3) for j in range(2)]
        plan_jobs += [("sh_gu", 0, t) for t in range(3)] + [("sh_d", 0, j, t) for t in range(3) for j in range(2)]
        plan_jobs += [("comb", 0, t) for t in range(3)]
        plan_jobs += [("kv", j, t) for j in range(4) for t in range(3)] + [("w_q", h) for h in range(FH)]
        plan_jobs += [("fox_wo", j, t) for t in range(3) for j in range(2)]
        plan_jobs += [("sh_gu", 1, t) for t in range(3)] + [("sh_d", 1, j, t) for t in range(3) for j in range(2)]
        plan_jobs += [("comb", 1, t) for t in range(3)]
        lin = BankRing(sem, "lin", [0, 1, 2], plan_jobs)
        stages = ["gla", "gla_o", "moe0", "kv", "fox", "fox_o", "moe1"]
        turn_jobs = [("lf",)]
        for s in stages:
            turn_jobs += [(s, t, half) for t in range(3) for half in range(2)]
            if s in ("moe0", "moe1"):
                turn_jobs += [("h_sh", int(s[-1]), t) for t in range(3)] + [("places", int(s[-1]))]
            if s == "kv":
                turn_jobs += [("kT", j, t) for j in range(2) for t in range(3)]
        turn = BankRing(sem, "turn", [3, 4], turn_jobs)
        adas = BankRing(sem, "ada", [5, 6], range(ADA_N))

        def last_use(ring_of_banks, job):
            n, b = divmod(ring_of_banks.at[job], len(ring_of_banks.banks))
            return (ring_of_banks.full[b], n + 1)

        wr = WeightRing()
        h_full, y_full = sem("h_full"), sem("y_full")
        kt_full, fo_full = sem("kt_full"), sem("fo_full")

        def plan():
            ada = 0
            for _ in range(FIRST_ADA):
                wr.take(("ada", ada), 2, last_use(adas, ada))
                ada += 1
            for j in range(W_IN_N // 512):
                wr.take(("w_in", j), 2, last_use(lin, ("w_in", j, 2)))
                for _ in range(ADA_AFTER[j]):
                    wr.take(("ada", ada), 2, last_use(adas, ada))
                    ada += 1
            for j in range(2):
                wr.take(("gla_wo", j), 2, last_use(lin, ("gla_wo", j, 2)))

            def moe(l):
                wr.at(6)
                wr.take(("sh_gu", l), 2, last_use(lin, ("sh_gu", l, 2)), loads=2)
                wr.take(("sh_d", l), 1, last_use(lin, ("sh_d", l, 1, 2)))
                wr.at(0)
                for e in range(NE):
                    wr.take(("gate", l, e), 1, (h_full, NE * l + e + 1))
                    wr.take(("up", l, e), 1, (h_full, NE * l + e + 1))
                    wr.take(("down", l, e), 1, (y_full, NE * l + e + 1))

            moe(0)
            for j in range(4):
                wr.take(("kv", j), 2, last_use(lin, ("kv", j, 2)))
            for j in range(2):
                wr.take(("w_q", j), 2, last_use(lin, ("w_q", 4 * j + 3)))
            wr.at(0)
            for g in range(2 * DB):
                if g % 2 == 0:
                    wr.at(0)
                wr.take(("fox_k", g), 2, (kt_full, 8 * g + 8), loads=PAGES)
                wr.take(("fox_v", g), 2, (fo_full, g + 1), loads=PAGES)
            for j in range(2):
                wr.take(("fox_wo", j), 2, last_use(lin, ("fox_wo", j, 2)))
            moe(1)

        plan()
        unit_full = [sem(f"unit_full{n}") for n in range(UNITS)]

        def weights_landed(eng, key):
            unit, fills, _ = wr.items[key]
            eng.wait_ge(unit_full[unit], 16 * fills)
            return unit

        def mod_wait(eng, chunk):
            eng.wait_ge(sem(f"ada_stored{chunk % 4}"), 16 * (chunk // 4 + 1))

        mods = ["gla", "moe0", "kv", "fox", "moe1"]
        gates = ["gate_a0", "gate_m0", "gate_a1", "gate_m1"]
        NSUB = 4

        def over_blocks(eng, body):
            head = eng.value_load(ov_idx[0:1, 0:1], min_val=0, max_val=1023)
            with eng.If(head < 512):
                with eng.Fori(0, OVER_GROUPS) as group:
                    head = eng.value_load(ov_idx[0:1, ds(group * 8, 1)], min_val=0, max_val=1023)
                    with eng.If(head < 512):
                        with eng.Fori(0, 8) as k:
                            j = group * 8 + k
                            col = eng.value_load(ov_idx[0:1, ds(j, 1)], min_val=0, max_val=1023)
                            with eng.If(col < 512):
                                body(j)
                            with eng.Else():
                                eng.nop()
                            eng.nop()
                        eng.nop()
                    with eng.Else():
                        eng.nop()
                    eng.nop()
                eng.nop()
            with eng.Else():
                eng.nop()

        block = ctx.enter_context(nc.Block())

        @block.sync
        def _(sp):
            def w_chunk(ap, j):
                return ap.rearrange("(p c) n -> p c n", c=KT)[:, :, j * 512:(j + 1) * 512]

            def free_units(key):
                for s, n in wr.items[key][2]:
                    sp.wait_ge(s, n)
                return wr.items[key][0]

            def load_ada(n):
                unit = free_units(("ada", n))
                w = W["ada_w"][n // 12] if n < 24 else W["kv_w_mod"]
                b = W["ada_b"][n // 12] if n < 24 else W["kv_b_mod"]
                j = n % 12
                sp.dma_start(ring_pair(unit), w_chunk(w, j)).then_inc(unit_full[unit], 16)
                if n >= 4:
                    adas.wait_drained(sp, n - 4)
                off = b.offset + j * 512
                sp.dma_start(ada_bias[:, n % 4, :],
                             dram(b, off, [[P, 4], [0, 32], [1, P]])).then_inc(sem(f"ada_bias{n % 4}"), 16)

            def load_linear(key, ap, j):
                unit = free_units(key)
                sp.dma_start(ring_pair(unit), w_chunk(ap, j)).then_inc(unit_full[unit], 16)

            def load_shared(l):
                unit = free_units(("sh_gu", l))
                for n, w in enumerate((W["sh_w_gate"], W["sh_w_up"])):
                    sp.dma_start(ring_pair(unit)[:, :, n * FE:(n + 1) * FE],
                                 w[l].rearrange("(p c) n -> p c n", c=KT)).then_inc(unit_full[unit], 16)
                unit = free_units(("sh_d", l))
                sp.dma_start(ring[:, unit, :].rearrange("p (f n) -> p f n", f=2),
                             W["sh_w_down"][l].rearrange("(f p) n -> p f n", f=2)).then_inc(unit_full[unit], 16)

            def load_expert(l, e, s):
                for n, name in enumerate(("exp_w_gate", "exp_w_up")):
                    w = W[name][l, ds(e, 1)].rearrange("o (h p j) n -> p (o h) (j n)", h=2, j=4)
                    sp.dma_start(ring[:, 3 * s + n, :].rearrange("p (h m) -> p h m", h=2), w)\
                      .then_inc(unit_full[3 * s + n], 16)

            def load_down(l, e, s):
                w = W["exp_w_down"][l, ds(e, 1)].rearrange("o (f p) n -> p (o f) n", f=2)
                sp.dma_start(ring[:, 3 * s + 2, :].rearrange("p (f n) -> p f n", f=2), w)\
                  .then_inc(unit_full[3 * s + 2], 16)

            def load_experts(l):
                for e in range(3):
                    free_units(("gate", l, e))
                    free_units(("up", l, e))
                    load_expert(l, e, e)
                    free_units(("down", l, e))
                    load_down(l, e, e)
                base = l * NE

                def steady(e, s):
                    sp.wait_ge(h_full, e + (base - 2))
                    load_expert(l, e, s)
                    sp.wait_ge(y_full, e + (base - 2))
                    load_down(l, e, s)

                with sp.Fori(1, NE // 3) as i:
                    for s in range(3):
                        steady(i * 3 + s, s)
                steady(NE - 1, 0)

            def load_pages(g, b, s, first):
                page = [sp.value_load(pages[0:1, ds(b * PAGES + j, 1)], min_val=0,
                                      max_val=W["cache_k"].shape[0] - 1) for j in range(PAGES)]
                for kind, cache, at, freed in (("fox_k", W["cache_k"], 4 * s, (kt_full, g * 8 - 8)),
                                               ("fox_v", W["cache_v"], 4 * s + 2, (fo_full, g - 1))):
                    if first:
                        free_units((kind, g))
                    else:
                        sp.wait_ge(*freed)
                    for j in range(PAGES):
                        rows = cache[ds(page[j], 1)].rearrange("o r h d -> (o r) (h d)")
                        sp.dma_start(ring_pair(at)[:, j, :], rows[:, s * 512:(s + 1) * 512])\
                          .then_inc(unit_full[at], 16)

            for n in range(FIRST_ADA):
                load_ada(n)
            n = FIRST_ADA
            for j in range(W_IN_N // 512):
                load_linear(("w_in", j), W["gla_w_in"][0], j)
                for _ in range(ADA_AFTER[j]):
                    load_ada(n)
                    n += 1
            for j in range(2):
                load_linear(("gla_wo", j), W["gla_w_o"][0], j)
            load_shared(0)
            load_experts(0)
            sp.wait_ge(sem("pairs_loaded1"), 48)
            for j in range(4):
                load_linear(("kv", j), W["kv_w"], j)
            for j in range(2):
                load_linear(("w_q", j), W["fox_w_q"][0], j)
            sp.wait_ge(sem("small_loaded"), 16 * SMALL_LOADS)
            for s in range(2):
                load_pages(s, 0, s, True)
            with sp.Fori(1, DB) as b:
                for s in range(2):
                    load_pages(b * 2 + s, b, s, False)
            for j in range(2):
                load_linear(("fox_wo", j), W["fox_w_o"][0], j)
            load_shared(1)
            load_experts(1)

        @block.gpsimd
        def _(pool):
            run = Steps(pool, sem("pool_step"))

            def triangle(out, compare, base, pattern, cm, fill=0.0):
                run.run(pool.affine_select(out=out, in_=out, pattern=pattern, compare_op=compare, fill=fill,
                                           base=base, channel_multiplier=cm))

            run.do(pool.memset(cT[:, :, :], 0.0))
            run.do(pool.memset(ident[:, :], 1.0))
            run.settle()
            triangle(ident[:, :], ALU.is_equal, 0, [[-1, P]], 1)
            sem_const = sem("consts_ready")
            pool.nop().then_inc(sem_const, 1)
            pool.wait_ge(sem("page_col_loaded"), 16)
            pool.indirect_dma_start(
                out=mgate[0:DB * PAGES, 0, :], out_offset=None,
                in_=W["cache_logf"].rearrange("n r h -> n (r h)"),
                in_offset=bass.IndirectOffsetOnAxis(ap=page_col[:, 0:1], axis=0)).then_inc(sem("lf_loaded"), 16)
            pool.wait_ge(sem("lf_loaded"), 16)
            for m in (upto, before, upto64, same64, upto8, same8, later, ones, group64, group8):
                run.do(pool.memset(m[:, :], 1.0))
            run.do(pool.memset(causal[:, :], 0.0))
            run.do(pool.memset(eps[:, 0:1], LN_EPS))
            run.do(pool.memset(eps[:, 1:2], RMS_EPS))
            run.do(pool.memset(causal8[:, :], 0.0))
            run.do(pool.memset(tri8[:, :, :], 1.0))
            run.do(pool.memset(qz_all[:, :], 0.0))
            run.settle()
            triangle(upto[:, :], ALU.is_ge, 0, [[1, P]], -1)
            triangle(before[:, :], ALU.is_ge, -1, [[1, P]], -1)
            triangle(later[:, 7 * P:], ALU.is_ge, -1, [[-1, P]], 1)
            for m, w in ((same64, 64), (upto64, 64), (same8, 8), (upto8, 8)):
                size = m.shape[1] // w
                blocks = m[:, :].rearrange("p (b c) -> p b c", c=w)
                triangle(blocks, ALU.is_ge, 0, [[-w, size], [0, w]], 1)
                triangle(blocks, ALU.is_ge, w - 1, [[w, size], [0, w]], -1)
            triangle(upto64[:, :], ALU.is_ge, 0, [[1, P]], -1)
            triangle(upto8[:, :], ALU.is_ge, 0, [[1, 64]], -1)
            for m, w in ((group64, 64), (group8, 8)):
                size = m.shape[1]
                triangle(m[:, :], ALU.is_ge, 0, [[-w, size]], 1)
                triangle(m[:, :], ALU.is_ge, w - 1, [[w, size]], -1)
            triangle(causal[:, :], ALU.is_ge, 0, [[-1, P]], 1, NEG)
            for i in range(4):
                triangle(causal8[32 * i:32 * i + 32, :], ALU.is_ge, 0, [[-1, DT]], 1, NEG)
            triangle(tri8[:, :, :], ALU.is_ge, -1, [[1, 8], [-1, 8]], 0)
            run.do(pool.iota(place0[:, :].bitcast(I32), pattern=[[TOK, NE]], base=1, channel_multiplier=0))
            run.do(pool.iota(pair_id[:, :, :], pattern=[[P * TOPK, 3], [1, TOPK]], base=0,
                             channel_multiplier=TOPK))
            run.run(pool.memset(half_id[:, :], 0.0))
            triangle(half_id[:, :], ALU.is_ge, 63, [[0, 1]], -1, 1.0)
            run.do(pool.iota(ov_code[:, :].bitcast(I32), pattern=[[-1, (BLOCKS - 1) * NE]], base=1000 - NE,
                             channel_multiplier=0))
            run.settle()
            run.do(pool.tensor_copy(place0[:, :], place0[:, :].bitcast(I32)))
            run.do(pool.tensor_copy(ov_code[:, :], ov_code[:, :].bitcast(I32)))
            run.settle()
            pool.nop().then_inc(sem_const, 1)

            wait(pool, "o_full", 2)
            pool.memset(qz_all[:, :], 0.0).then_inc(sem("qz_cleared"), 1)

            def dispatch(l):
                pool.wait_ge(sem("u_ready"), 3 * (stages.index(f"moe{l}") + 1))
                run.run(pool.memset(tab_i, NOBODY))
                pool.dma_start(places_d.rearrange("(e r) o -> e (r o)", e=NE), tab_i)\
                    .then_inc(sem("places_blank"), 16)
                pool.wait_ge(sem("places_blank"), 16 * (l + 1))
                for t in range(3):
                    r = tile_rows(t)
                    wait(pool, "route_done", 3 * l + t + 1)
                    for j in range(TOPK):
                        pool.indirect_dma_start(
                            out=places_d, out_offset=bass.IndirectOffsetOnAxis(ap=place_i[0:r, t, j:j + 1], axis=0),
                            in_=pair_id[0:r, t, j:j + 1], in_offset=None).then_inc(sem("places_stored"), 16)

            def gather(s, landed):
                pool.sem_inc(sem("pool_passed"), 1)
                pool.indirect_dma_start(
                    out=xg[:, s, :], out_offset=None, in_=u_d,
                    in_offset=bass.IndirectOffsetOnAxis(ap=xi[:, s:s + 1], axis=0),
                    bounds_check=2 * TOK - 1, oob_is_err=False).then_inc(landed, 16)

            def scatter(s, stored):
                pool.sem_inc(sem("pool_passed"), 1)
                pool.indirect_dma_start(
                    out=pair_d, out_offset=bass.IndirectOffsetOnAxis(ap=yi[:, s:s + 1], axis=0),
                    in_=y_sb[:, s, :], in_offset=None,
                    bounds_check=2 * TOK * TOPK - 1, oob_is_err=False).then_inc(stored, 16)

            def experts(l):
                base = l * NE
                wait(pool, "index_ready", l + 1)
                for t in range(3):
                    pool.wait_ge(sem(f"u_stored{t}"), 16 * (l + 1))

                def one(e, s, first=False, last=False):
                    if not last:
                        if not first:
                            pool.wait_ge(sem("xT_full"), e + base)
                        pool.wait_ge(sem("xi_ready"), e + (base + 3))
                        gather((s + 2) % 3, sem(f"xg_full{(s + 2) % 3}"))
                    if not first:
                        pool.wait_ge(sem("yi_ready"), e + base)
                        scatter((s + 2) % 3, sem(f"y_stored{(s + 2) % 3}"))

                pool.wait_ge(sem("xi_ready"), base + 2)
                for e in range(2):
                    gather(e, sem(f"xg_full{e}"))
                for e in range(3):
                    one(e, e, first=(e == 0))
                with pool.Fori(1, 20) as i:
                    for s in range(3):
                        one(i * 3 + s, s)
                for e in range(60, 64):
                    one(e, e % 3, last=(e >= 62))
                pool.wait_ge(sem("yi_ready"), base + NE)
                scatter(0, sem("y_stored0"))

            def overflow(l):
                done = sem(f"pool_over{l}")
                wait(pool, "over_ready", l + 1)
                for s in range(3):
                    pool.wait_ge(sem(f"y_stored{s}"), 16 * Y_STORED[l][s])

                def body(j):
                    col = pool.value_load(ov_idx[0:1, ds(j, 1)], min_val=0, max_val=BLOCKS * NE - 1)
                    pool.tensor_copy(xi[:, 0:1], xidx[:, ds(col, 1)]).then_inc(done, 1)
                    pool.tensor_copy(yi[:, 0:1], yidx[:, ds(col, 1)]).then_inc(done, 1)
                    pool.wait_ge(done, j * 2 + 2)
                    pool.sem_inc(sem("pool_passed"), 1)
                    pool.indirect_dma_start(
                        out=xg[:, 0, :], out_offset=None, in_=u_d,
                        in_offset=bass.IndirectOffsetOnAxis(ap=xi[:, 0:1], axis=0),
                        bounds_check=2 * TOK - 1, oob_is_err=False).then_inc(sem(f"over_xg{l}"), 16)
                    pool.wait_ge(sem(f"act_over{l}"), j * 2 + 2)
                    pool.sem_inc(sem("pool_passed"), 1)
                    pool.indirect_dma_start(
                        out=pair_d, out_offset=bass.IndirectOffsetOnAxis(ap=yi[:, 0:1], axis=0),
                        in_=y_sb[:, 0, :], in_offset=None,
                        bounds_check=2 * TOK * TOPK - 1, oob_is_err=False).then_inc(sem(f"over_stored{l}"), 16)
                    pool.wait_ge(sem(f"over_stored{l}"), j * 16 + 16)

                over_blocks(pool, body)
                pool.nop().then_inc(sem("pairs_stored"), 1)

            dispatch(0)
            experts(0)
            overflow(0)

            pool.wait_ge(sem("ln_done"), 3 * 2)
            run.run(pool.memset(selneg, -1.0))
            triangle(selneg, ALU.is_equal, 0, [[-1, FH], [0, P]], 1)
            run.do(pool.memset(qz[:, :, :, :], 0.0))
            run.do(pool.memset(fqc, 0.0))
            run.settle()
            pool.nop().then_inc(sem("fox_cleared"), 1)
            pool.wait_ge(sem("u_ready"), 3 * (stages.index("fox") + 1))
            for kb in key_bias:
                run.do(pool.memset(kb, 0.0))
            run.settle()
            pool.wait_ge(sem("bias_stored"), 16 * (1 + DB))
            pool.wait_ge(sem("v_stored"), 16 * 8)
            for n in (2, 3):
                pool.wait_ge(sem(f"kv_out{n}"), 32)
            for i in range(4):
                for s in range(2):
                    pool.dma_start(fqc[32 * i:32 * i + DT, s::2],
                                   dram(fq_d, 4 * s + i, [[FH, DT], [DT * FH, DB]]),
                                   allow_slow_non_contiguous=True).then_inc(sem("fqc_loaded"), 16)

            def fetch(b, s):
                for i in range(4):
                    row = bias_d[ds((s * 4 + i) * DB + b, 1), :]
                    pool.dma_start(key_bias[s][32 * i:32 * i + DT, :], row.to_broadcast([DT, CTX])).then_inc(sem(f"fetched{s}"), 16)
                pool.dma_start(vn[0:DT, s, :], O["v_sample"][ds(b, 1)].rearrange("o t h d -> (o t) (h d)")
                               [:, s * 512:(s + 1) * 512]).then_inc(sem(f"fetched{s}"), 16)

            def put(g, b, s):
                pool.wait_ge(sem("og_ready"), g)
                pool.dma_start(og_d[ds((b * 2 + s) * P, P), :], og[:, s, :]).then_inc(sem(f"og_stored{s}"), 16)

            for s in range(2):
                fetch(0, s)
            with pool.Fori(1, DB) as b:
                for s in range(2):
                    put(b * 2 + (s - 1), b - 1, s)
                    fetch(b, s)
            for s in range(2):
                put(2 * DB - 1 + s, DB - 1, s)
            dispatch(1)
            experts(1)
            overflow(1)

        SI = {s: n for n, s in enumerate(stages)}

        def u_ready(eng, stage, t):
            eng.wait_ge(sem("u_ready"), 3 * SI[stage] + t + 1)

        @block.scalar
        def _(act):
            run = Steps(act, sem("act_step"))
            small = sem("small_loaded")
            row = lambda ap, n: dram(ap, ap.offset, [[0, P], [1, n]])

            act.dma_start(ln[0:1, 0, :], W["c_prompt"]).then_inc(sem("c_loaded"), 16)
            act.dma_start(ln[1:9, 0, :], W["c_sample"]).then_inc(sem("c_loaded"), 16)
            act.dma_start(page_col[:, :], W["page_table"].rearrange("b (n o) -> (b n) o", o=1))\
               .then_inc(sem("page_col_loaded"), 16)
            for t in range(2):
                act.dma_start(x[:, t, :], W["x_prompt"][0, t * P:(t + 1) * P, :]).then_inc(sem("x_loaded"), 16)
            act.dma_start(x[0:64, 2, :], W["x_sample"].rearrange("b t d -> (b t) d")).then_inc(sem("x_loaded"), 16)
            act.dma_start(w_small[:, :, 0:RANK], W["gla_w_in"][0].rearrange("(p c) n -> p c n", c=KT)
                          [:, :, W_IN_N:W_IN_N + RANK]).then_inc(small, 16)
            act.dma_start(w_a2[:, :], W["gla_w_a2"][0]).then_inc(small, 16)

            def load_mod(n, dst, name, l, landed):
                c = MOD_CHUNK[(name, l)]
                mod_wait(act, c)
                mod_wait(act, c + 1)
                at = c // 2 * 32 * D
                act.dma_start(dst[:, 0, :], dram(mod_d, at, [[0, P], [1, D]])).then_inc(landed, 16)
                act.dma_start(dst[0:DB * DT, 1, :], dram(mod_d, at + D, [[D, DB], [0, DT], [1, D]]))\
                   .then_inc(landed, 16)

            def load_modulation(n, l, which):
                load_mod(n, mscale, f"scale_{which}", l, sem("mod_loaded"))
                load_mod(n, mshift, f"shift_{which}", l, sem("mod_loaded"))

            def load_gate(n):
                l, sub = divmod(n, 2)
                load_mod(n, mgate, "gate_" + "am"[sub], l, sem("gate_loaded"))
                load_norm(l, sub)

            def load_norm(l, sub):
                for i, w in enumerate((W["ln_g"], W["ln_b"])):
                    act.dma_start(ln[:, i, :], row(w[l, sub], D)).then_inc(sem("gate_loaded"), 16)

            def turned(stage):
                for t, (t0, r) in enumerate(TILES):
                    for half in range(2):
                        job = (stage, t, half)
                        turn.wait_full(act, job)
                        act.copy(uT[:, 4 * half:4 * half + 4, t0:t0 + r],
                                 psum[turn.bank(job)][:, :].rearrange("p (c n) -> p c n", c=4)[:, :, 0:r])\
                           .then_inc(turn.is_free(job), 1)

            def store_ada(n):
                wait(act, "ada_added", n + 1)
                act.dma_start(dram(mod_d, n // 2 * 32 * D + n % 2 * 512, [[P, 4], [D, 32], [1, P]]),
                              ada_out[:, n % 4, :]).then_inc(sem(f"ada_stored{n % 4}"), 16)

            def std_tile(n, t):
                r = tile_rows(t)
                act.wait_ge(sem("var_ready"), 3 * n + t + 1)
                act.activation(stat[0:r, 47:48], stat[0:r, 45:46], ACT.Sqrt, bias=eps[0:r, 0:1])\
                   .then_inc(sem("std_ready"), 1)

            def std(n):
                for t in range(3):
                    std_tile(n, t)

            act.wait_ge(sem("c_loaded"), 32)
            act.activation(ln[0:9, 1, :], ln[0:9, 0, :], ACT.Silu).then_inc(signal("c_silu"), 1)
            wait(act, "c_turned", 1)
            act.copy(cT[:, :, 0:9], psum[7][:, 0:KT * 16].rearrange("p (c n) -> p c n", c=KT)[:, :, 0:9])\
               .then_inc(signal("cT_ready"), 1)
            for n in range(4):
                store_ada(n)
            turn.wait_full(act, ("lf",))
            act.copy(lf_pages[:, 0, :].rearrange("p (j h b) -> p h b j", j=PAGES, h=FH),
                     psum[turn.bank(("lf",))][:, :].rearrange("p (h b j) -> p h b j", h=FH, b=DB))\
               .then_inc(turn.is_free(("lf",)), 1)
            load_modulation(0, 0, "a")
            for n in range(4, FIRST_ADA):
                store_ada(n)
            act.dma_start(b_a[:, :], row(W["gla_b_a"], GD)).then_inc(small, 16)
            act.dma_start(norm_g[:, :], row(W["gla_norm_g"], GV)).then_inc(small, 16)
            act.dma_start(b_f[:, :], row(W["fox_b_f"], FH)).then_inc(small, 16)
            act.dma_start(pages[:, :], W["page_table"].rearrange("(o b) n -> o (b n)", o=1)).then_inc(small, 16)
            for n in range(2):
                lin.wait_full(act, ("suf", n))
                act.copy(mgate[0:64, 1, n * 512:(n + 1) * 512], psum[lin.bank(("suf", n))][0:64, :])\
                   .then_inc(lin.is_free(("suf", n)), 1)
            lin.wait_drained(act, ("suf", 1))
            act.dma_start(bias_d[:, 0:PAST], mgate[0:64, 1, :]).then_inc(sem("bias_stored"), 16)
            turned("gla")
            n = FIRST_ADA
            for j in range(W_IN_N // 512):
                for t in range(3):
                    r = tile_rows(t)
                    job = ("w_in", j, t)
                    lin.wait_full(act, job)
                    src = psum[lin.bank(job)][0:r, :]
                    if j == 0:
                        ins = act.activation(q[0:r, t, :], src, ACT.Copy, scale=GK ** -0.5)
                    elif j == 1:
                        ins = act.copy(k[0:r, t, :], src)
                    elif j < 4:
                        ins = act.copy(v[0:r, t, (j - 2) * 512:(j - 1) * 512], src)
                    else:
                        ins = act.activation(gs[0:r, t, (j - 4) * 512:(j - 3) * 512], src, ACT.Silu)
                    ins.then_inc(lin.is_free(job), 1)
                if j == 0:
                    wait(act, "alr_full", 1)
                    act.copy(alrT[:, :], psum[7][0:RANK, 0:TOK]).then_inc(signal("alrT_ready"), 1)
                    act.dma_start(w_small[:, :, :], W["router_w"][0].rearrange("(p c) n -> p c n", c=KT))\
                       .then_inc(sem("router_loaded"), 16)
                    act.dma_start(r_bias[:, :], row(W["router_bias"][0], NE)).then_inc(sem("router_loaded"), 16)
                for _ in range(ADA_AFTER[j]):
                    store_ada(n)
                    n += 1
                if 1 <= j <= 3:
                    r = tile_rows(j - 1)
                    wait(act, "z_neg_ready", j)
                    run.run(act.activation(z_neg[0:r, :], z_neg[0:r, :], ACT.Exp))
                    act.activation(z_neg[0:r, :], z_neg[0:r, :], ACT.Ln, bias=ones[0:r, 0:1])\
                       .then_inc(signal("z_log_ready"), 1)

            def load_state(b):
                if b >= 2:
                    wait(act, "sup_ready", b - 1)
                act.dma_start(s_in[:, b % 2, :].rearrange("p (h e) -> p h e", h=GH),
                              W["state_gla"][0, b].rearrange("h d e -> d h e")).then_inc(sem(f"state_loaded{b % 2}"), 16)

            for b in range(2):
                load_state(b)
            for t in range(3):
                r = tile_rows(t)
                groups = state_of(t)[3]
                wait(act, "dec_full", t + 1)
                run.do(act.copy(cum_sb[0:r, :], psum[0][0:r, :]))
                run.do(act.activation(e_cum[0:r, :], psum[0][0:r, :], ACT.Exp))
                run.do(act.activation(kd[0:r, :], psum[0][0:r, :], ACT.Exp, scale=-1.0))
                act.activation(egT[:, :, 0:groups], psum[2][:, 0:GH * groups].rearrange("p (h g) -> p h g", h=GH),
                               ACT.Exp).then_inc(signal("e_ready"), 1)
                run.settle()
                wait(act, "end_gap_ready", t + 1)
                act.activation(e_end[0:r, :], e_end[0:r, :], ACT.Exp).then_inc(signal("e_end_ready"), 1)
                wait(act, "qdT_full", t + 1)
                bank3 = psum[3][:, :].rearrange("p (h n) -> p h n", h=GH)
                run.do(act.copy(qdT[:, :, 0:r], bank3[:, :, 0:r]))
                if t < ST:
                    diag = qz64.rearrange("p h (g s) -> p h g s", s=192)[:, :, :, 0:64]
                    src = bank3.rearrange("p h (g j) -> p h g j", g=2)
                else:
                    act.wait_ge(sem("qz_cleared"), 1)
                    diag = qz8.rearrange("p h (g s) -> p h g s", s=72)[:, :, :, 0:8]
                    src = bank3[:, :, 0:64].rearrange("p h (g j) -> p h g j", g=8)
                run.settle()
                act.copy(diag, src).then_inc(signal("qdT_ready"), 1)
                if t == ST:
                    for b in range(DB):
                        if b + 2 < DB:
                            load_state(b + 2)
                        wait(act, "sup_ready", b + 1)
                        act.dma_start(O["gla_sample"][0, b].rearrange("h d e -> d h e"),
                                      s_out[:, b % 2, :].rearrange("p (h e) -> p h e", h=GH))\
                           .then_inc(sem(f"state_stored{b % 2}"), 16)
                if t == 1:
                    wait(act, "prompt_state_ready", 4)
                    act.dma_start(O["gla_prompt"][0, 0].rearrange("h d e -> d h e"),
                                  s_p.rearrange("p (h e) -> p h e", h=GH)).then_inc(sem("gla_stored"), 16)
                wait(act, "o_full", t + 1)
                for h in range(GH):
                    ins = act.activation(e_cum[0:r, 0:GV], psum[6 + h // 2][0:r, (h % 2) * GV:(h % 2 + 1) * GV],
                                         ACT.Square, accum_out=stat[0:r, h:h + 1])
                    run.run(ins)
                act.activation(stat[0:r, 48:52], stat[0:r, 0:4], ACT.Sqrt, scale=1.0 / GV, bias=eps[0:r, 1:2])\
                   .then_inc(signal("rms_ready"), 1)
            for b in range(2):
                act.wait_ge(sem(f"state_stored{b}"), 64)
            act.wait_ge(sem("gla_stored"), 16)
            u_ready(act, "gla_o", 2)
            turned("gla_o")
            load_gate(0)
            load_modulation(1, 0, "m")
            std(0)

            def moe_front(l):
                stage = f"moe{l}"
                for t in range(3):
                    t0, r = TILES[t]
                    u_ready(act, stage, t)
                    act.dma_start(u_d[2 * t0:2 * (t0 + r), :].rearrange("(p a) n -> p a n", a=2),
                                  u[0:r, t, :].rearrange("p (a n) -> p a n", a=2)).then_inc(sem(f"u_stored{t}"), 16)
                turned(stage)
                for t in range(3):
                    r = tile_rows(t)
                    wait(act, "router_full", 3 * l + t + 1)
                    if 3 * l + t:
                        wait(act, "chosen", 3 * l + t)
                    act.activation(route[0:r, 0, :], psum[5 + t][0:r, 0:NE], ACT.Sigmoid).then_inc(signal("sigmoid_ready"), 1)
                for t in range(3):
                    r = tile_rows(t)
                    lin.wait_full(act, ("sh_gu", l, t))
                    if t:
                        turn.wait_full(act, ("h_sh", l, t - 1))
                    act.activation(h_sh[0:r, :], psum[lin.bank(("sh_gu", l, t))][0:r, 0:FE], ACT.Silu)\
                       .then_inc(signal("sh_silu_ready"), 1)
                    if t:
                        shared_down(l, t - 1)
                    turn.wait_full(act, ("h_sh", l, t))
                    act.copy(hT_sh[:, :, 0:r], psum[turn.bank(("h_sh", l, t))][:, 0:2 * P]
                             .rearrange("p (f n) -> p f n", f=2)[:, :, 0:r]).then_inc(turn.is_free(("h_sh", l, t)), 1)
                act.wait_ge(sem("places_stored"), 16 * 3 * TOPK * (l + 1))
                act.dma_start(tab_i, places_d.rearrange("(e r) o -> e (r o)", e=NE)).then_inc(sem("places_loaded"), 16)
                shared_down(l, 2)

            def shared_down(l, t):
                r = tile_rows(t)
                for j in range(2):
                    job = ("sh_d", l, j, t)
                    lin.wait_full(act, job)
                    act.copy(ysh[0:r, t, j * 512:(j + 1) * 512], psum[lin.bank(job)][0:r, :]).then_inc(lin.is_free(job), 1)

            def experts(l):
                base = l * NE

                def y_out(e, s, n_stored):
                    act.wait_ge(y_full, e + (base + 1))
                    if n_stored is not None:
                        act.wait_ge(sem(f"y_stored{s}"), n_stored)
                    act.copy(y_sb[:, s, :], psum[3 + s][:, :]).then_inc(sem("y_ready"), 1)

                def one(e, s, i, first=False):
                    act.wait_ge(h_full, e + (base + 1))
                    act.activation(sil[:, s, :], psum[s][:, 0:P], ACT.Silu).then_inc(sem("sil_ready"), 1)
                    if not first:
                        y_out(e - 1, (s + 2) % 3, stored_before(e - 1, (s + 2) % 3, i))

                before_l = [Y_STORED[l - 1][s] if l else 0 for s in range(3)]

                def stored_before(e, s, i):
                    n = (i if s < 2 else i - 1) if not isinstance(e, int) else e // 3
                    n = n + before_l[s]
                    return None if isinstance(n, int) and n == 0 else n * 16

                for e in range(3):
                    one(e, e, 0, first=(e == 0))
                with act.Fori(1, 20) as i:
                    for s in range(3):
                        one(i * 3 + s, s, i)
                for e in range(60, 64):
                    one(e, e % 3, 0)
                y_out(NE - 1, 0, stored_before(NE - 1, 0, 0))

            def load_over_weights(l, j):
                col = act.value_load(ov_idx[0:1, ds(j, 1)], min_val=0, max_val=1023)
                with act.If(col < 512):
                    e = act.value_load(ov_e[0:1, ds(j, 1)], min_val=0, max_val=NE - 1)
                    for name, dst in (("exp_w_gate", ov_gate), ("exp_w_up", ov_up)):
                        act.dma_start(dst[:, :, :], W[name][l, ds(e, 1)].rearrange(
                            "o (h p j) n -> p (o h) (j n)", h=2, j=4)).then_inc(sem(f"over_w{l}"), 16)
                    act.dma_start(ov_down, W["exp_w_down"][l, ds(e, 1)].rearrange(
                        "o (f p) n -> p (o f) n", f=2)).then_inc(sem(f"over_w{l}"), 16)
                with act.Else():
                    act.nop()

            def before_overflow(l):
                wait(act, "index_ready", l + 1)
                for t in range(3):
                    act.wait_ge(sem(f"u_stored{t}"), 16 * (l + 1))
                load_over_weights(l, 0)

            def overflow(l):
                done = sem(f"act_over{l}")

                def body(j):
                    act.wait_ge(sem(f"over_pe{l}"), j * 4 + 2)
                    act.activation(sil[:, 0, :], psum[0][:, 0:P], ACT.Silu).then_inc(done, 1)
                    act.wait_ge(sem(f"over_pe{l}"), j * 4 + 4)
                    act.copy(y_sb[:, 0, :], psum[3][:, :]).then_inc(done, 1)
                    load_over_weights(l, j + 1)
                    act.wait_ge(sem(f"over_stored{l}"), j * 16 + 16)
                    act.sem_inc(sem("act_passed"), 1)

                over_blocks(act, body)

            def load_pairs(l):
                act.wait_ge(sem("pairs_stored"), l + 1)
                for n in range(6):
                    t, half = divmod(n, 2)
                    t0, r = TILES[t]
                    if n == 2 and l == 0:
                        load_modulation(2, 1, "kv")
                    if t and half == 0:
                        act.wait_ge(sem("pairs_used"), 3 * l + t)
                    elif t:
                        lin.wait_full(act, ("comb", l, t - 1))
                    act.dma_start(y_pairs[0:r, half, :, :],
                                  dram(pair_d, t0 * TOPK * D + half * 512, [[TOPK * D, r], [D, TOPK], [1, 512]]))\
                       .then_inc(sem(f"pairs_loaded{half}"), 16)
                    if t and half:
                        std_tile(2 * l + 1, t - 1)
                std_tile(2 * l + 1, 2)

            moe_front(0)
            act.wait_ge(sem("ln_done"), 3)
            load_gate(1)
            before_overflow(0)
            experts(0)
            overflow(0)
            load_pairs(0)
            act.dma_start(w_small[:, :, 0:FH], W["kv_w"].rearrange("(p c) n -> p c n", c=KT)[:, :, 2 * D:2 * D + FH])\
               .then_inc(sem("router_loaded"), 16)
            u_ready(act, "kv", 2)
            load_modulation(3, 1, "a")
            turned("kv")
            for (j, t), slot in KV_SLOTS:
                if (j, t) == (3, 0):
                    wait(act, "lf_neg_ready", 1)
                    run.run(act.activation(lf_t[:, :, :], lf_t[:, :, :], ACT.Exp))
                    act.activation(lf_t[:, :, :], lf_t[:, :, :], ACT.Ln, bias=ones[:, 0:1])\
                       .then_inc(signal("lf_log_ready"), 1)
                t0, r = TILES[t]
                job = ("kv", j, t)
                lin.wait_full(act, job)
                if slot is None:
                    dst = vp[0:r, t, (j - 2) * 512:(j - 1) * 512]
                else:
                    if slot >= 4:
                        n_before = (slot - 4) // 4 + 1
                        act.wait_ge(sem(f"kv_out{slot % 4}"), 16 * n_before)
                        if slot - 4 < 6:
                            turn.wait_full(act, ("kT",) + KV_SLOTS[slot - 4][0])
                    dst = kv_rows[0:r, slot % 4, :]
                act.copy(dst, psum[lin.bank(job)][0:r, :]).then_inc(lin.is_free(job), 1)
                lin.wait_freed(act, job)
                out = O[("k" if j < 2 else "v") + ("_prompt" if t < ST else "_sample")]\
                    .rearrange("b t h d -> (b t) (h d)")
                at = t0 if t < ST else 0
                done = sem("v_stored") if slot is None else sem(f"kv_out{slot % 4}")
                act.dma_start(out[at:at + r, (j % 2) * 512:(j % 2 + 1) * 512], dst).then_inc(done, 16)
            turned("fox")
            wait(act, "lf_ready", 1)
            for t in range(2):
                act.dma_start(O["logf_prompt"][0, t * P:(t + 1) * P, :], lf[:, t, :]).then_inc(sem("v_stored"), 16)
            act.dma_start(O["logf_sample"].rearrange("b t h -> (b t) h"), lf[0:64, 2, :]).then_inc(sem("v_stored"), 16)
            wait(act, "f_ready", 1)
            act.dma_start(fq_d, f_s[0:64, :]).then_inc(sem("v_stored"), 16)
            for b in range(DB):
                act.dma_start(dram(bias_d, b * CTX + PAST, [[1, DT], [DB * CTX, FH]]), nf_s[b * DT:(b + 1) * DT, :],
                              allow_slow_non_contiguous=True)\
                   .then_inc(sem("bias_stored"), 16)
            for h in range(FH):
                lin.wait_full(act, ("w_q", h))
                act.activation(qT[:, h, :], psum[lin.bank(("w_q", h))][:, 0:TOK], ACT.Copy, scale=HD ** -0.5)\
                   .then_inc(lin.is_free(("w_q", h)), 1)
            for n in range(2 * FH + 2):
                if n < 2 * FH:
                    nk = P * (n % 2 + 1)
                    wait(act, "p_max_ready", n + 1)
                    act.activation(p_sc[:, n % 4, 0:nk], p_sc[:, n % 4, 0:nk], ACT.Exp,
                                   bias=stat[:, 52 + n % 4:53 + n % 4],
                                   accum_out=stat[:, 56 + n % 4:57 + n % 4]).then_inc(signal("p_exp_ready"), 1)
                if n >= 2:
                    m = n - 2
                    wait(act, "p_turned", m + 1)
                    if m >= 4:
                        wait(act, "po_full", m - 3)
                    act.copy(p_T[:, m % 4, 0:m % 2 + 1, :], psum[5 + m % 2][:, 0:P * (m % 2 + 1)]
                             .rearrange("p (a n) -> p a n", n=P)).then_inc(signal("p_T_ready"), 1)
            wait(act, "po_full", 2 * FH)
            load_mod(2, mgate, "gate_a", 1, sem("gate_loaded"))
            act.dma_start(w_small[:, :, :], W["router_w"][1].rearrange("(p c) n -> p c n", c=KT))\
               .then_inc(sem("router_loaded"), 16)
            act.dma_start(r_bias[:, :], row(W["router_bias"][1], NE)).then_inc(sem("router_loaded"), 16)

            def keys_turned(g, i):
                act.wait_ge(kt_full, g * 8 + (2 * i + 1))
                if i >= 2:
                    act.wait_ge(sem("s_full"), g * 4 + (i - 1))
                act.copy(kt_sb[:, i % 2, 0:512], psum[0][:, :]).then_inc(sem("kt_act"), 1)

            def probs_turned(g):
                act.wait_ge(sem("pt_full"), g * 3 + 1)
                act.copy(pT[:, 0:4, :].rearrange("p a b -> p (a b)"), psum[5][:, :]).then_inc(sem("pt_act"), 1)

            def fox_group(g, s, first=False, last=False):
                keys_turned(g, 2)
                if not first:
                    probs_turned(g - 1)
                keys_turned(g, 3)
                if not last:
                    keys_turned(g + 1, 0)
                    keys_turned(g + 1, 1)
                act.wait_ge(sem("max_ready"), g + 1)
                act.activation(sc, sc, ACT.Exp, bias=stat[:, 16:17], accum_out=stat[:, 18 + s:19 + s])\
                   .then_inc(sem("exp_ready"), 1)

            keys_turned(0, 0)
            keys_turned(0, 1)
            for s in range(2):
                fox_group(s, s, first=(s == 0))
            with act.Fori(1, DB - 1) as b:
                for s in range(2):
                    fox_group(b * 2 + s, s)
            for s in range(2):
                fox_group(2 * DB - 2 + s, s, last=(s == 1))
            probs_turned(2 * DB - 1)
            for s in range(2):
                act.wait_ge(sem(f"og_stored{s}"), 16 * DB)
            wait(act, "o_prompt_done", 2 * FH)
            for b in range(DB):
                act.dma_start(u[b * DT:(b + 1) * DT, ST, :].rearrange("p (k n) -> p k n", n=HD),
                              dram(og_d, b * 2 * P * HD, [[HD, DT], [32 * HD, FH], [1, HD]])).then_inc(sem("og_loaded"), 16)
            load_norm(1, 0)
            turned("fox_o")
            load_modulation(4, 1, "m")
            std(2)
            moe_front(1)
            act.wait_ge(sem("ln_done"), 9)
            load_gate(3)
            before_overflow(1)
            experts(1)
            overflow(1)
            load_pairs(1)
            for t in range(2):
                act.wait_ge(sem("ln_done"), 9 + t + 1)
                act.dma_start(O["y_prompt"][0, t * P:(t + 1) * P, :], x[:, t, :]).then_inc(sem("y_out"), 16)
            act.wait_ge(sem("ln_done"), 12)
            act.dma_start(O["y_sample"].rearrange("b t d -> (b t) d"), x[0:64, 2, :]).then_inc(sem("y_out"), 16)
            act.wait_ge(sem("y_out"), 48)
            act.wait_ge(sem("v_stored"), 16 * (4 + 3 + 1))
            for n in range(4):
                act.wait_ge(sem(f"kv_out{n}"), 32)

        @block.vector
        def _(dve):
            run = Steps(dve, sem("dve_step"))
            stt, tt, ts = dve.scalar_tensor_tensor, dve.tensor_tensor, dve.tensor_scalar

            def side(m, t):
                return m[0:tile_rows(t), 0 if t < ST else 1, :]

            def add_ada(n):
                adas.wait_full(dve, n)
                dve.wait_ge(sem(f"ada_bias{n % 4}"), 16 * (n // 4 + 1))
                if n >= 4:
                    mod_wait(dve, n - 4)
                tt(ada_out[:, n % 4, :], psum[adas.bank(n)][:, 0:P], ada_bias[:, n % 4, :], ALU.add)\
                    .then_inc(adas.is_free(n), 1)
                adas.wait_freed(dve, n)
                dve.nop().then_inc(signal("ada_added"), 1)

            def modulate_tile(n, t):
                r = tile_rows(t)
                dve.wait_ge(sem("mod_loaded"), 16 * 4 * (n + 1))
                run.run(stt(u[0:r, t, :], side(mscale, t), 1.0, x[0:r, t, :], ALU.add, ALU.mult))
                tt(u[0:r, t, :], u[0:r, t, :], side(mshift, t), ALU.add).then_inc(sem("u_ready"), 1)

            def modulate(n):
                for t in range(3):
                    modulate_tile(n, t)

            def norm_tile(n, t):
                r = tile_rows(t)
                xt = x[0:r, t, :]
                st, mv, rstd = stat[0:r, 32:44], stat[0:r, 44:46], stat[0:r, 46:47]
                for h in range(2):
                    run.do(dve.bn_stats(st[:, 6 * h:6 * h + 6], xt[:, h * 512:(h + 1) * 512]))
                run.settle()
                dve.bn_aggr(mv, st).then_inc(sem("var_ready"), 1)
                dve.wait_ge(sem("var_ready"), 3 * n + t + 1)
                run.do(stt(xt, xt, mv[:, 0:1], ln[0:r, 0, :], ALU.subtract, ALU.mult))
                dve.wait_ge(sem("std_ready"), 3 * n + t + 1)
                run.run(dve.reciprocal(rstd, stat[0:r, 47:48]))
                stt(xt, xt, rstd, ln[0:r, 1, :], ALU.mult, ALU.add).then_inc(sem("ln_done"), 1)

            def residual(n, name, mod):
                dve.wait_ge(sem("gate_loaded"), 16 * 4 * (n + 1))
                for t in range(3):
                    r = tile_rows(t)
                    for j in range(2):
                        cols = slice(j * 512, (j + 1) * 512)
                        job = (name, j, t)
                        lin.wait_full(dve, job)
                        stt(u[0:r, t, cols], side(mgate, t)[:, cols], 1.0, psum[lin.bank(job)][0:r, :],
                            ALU.add, ALU.mult).then_inc(lin.is_free(job), 1)
                    lin.wait_drained(dve, (name, 1, t))
                    run.run(stt(x[0:r, t, :], x[0:r, t, :], ALPHA, u[0:r, t, :], ALU.mult, ALU.add))
                    norm_tile(n, t)
                    dve.wait_ge(sem("ln_done"), 3 * n + t + 1)
                    modulate_tile(mod, t)

            dve.wait_ge(sem("consts_ready"), 1)
            for n in range(FIRST_ADA):
                add_ada(n)
            dve.wait_ge(sem("x_loaded"), 48)
            modulate(0)
            def log_decay(t):
                r = tile_rows(t)
                wait(dve, "z_full", t + 1)
                z = la[0:r, t, :]
                run.run(tt(z, psum[7][0:r, :], b_a[0:r, :], ALU.add))
                stt(z_neg[0:r, :], z, -1.0, z, ALU.mult, ALU.min).then_inc(signal("z_neg_ready"), 1)
                wait(dve, "z_log_ready", t + 1)
                run.run(stt(z, z, 0.0, z_neg[0:r, :], ALU.min, ALU.subtract))
                ts(z, z, 1.0 / TAU, None, ALU.mult).then_inc(signal("la_ready"), 1)

            dve.wait_ge(sem("small_loaded"), 16 * SMALL_LOADS)
            dve.wait_ge(sem("consts_ready"), 2)
            dve.wait_ge(sem("bias_stored"), 16)
            n = FIRST_ADA
            for j in range(W_IN_N // 512):
                for _ in range(ADA_AFTER[j]):
                    add_ada(n)
                    n += 1
                if 1 <= j <= 3:
                    log_decay(j - 1)

            wait(dve, "la_ready", 3)
            for t in range(3):
                r = tile_rows(t)
                mask, _, _, groups = state_of(t)
                wait(dve, "e_ready", t + 1)
                tt(e_end[0:r, :], psum[1][0:r, :], cum_sb[0:r, :], ALU.subtract).then_inc(signal("end_gap_ready"), 1)
                tt(q[0:r, t, :], q[0:r, t, :], e_cum[0:r, :], ALU.mult).then_inc(signal("qd_ready"), 1)
                tt(kd[0:r, :], k[0:r, t, :], kd[0:r, :], ALU.mult).then_inc(signal("kd_ready"), 1)
                wait(dve, "e_end_ready", t + 1)
                wait(dve, "kd_ready", t + 1)
                tt(k[0:r, t, :], k[0:r, t, :], e_end[0:r, :], ALU.mult).then_inc(signal("ke_ready"), 1)
                wait(dve, "kdT_full", t + 1)
                dve.tensor_copy(kdT[:, :, 0:r], psum[4][:, :].rearrange("p (h n) -> p h n", h=GH)[:, :, 0:r])\
                   .then_inc(signal("kdT_ready"), 1)
                wait(dve, "att_full", t + 1)
                tt(att[0:r, :, 0:r], psum[5][0:r, :].rearrange("p (h n) -> p h n", h=GH)[:, :, 0:r],
                   mask[0:r, 0:r].unsqueeze(1).to_broadcast([r, GH, r]), ALU.mult).then_inc(signal("att_ready"), 1)

                def state_step(new, old, g, bank=0):
                    for h in range(GH):
                        part = slice(h * GV, (h + 1) * GV)
                        upd = psum[bank + h // 2][:, (h % 2) * GV:(h % 2 + 1) * GV]
                        if old is None:
                            run.do(dve.tensor_copy(new[:, part], upd))
                        else:
                            run.do(stt(new[:, part], old[:, part], egT[:, h, g:g + 1], upd, ALU.mult, ALU.add))
                    run.settle()

                if t < ST:
                    for g in range(2):
                        c = 2 * t + g
                        wait(dve, "upd_full", c + 1)
                        state_step(s_p, s_p if c else None, g)
                        dve.nop().then_inc(signal("prompt_state_ready"), 1)
                else:
                    def own_keys(b):
                        if b >= 2:
                            wait(dve, "upd_full", 3 + b)
                        ts(kem[b % 2][0:r, :], k[0:r, t, :], group8[:, b:b + 1], None, ALU.mult)\
                            .then_inc(signal("kem_ready"), 1)

                    own_keys(0)
                    for b in range(DB):
                        if b + 1 < DB:
                            own_keys(b + 1)
                        wait(dve, "upd_full", 5 + b)
                        dve.wait_ge(sem(f"state_loaded{b % 2}"), 16 * (b // 2 + 1))
                        if b >= 2:
                            dve.wait_ge(sem(f"state_stored{b % 2}"), 16 * (b // 2))
                        state_step(s_out[:, b % 2, :], s_in[:, b % 2, :], b, bank=3 * (b % 2))
                        dve.nop().then_inc(signal("sup_ready"), 1)
                wait(dve, "rms_ready", t + 1)
                run.run(dve.reciprocal(stat[0:r, 4:8], stat[0:r, 48:52]))
                for h in range(GH):
                    run.do(stt(u[0:r, t, h * GV:(h + 1) * GV], psum[6 + h // 2][0:r, (h % 2) * GV:(h % 2 + 1) * GV],
                               stat[0:r, 4 + h:5 + h], norm_g[0:r, :], ALU.mult, ALU.mult))
                run.settle()
                tt(u[0:r, t, :], u[0:r, t, :], gs[0:r, t, :], ALU.mult).then_inc(sem("u_ready"), 1)
            residual(0, "gla_wo", 1)

            def choose(l, t):
                r = tile_rows(t)
                R = route[0:r, :, :]
                s, sb_, rep, msk = R[:, 0, :], R[:, 1, :], R[:, 2, :], R[:, 3, :]
                grp = lambda a: a.rearrange("p (g e) -> p g e", g=NG)
                top, two, eqs = R[:, 4, :], R[:, 5, 0:NG], R[:, 6, :]
                rank8, best = R[:, 5, NG:2 * NG], R[:, 5, 16:24]
                wait(dve, "sigmoid_ready", 3 * l + t + 1)
                run.run(tt(sb_, s, r_bias[0:r, :], ALU.add))
                for g in range(NG):
                    run.do(dve.max(out=top[:, g * 8:g * 8 + 8], in_=sb_[:, g * 8:g * 8 + 8]))
                run.settle()
                run.run(tt(two, grp(top)[:, :, 0], grp(top)[:, :, 1], ALU.add))
                mine = two.unsqueeze(2).to_broadcast([r, NG, NG])
                other = two.unsqueeze(1).to_broadcast([r, NG, NG])
                run.do(tt(grp(rep), other, mine, ALU.is_gt))
                run.do(tt(grp(eqs), other, mine, ALU.is_equal))
                run.settle()
                run.run(tt(grp(eqs), grp(eqs), tri8[0:r, :, :], ALU.mult))
                run.run(tt(rep, rep, eqs, ALU.add))
                run.run(dve.tensor_reduce(rank8, grp(rep), AX, ALU.add))
                run.run(ts(rank8, rank8, float(TOPG) - 0.5, NEG, ALU.is_gt, ALU.mult))
                run.run(tt(grp(msk), grp(sb_), rank8.unsqueeze(2).to_broadcast([r, NG, 8]), ALU.add))
                run.run(dve.max(out=best, in_=msk))
                run.run(dve.match_replace(out=rep, in_to_replace=best, in_values=msk, imm_value=4 * NEG))
                run.run(tt(sel[0:r, t, :], rep, msk, ALU.not_equal))
                w = wgt[0:r, t, :]
                run.run(tt(w, s, sel[0:r, t, :], ALU.mult))
                run.run(dve.tensor_reduce(R[:, 5, 24:25], w, AX, ALU.add))
                run.run(dve.reciprocal(R[:, 5, 25:26], R[:, 5, 24:25]))
                ts(w, w, R[:, 5, 25:26], ROUTED, ALU.mult, ALU.mult).then_inc(signal("chosen"), 1)

            def place(l, t):
                r = tile_rows(t)
                wait(dve, "rank_full", 3 * l + t + 1)
                pl = route[0:r, 7, :]
                run.run(tt(pl, psum[5 + t][0:r, 0:NE], place0[0:r, :], ALU.add))
                run.run(tt(pl, pl, sel[0:r, t, :], ALU.mult))
                run.run(dve.max(out=place8[0:r, t, :], in_=pl))
                e3 = eq3[0:r, :, :]
                run.run(tt(e3, pl.unsqueeze(1).to_broadcast([r, TOPK, NE]),
                           place8[0:r, t, :].unsqueeze(2).to_broadcast([r, TOPK, NE]), ALU.is_equal))
                run.run(tt(e3, e3, wgt[0:r, t, :].unsqueeze(1).to_broadcast([r, TOPK, NE]), ALU.mult))
                run.run(dve.tensor_reduce(w8[0:r, t, :], e3, AX, ALU.add))
                ts(place_i[0:r, t, :], place8[0:r, t, :], 1.0, None, ALU.subtract).then_inc(signal("route_done"), 1)

            def moe_front(l):
                dve.wait_ge(sem("router_loaded"), 16 * (2 + 3 * l))
                choose(l, 0)
                choose(l, 1)
                place(l, 0)
                choose(l, 2)
                place(l, 1)
                place(l, 2)
                for t in range(3):
                    r = tile_rows(t)
                    wait(dve, "sh_silu_ready", 3 * l + t + 1)
                    tt(h_sh[0:r, :], h_sh[0:r, :], psum[lin.bank(("sh_gu", l, t))][0:r, FE:2 * FE], ALU.mult)\
                        .then_inc(lin.is_free(("sh_gu", l, t)), 1)
                for b in range(1, BLOCKS):
                    run.do(ts(ov_row[:, (b - 1) * NE:b * NE], psum[7][0:1, NE:2 * NE], float(CAP * b), None, ALU.is_gt))
                run.settle()
                run.run(tt(ov_row, ov_row, ov_code[:, :], ALU.mult))
                for n in range(OVER_LIST // 8):
                    run.run(dve.max(out=ov_top[0:1, 8 * n:8 * n + 8], in_=ov_row))
                    run.run(dve.match_replace(out=ov_row, in_to_replace=ov_top[0:1, 8 * n:8 * n + 8],
                                              in_values=ov_row, imm_value=0.0))
                run.run(ts(ov_idx[0:1, :], ov_top[0:1, :], -1.0, 1000.0, ALU.mult, ALU.add))
                ts(ov_e[0:1, :], ov_idx[0:1, :], NE - 1, None, ALU.bitwise_and).then_inc(signal("over_ready"), 1)
                run.run(dve.memset(xg[:, :, :], 0.0))
                dve.wait_ge(sem("places_loaded"), 16 * (l + 1))
                for h in range(2):
                    run.do(dve.tensor_copy(tab2[:, :, h, :], tab_i.rearrange("e (b r) -> e b r", b=BLOCKS)))
                run.settle()
                dve.nop().then_inc(signal("tab2_ready"), 1)
                job = ("places", l)
                turn.wait_full(dve, job)
                run.run(dve.tensor_copy(yidx, psum[turn.bank(job)][:, 0:BLOCKS * NE]))
                run.run(ts(xidx, yidx, 3, None, ALU.arith_shift_right))
                run.do(ts(xidx, xidx, 2.0, half_id[:, 0:1], ALU.mult, ALU.add))
                ts(yidx, yidx, 2.0, half_id[:, 0:1], ALU.mult, ALU.add).then_inc(turn.is_free(job), 1)
                run.settle()
                turn.wait_freed(dve, job)
                dve.nop().then_inc(signal("index_ready"), 1)

            def experts(l):
                base = l * NE

                def rows_turned(e, s):
                    dve.wait_ge(sem("xT_full"), e + (base + 1))
                    dve.tensor_copy(xT[:, s, :], psum[3 + s][:, :]).then_inc(sem("xT_ready"), 1)

                def rows_wanted(e, s):
                    dve.tensor_copy(xi[:, s:s + 1], xidx[:, ds(e, 1)]).then_inc(sem("xi_ready"), 1)

                def rows_returned(e, s):
                    dve.wait_ge(sem("y_ready"), e + (base + 1))
                    dve.tensor_copy(yi[:, s:s + 1], yidx[:, ds(e, 1)]).then_inc(sem("yi_ready"), 1)

                def one(e, s, first=False, fetch=True, turn_next=True):
                    dve.wait_ge(sem("sil_ready"), e + (base + 1))
                    if fetch:
                        rows_wanted(e + 2, (s + 2) % 3)
                    tt(hs[:, s, :], sil[:, s, :], psum[s][:, P:2 * P], ALU.mult).then_inc(sem("h_ready"), 1)
                    if turn_next:
                        rows_turned(e + 1, (s + 1) % 3)
                    dve.wait_ge(sem("hT_full"), e + (base + 1))
                    dve.tensor_copy(hT[:, s, :], psum[s][:, 2 * P:3 * P]).then_inc(sem("hT_ready"), 1)
                    if not first:
                        rows_returned(e - 1, (s + 2) % 3)

                for e in range(2):
                    rows_wanted(e, e)
                for t in range(3):
                    r = tile_rows(t)
                    run.do(tt(diag[t], ident[0:r, 0:r].unsqueeze(1).to_broadcast([r, TOPK, r]),
                              w8[0:r, t, :].unsqueeze(2).to_broadcast([r, TOPK, r]), ALU.mult))
                run.settle()
                dve.nop().then_inc(signal("diag_ready"), 1)
                rows_turned(0, 0)
                for e in range(3):
                    one(e, e, first=(e == 0))
                with dve.Fori(1, 20) as i:
                    for s in range(3):
                        one(i * 3 + s, s)
                for e in range(60, 64):
                    one(e, e % 3, fetch=(e < 62), turn_next=(e < 63))
                rows_returned(NE - 1, 0)

            def overflow(l):
                wait(dve, "over_ready", l + 1)
                done = sem(f"over_dve{l}")

                def body(j):
                    dve.wait_ge(sem(f"over_pe{l}"), j * 4 + 1)
                    dve.tensor_copy(xT[:, 0, :], psum[3][:, :]).then_inc(done, 1)
                    dve.wait_ge(sem(f"act_over{l}"), j * 2 + 1)
                    tt(hs[:, 0, :], sil[:, 0, :], psum[0][:, P:2 * P], ALU.mult).then_inc(done, 1)
                    dve.wait_ge(sem(f"over_pe{l}"), j * 4 + 3)
                    dve.tensor_copy(hT[:, 0, :], psum[0][:, 2 * P:3 * P]).then_inc(done, 1)

                over_blocks(dve, body)

            def combine(l, mod=None):
                dve.wait_ge(sem("gate_loaded"), 16 * 4 * (2 * l + 2))
                for t in range(3):
                    r = tile_rows(t)
                    dve.wait_ge(sem("pairs_loaded0"), 16 * (3 * l + t + 1))
                    y = ysh[0:r, t, 0:512]
                    for j in range(TOPK):
                        ins = stt(y, y_pairs[0:r, 0, j, :], w8[0:r, t, j:j + 1], y, ALU.mult, ALU.add)
                        if j < TOPK - 1:
                            run.run(ins)
                    ins.then_inc(sem("pairs_used"), 1)
                    job = ("comb", l, t)
                    lin.wait_full(dve, job)
                    y = ysh[0:r, t, 512:1024]
                    tt(y, y, psum[lin.bank(job)][0:r, :], ALU.add).then_inc(lin.is_free(job), 1)
                    dve.wait_ge(sem("pairs_used"), 3 * l + t + 1)
                    lin.wait_freed(dve, job)
                    run.run(stt(u[0:r, t, :], side(mgate, t), 1.0, ysh[0:r, t, :], ALU.add, ALU.mult))
                    run.run(stt(x[0:r, t, :], x[0:r, t, :], ALPHA, u[0:r, t, :], ALU.mult, ALU.add))
                    norm_tile(2 * l + 1, t)
                    if mod is not None:
                        dve.wait_ge(sem("ln_done"), 3 * (2 * l + 1) + t + 1)
                        modulate_tile(mod, t)

            moe_front(0)
            experts(0)
            overflow(0)
            combine(0, 2)

            turn.wait_full(dve, ("kv", 2, 1))
            modulate(3)
            for j in range(2):
                for t in range(3):
                    t0, r = TILES[t]
                    job = ("kT", j, t)
                    turn.wait_full(dve, job)
                    src = psum[turn.bank(job)][:, :].rearrange("p (h n) -> p h n", h=4)[:, :, 0:r]
                    dst = kTp[:, 4 * j:4 * j + 4, t0:t0 + r] if t < ST else kTs[:, 4 * j:4 * j + 4, :]
                    dve.tensor_copy(dst, src).then_inc(turn.is_free(job), 1)
            turn.wait_drained(dve, ("kT", 1, 2))
            wait(dve, "lf_full", 1)
            run.do(dve.memset(lf[:, :, :], 0.0))
            run.do(dve.memset(lf_t[:, :, :], 0.0))
            run.settle()
            for t in range(3):
                r = tile_rows(t)
                run.do(tt(lf[0:r, t, :], psum[5 + t][0:r, 0:FH], b_f[0:r, :], ALU.add))
            run.settle()
            stt(lf_t[:, :, :], lf[:, :, :], -1.0, lf[:, :, :], ALU.mult, ALU.min).then_inc(signal("lf_neg_ready"), 1)
            wait(dve, "lf_log_ready", 1)
            stt(lf[:, :, :], lf[:, :, :], 0.0, lf_t[:, :, :], ALU.min, ALU.subtract).then_inc(signal("lf_ready"), 1)
            wait(dve, "f_full", 1)
            run.do(dve.tensor_copy(f_p[:, 0, :], psum[5][:, 64:64 + FH]))
            run.do(dve.tensor_copy(f_p[:, 1, :], psum[6][:, 64:64 + FH]))
            run.do(ts(nf_s[0:64, :], psum[7][0:64, 64:64 + FH], -1.0, None, ALU.mult))
            run.do(dve.tensor_copy(f_s[0:64, :], psum[7][0:64, 64:64 + FH]))
            run.settle()
            dve.nop().then_inc(signal("f_ready"), 1)
            wait(dve, "fT_full", 1)
            dve.tensor_copy(fT, psum[7][0:FH, 0:SEQ]).then_inc(signal("fT_ready"), 1)

            dve.wait_ge(sem("consts_ready"), 2)
            for n in range(4):
                dve.wait_ge(sem(f"kv_out{n}"), 32)

            def p_out(m):
                h, qt = divmod(m, 2)
                wait(dve, "po_full", m + 1)
                run.run(dve.reciprocal(stat[:, 60 + qt:61 + qt], stat[:, 56 + m % 4:57 + m % 4]))
                ts(u[:, qt, h * HD:(h + 1) * HD], psum[(7, 4)[m % 2]][:, 0:HD], stat[:, 60 + qt:61 + qt], None, ALU.mult)\
                    .then_inc(signal("o_prompt_done"), 1)

            for n in range(2 * FH):
                h, qt = divmod(n, 2)
                wait(dve, "ps_full", n + 1)
                if n >= 4:
                    wait(dve, "p_turned", n - 3)
                s, bank = p_sc[:, n % 4, :], psum[n % 4]
                run.do(stt(s[:, qt * P:(qt + 1) * P], bank[:, qt * P:(qt + 1) * P], f_p[:, qt, h:h + 1], causal[:, :],
                           ALU.add, ALU.add))
                if qt:
                    run.do(ts(s[:, 0:P], bank[:, 0:P], f_p[:, qt, h:h + 1], None, ALU.add))
                run.settle()
                dve.tensor_reduce(stat[:, 52 + n % 4:53 + n % 4], s[:, 0:P * (qt + 1)], AX, ALU.max, negate=True)\
                   .then_inc(signal("p_max_ready"), 1)
                if n >= 3:
                    p_out(n - 3)
            for m in range(2 * FH - 3, 2 * FH):
                p_out(m)

            dve.wait_ge(sem("fox_cleared"), 1)
            dve.wait_ge(sem("fqc_loaded"), 128)

            def prepare(b, s):
                run.do(dve.tensor_copy(qz[:, s, :, 0:DT], qT[:, 4 * s:4 * s + 4, ds(b * DT + SEQ, DT)]))
                dve.tensor_copy(kn[:, s, :, :], kTs[:, 4 * s:4 * s + 4, ds(b * DT, DT)]).then_inc(sem("kn_ready"), 1)

            def keys_turned(g, i):
                dve.wait_ge(kt_full, g * 8 + (2 * i + 2))
                if i >= 2:
                    dve.wait_ge(sem("s_full"), g * 4 + (i - 1))
                dve.tensor_copy(kt_sb[:, i % 2, 512:1024], psum[1][:, :]).then_inc(sem("kt_dve"), 1)

            def group_out(g, s):
                dve.wait_ge(fo_full, g + 1)
                run.run(dve.reciprocal(stat[:, 20 + s:21 + s], stat[:, 18 + s:19 + s]))
                ts(og[:, s, :], psum[7][:, 256:256 + HD], stat[:, 20 + s:21 + s], None, ALU.mult)\
                    .then_inc(sem("og_ready"), 1)

            def probs_turned(g):
                dve.wait_ge(sem("pt_full"), g * 3 + 3)
                run.do(dve.tensor_copy(pTn[0:DT, :], psum[7][0:DT, 0:P]))
                dve.tensor_copy(pT[:, 4:8, :].rearrange("p a b -> p (a b)"), psum[6][:, :]).then_inc(sem("pt_dve"), 1)

            def fox_group(g, b, s, stored, first=False, last=False):
                keys_turned(g, 2)
                if not first:
                    probs_turned(g - 1)
                keys_turned(g, 3)
                if not first:
                    if stored is not None:
                        dve.wait_ge(sem(f"og_stored{1 - s}"), stored)
                    group_out(g - 1, 1 - s)
                if not last:
                    prepare(b + s, 1 - s)
                dve.wait_ge(sem("s_full"), g * 4 + 4)
                dve.wait_ge(sem(f"fetched{s}"), b * 80 + 80)
                run.run(tt(key_bias[s][:, PAST:], key_bias[s][:, PAST:], causal8[:, :], ALU.add))
                run.do(stt(sc[:, 0:512], psum[2][:, :], fqc[:, ds(g, 1)], key_bias[s][:, 0:512], ALU.add, ALU.add))
                run.do(stt(sc[:, 512:1024], psum[3][:, :], fqc[:, ds(g, 1)], key_bias[s][:, 512:1024], ALU.add, ALU.add))
                stt(sc[:, PAST:], psum[4][:, 0:DT], fqc[:, ds(g, 1)], key_bias[s][:, PAST:], ALU.add, ALU.add)\
                    .then_inc(sem("sc_ready"), 1)
                if not last:
                    keys_turned(g + 1, 0)
                run.settle()
                dve.wait_ge(sem("sc_ready"), g + 1)
                dve.tensor_reduce(stat[:, 16:17], sc, AX, ALU.max, negate=True).then_inc(sem("max_ready"), 1)
                if not last:
                    keys_turned(g + 1, 1)

            prepare(0, 0)
            keys_turned(0, 0)
            keys_turned(0, 1)
            fox_group(0, 0, 0, None, first=True)
            fox_group(1, 0, 1, None)
            fox_group(2, 1, 0, None)
            fox_group(3, 1, 1, 16)
            per, start = FOX_STEPS, run.n
            with dve.Fori(2, DB - 1) as b:
                run.base, run.n = b * (2 * per) + (start - 4 * per), 0
                for s in range(2):
                    fox_group(b * 2 + s, b, s, (b + (s - 1)) * 16)
                assert run.n == 2 * per, run.n
            run.base, run.n = start + (DB - 3) * 2 * per, 0
            for s in range(2):
                fox_group(2 * DB - 2 + s, DB - 1, s, (DB - 2 + s) * 16, last=(s == 1))
            probs_turned(2 * DB - 1)
            dve.wait_ge(sem("og_stored1"), 16 * (DB - 1))
            group_out(2 * DB - 1, 1)
            wait(dve, "o_prompt_done", 2 * FH)
            for _ in range(2):
                dve.nop().then_inc(sem("u_ready"), 1)
            dve.wait_ge(sem("og_loaded"), 16 * DB)
            dve.nop().then_inc(sem("u_ready"), 1)
            residual(2, "fox_wo", 4)
            moe_front(1)
            experts(1)
            overflow(1)
            combine(1)

        @block.tensor
        def _(pe):
            mm = pe.matmul

            def turn_stage(stage):
                for t, (t0, r) in enumerate(TILES):
                    u_ready(pe, stage, t)
                    for half in range(2):
                        job = (stage, t, half)
                        turn.wait_free(pe, job)
                        for i in range(4):
                            c = 4 * half + i
                            ins = pe.transpose(psum[turn.bank(job)][:, i * P:i * P + r],
                                               u[0:r, t, c:D:KT], ident[0:r, 0:r])
                        ins.then_inc(turn.is_full(job), 1)
                turn.wait_drained(pe, (stage, 2, 1))

            def product(job, t, unit):
                t0, r = TILES[t]
                lin.wait_free(pe, job)
                for c in range(KT):
                    ins = mm(psum[lin.bank(job)][0:r, :], uT[:, c, t0:t0 + r], ring_pair(unit)[:, c, :],
                             start=(c == 0), stop=(c == KT - 1))
                ins.then_inc(lin.is_full(job), 1)

            def linear(name, j):
                unit = weights_landed(pe, (name, j))
                for t in range(3):
                    product((name, j, t), t, unit)

            def projection(name):
                units = [weights_landed(pe, (name, j)) for j in range(2)]
                for t in range(3):
                    for j in range(2):
                        product((name, j, t), t, units[j])

            def ada(n):
                unit = weights_landed(pe, ("ada", n))
                adas.wait_free(pe, n)
                for c in range(KT):
                    for i in range(4):
                        ins = mm(psum[adas.bank(n)][32 * i:32 * i + 32, 0:P], cT[:, c, :],
                                 ring_pair(unit)[:, c, i * P:(i + 1) * P], start=(c == 0), stop=(c == KT - 1),
                                 tile_position=(0, 32 * i), skip_group_check=True)
                ins.then_inc(adas.is_full(n), 1)

            pe.wait_ge(sem("consts_ready"), 1)
            wait(pe, "c_silu", 1)
            for c in range(KT):
                ins = pe.transpose(psum[7][:, c * 16:c * 16 + 9], ln[0:9, 1, c:D:KT], ident[0:9, 0:9])
            ins.then_inc(signal("c_turned"), 1)
            wait(pe, "cT_ready", 1)
            for n in range(4):
                ada(n)
            pe.wait_ge(sem("lf_loaded"), 16)
            for h in range(FH):
                ins = pe.transpose(psum[turn.bank(("lf",))][:, h * 64:(h + 1) * 64], mgate[0:64, 0, h:D:FH],
                                   ident[0:64, 0:64])
            ins.then_inc(turn.is_full(("lf",)), 1)
            for n in range(4, FIRST_ADA):
                ada(n)
            turn.wait_freed(pe, ("lf",))
            pe.wait_ge(sem("consts_ready"), 2)
            for n in range(2):
                lin.wait_free(pe, ("suf", n))
                for page in range(PAGES - 1, 4 * n - 1, -1):
                    width = min(512, (page + 1) * P - n * 512)
                    first = (PAGES - 1 - page) * P + n * 512
                    ins = mm(psum[lin.bank(("suf", n))][0:64, 0:width], lf_pages[:, 0, page * 64:(page + 1) * 64],
                             later[:, first:first + width], start=(page == PAGES - 1), stop=(page == 4 * n),
                             skip_group_check=True)
                ins.then_inc(lin.is_full(("suf", n)), 1)
            turn_stage("gla")
            n = FIRST_ADA
            for j in range(W_IN_N // 512):
                linear("w_in", j)
                if j == 0:
                    pe.wait_ge(sem("small_loaded"), 16 * SMALL_LOADS)
                    for c in range(KT):
                        ins = mm(psum[7][0:RANK, 0:TOK], w_small[:, c, 0:RANK], uT[:, c, :],
                                 start=(c == 0), stop=(c == KT - 1))
                    ins.then_inc(signal("alr_full"), 1)
                if 1 <= j <= 3:
                    t0, r = TILES[j - 1]
                    wait(pe, "alrT_ready", 1)
                    if j > 1:
                        wait(pe, "z_neg_ready", j - 1)
                    mm(psum[7][0:r, :], alrT[:, t0:t0 + r], w_a2[:, :], start=True, stop=True)\
                        .then_inc(signal("z_full"), 1)
                for _ in range(ADA_AFTER[j]):
                    ada(n)
                    n += 1

            adas.wait_drained(pe, ADA_N - 1)
            lin.wait_drained(pe, ("w_in", 5, 2))
            for t, (t0, r) in enumerate(TILES):
                mask, same, group, groups = state_of(t)
                wait(pe, "la_ready", 3 if t == 0 else t + 1)
                if t:
                    wait(pe, "prompt_state_ready", 2 * t)
                mm(psum[0][0:r, :], mask[0:r, 0:r], la[0:r, t, :], start=True, stop=True)
                mm(psum[1][0:r, :], same[0:r, 0:r], la[0:r, t, :], start=True, stop=True)
                for h in range(GH):
                    ins = mm(psum[2][:, h * groups:(h + 1) * groups], la[0:r, t, h * GK:(h + 1) * GK], group[0:r, :],
                             start=True, stop=True)
                ins.then_inc(signal("dec_full"), 1)
                wait(pe, "qd_ready", t + 1)
                for h in range(GH):
                    ins = pe.transpose(psum[3][:, h * P:h * P + r], q[0:r, t, h * GK:(h + 1) * GK], ident[0:r, 0:r])
                ins.then_inc(signal("qdT_full"), 1)
                wait(pe, "kd_ready", t + 1)
                for h in range(GH):
                    ins = pe.transpose(psum[4][:, h * P:h * P + r], kd[0:r, h * GK:(h + 1) * GK], ident[0:r, 0:r])
                ins.then_inc(signal("kdT_full"), 1)
                wait(pe, "qdT_ready", t + 1)
                wait(pe, "kdT_ready", t + 1)
                if t:
                    u_ready(pe, "gla_o", t - 1)
                for h in range(GH):
                    ins = mm(psum[5][0:r, h * P:h * P + r], kdT[:, h, 0:r], qdT[:, h, 0:r], start=True, stop=True)
                ins.then_inc(signal("att_full"), 1)
                wait(pe, "att_ready", t + 1)
                wait(pe, "ke_ready", t + 1)

                def o_part(h, lhsT, rhs, start=False, stop=False):
                    return mm(psum[6 + h // 2][0:r, (h % 2) * GV:(h % 2 + 1) * GV], lhsT, rhs,
                              start=start and h % 2 == 0, stop=stop, skip_group_check=True)

                def update(h, lhsT, rhs, bank=0):
                    return mm(psum[bank + h // 2][:, (h % 2) * GV:(h % 2 + 1) * GV], lhsT, rhs, start=True, stop=True)

                for h in range(GH):
                    o_part(h, att[0:r, h, 0:r], v[0:r, t, h * GV:(h + 1) * GV], start=True)
                if t < ST:
                    for g in range(2):
                        c = 2 * t + g
                        if c:
                            wait(pe, "prompt_state_ready", c)
                            for h in range(GH):
                                ins = o_part(h, qz64[:, h, g * P:(g + 1) * P], s_p[:, h * GV:(h + 1) * GV], stop=(g == 1))
                            if g:
                                ins.then_inc(signal("o_full"), 1)
                        rows = slice(64 * g, 64 * g + 64)
                        for h in range(GH):
                            ins = update(h, k[rows, t, h * GK:(h + 1) * GK], v[rows, t, h * GV:(h + 1) * GV])
                        ins.then_inc(signal("upd_full"), 1)
                else:
                    for b in range(DB):
                        wait(pe, "kem_ready", b + 1)
                        pe.wait_ge(sem(f"state_loaded{b % 2}"), 16 * (b // 2 + 1))
                        for h in range(GH):
                            ins = o_part(h, qz8[:, h, b * 64:(b + 1) * 64], s_in[:, b % 2, h * GV:(h + 1) * GV],
                                         stop=(b == DB - 1))
                        if b == DB - 1:
                            ins.then_inc(signal("o_full"), 1)
                        if b >= 2:
                            wait(pe, "sup_ready", b - 1)
                        for h in range(GH):
                            ins = update(h, kem[b % 2][0:64, h * GK:(h + 1) * GK], v[0:64, t, h * GV:(h + 1) * GV],
                                         bank=3 * (b % 2))
                        ins.then_inc(signal("upd_full"), 1)
            wait(pe, "sup_ready", DB)
            turn_stage("gla_o")
            projection("gla_wo")

            def moe_front(l):
                stage = f"moe{l}"
                turn_stage(stage)
                pe.wait_ge(sem("router_loaded"), 16 * (2 + 3 * l))
                for t, (t0, r) in enumerate(TILES):
                    for c in range(KT):
                        ins = mm(psum[5 + t][0:r, 0:NE], uT[:, c, t0:t0 + r], w_small[:, c, :],
                                 start=(c == 0), stop=(c == KT - 1))
                    ins.then_inc(signal("router_full"), 1)
                unit = weights_landed(pe, ("sh_gu", l))
                for t, (t0, r) in enumerate(TILES):
                    product(("sh_gu", l, t), t, unit)
                    wait(pe, "chosen", 3 * l + t + 1)
                    if t == ST:
                        for s in range(3):
                            rs = tile_rows(s)
                            mm(psum[7][:, NE:2 * NE], ones[0:rs, :], sel[0:rs, s, :], start=(s == 0), stop=(s == 2))
                    for s in range(t):
                        mm(psum[5 + t][0:r, 0:NE], ones[:, 0:r], sel[:, s, :], start=(s == 0), stop=False)
                    mm(psum[5 + t][0:r, 0:NE], before[0:r, 0:r], sel[0:r, t, :], start=(t == 0), stop=True)\
                        .then_inc(signal("rank_full"), 1)
                unit = weights_landed(pe, ("sh_d", l))
                for t, (t0, r) in enumerate(TILES):
                    lin.wait_freed(pe, ("sh_gu", l, t))
                    job = ("h_sh", l, t)
                    turn.wait_free(pe, job)
                    for f in range(2):
                        ins = pe.transpose(psum[turn.bank(job)][:, f * P:f * P + r], h_sh[0:r, f * P:(f + 1) * P],
                                           ident[0:r, 0:r])
                    ins.then_inc(turn.is_full(job), 1)
                    turn.wait_freed(pe, job)
                    for j in range(2):
                        job = ("sh_d", l, j, t)
                        lin.wait_free(pe, job)
                        for f in range(2):
                            ins = mm(psum[lin.bank(job)][0:r, :], hT_sh[:, f, 0:r],
                                     ring[:, unit, f * D + j * 512:f * D + (j + 1) * 512], start=(f == 0), stop=(f == 1))
                        ins.then_inc(lin.is_full(job), 1)
                wait(pe, "tab2_ready", l + 1)
                job = ("places", l)
                turn.wait_free(pe, job)
                for b in range(BLOCKS):
                    ins = pe.transpose(psum[turn.bank(job)][:, b * NE:(b + 1) * NE],
                                       tab2[:, b, :, :].rearrange("e h r -> e (h r)"), ident[0:NE, 0:NE])
                ins.then_inc(turn.is_full(job), 1)
                turn.wait_drained(pe, job)
                lin.wait_drained(pe, ("sh_d", l, 1, 2))

            def turn_rows(s, event):
                for j in range(4):
                    ins = pe.transpose(psum[3 + s][:, j * P:(j + 1) * P], xg[:, s, j:512:4], ident[:, :])
                ins.then_inc(event, 1)

            def gate_up(s, gu, event):
                for kk in range(KT):
                    half, j = divmod(kk, 4)
                    for c in range(2):
                        ins = mm(psum[s][64 * c:64 * c + 64, 0:2 * P].rearrange("p (a n) -> p a n", a=2),
                                 xT[:, s, j * P + 64 * half:j * P + 64 * half + 64],
                                 gu[:, kk, :, c * P:(c + 1) * P], start=(kk == 0), stop=(kk == KT - 1),
                                 skip_group_check=True)
                ins.then_inc(event, 1)

            def turn_hidden(s, event):
                pe.transpose(psum[s][:, 2 * P:3 * P], hs[:, s, :], ident[:, :]).then_inc(event, 1)

            def down(s, w, event):
                for f in range(2):
                    for c in range(2):
                        ins = mm(psum[3 + s][64 * c:64 * c + 64, :], hT[:, s, 64 * f:64 * f + 64],
                                 w[:, f, c * 512:(c + 1) * 512], start=(f == 0), stop=(f == 1),
                                 skip_group_check=True)
                ins.then_inc(event, 1)

            def experts(l):
                base = l * NE
                loads = [[wr.items[(kind, l, s)][1] for s in range(3)] for kind in ("gate", "up", "down")]

                def rows(e, s, i, fresh=False):
                    pe.wait_ge(sem(f"xg_full{s}"), (i + (Y_STORED[l - 1][s] if l else 0) + 1) * 16)
                    if not fresh:
                        pe.wait_ge(sem("y_ready"), e + (base - 2))
                    turn_rows(s, sem("xT_full"))

                def one(e, s, i, first=False, fresh=False, last=False):
                    pe.wait_ge(sem("xT_ready"), e + (base + 1))
                    for n in range(2):
                        pe.wait_ge(unit_full[3 * s + n], (i + loads[n][s]) * 16)
                    gu = ring[:, 3 * s:3 * s + 2, :].rearrange("p a (k n) -> p k a n", n=FE)
                    gate_up(s, gu, h_full)
                    if not last:
                        s1 = (s + 1) % 3
                        rows(e + 1, s1, i + (s + 1) // 3, fresh=fresh)
                    if not first:
                        s0 = (s + 2) % 3
                        i0 = i if s else i - 1
                        pe.wait_ge(unit_full[3 * s0 + 2], (i0 + loads[2][s0]) * 16)
                        pe.wait_ge(sem("hT_ready"), e + base)
                        down(s0, ring[:, 3 * s0 + 2, :].rearrange("p (f n) -> p f n", f=2), y_full)
                    pe.wait_ge(sem("h_ready"), e + (base + 1))
                    turn_hidden(s, sem("hT_full"))

                wait(pe, "index_ready", l + 1)
                rows(0, 0, 0, fresh=True)
                for e in range(3):
                    one(e, e, 0, first=(e == 0), fresh=(e < 2))
                with pe.Fori(1, NE // 3) as i:
                    for s in range(3):
                        one(i * 3 + s, s, i)
                one(NE - 1, 0, NE // 3, last=True)
                pe.wait_ge(unit_full[2], (NE // 3 + loads[2][0]) * 16)
                pe.wait_ge(sem("hT_ready"), base + NE)
                down(0, ring[:, 2, :].rearrange("p (f n) -> p f n", f=2), y_full)

            def overflow(l):
                wait(pe, "over_ready", l + 1)
                done = sem(f"over_pe{l}")

                def body(j):
                    pe.wait_ge(sem(f"over_xg{l}"), j * 16 + 16)
                    pe.wait_ge(sem("y_ready"), NE * (l + 1))
                    turn_rows(0, done)
                    pe.wait_ge(sem(f"over_dve{l}"), j * 3 + 1)
                    pe.wait_ge(sem(f"over_w{l}"), j * 48 + 48)
                    for kk in range(KT):
                        half, jj = divmod(kk, 4)
                        for c in range(2):
                            for a, w in enumerate((ov_gate, ov_up)):
                                ins = mm(psum[0][64 * c:64 * c + 64, a * P:(a + 1) * P],
                                         xT[:, 0, jj * P + 64 * half:jj * P + 64 * half + 64],
                                         w[:, :, :].rearrange("p a (k n) -> p (a k) n", n=FE)
                                         [:, kk, c * P:(c + 1) * P], start=(kk == 0 and a == 0),
                                         stop=(kk == KT - 1), skip_group_check=True)
                    ins.then_inc(done, 1)
                    pe.wait_ge(sem(f"over_dve{l}"), j * 3 + 2)
                    turn_hidden(0, done)
                    pe.wait_ge(sem(f"over_dve{l}"), j * 3 + 3)
                    down(0, ov_down, done)

                over_blocks(pe, body)

            def combine(l):
                wait(pe, "diag_ready", l + 1)
                for t in range(3):
                    r = tile_rows(t)
                    pe.wait_ge(sem("pairs_loaded1"), 16 * (3 * l + t + 1))
                    job = ("comb", l, t)
                    lin.wait_free(pe, job)
                    for j in range(TOPK):
                        ins = mm(psum[lin.bank(job)][0:r, :], diag[t][:, j, :], y_pairs[0:r, 1, j, :],
                                 start=(j == 0), stop=(j == TOPK - 1))
                    ins.then_inc(lin.is_full(job), 1)

            moe_front(0)
            experts(0)
            overflow(0)
            combine(0)

            turn_stage("kv")
            pe.wait_ge(sem("router_loaded"), 48)
            for t, (t0, r) in enumerate(TILES):
                for c in range(KT):
                    ins = mm(psum[5 + t][0:r, 0:FH], uT[:, c, t0:t0 + r], w_small[:, c, 0:FH],
                             start=(c == 0), stop=(c == KT - 1))
            ins.then_inc(signal("lf_full"), 1)

            def turn_new_keys(j, t):
                slot = (3 * j + t) % 4
                r = tile_rows(t)
                lin.wait_freed(pe, ("kv", j, t))
                job = ("kT", j, t)
                turn.wait_free(pe, job)
                for i in range(4):
                    ins = pe.transpose(psum[turn.bank(job)][:, i * P:i * P + r],
                                       kv_rows[0:r, slot, i * P:(i + 1) * P], ident[0:r, 0:r])
                ins.then_inc(turn.is_full(job), 1)

            for j in range(4):
                unit = weights_landed(pe, ("kv", j))
                for t in range(3):
                    product(("kv", j, t), t, unit)
                    n = 3 * j + t - 1
                    if 0 <= n < 6:
                        turn_new_keys(n // 3, n % 3)
            turn_stage("fox")
            wait(pe, "lf_ready", 1)
            mm(psum[5][:, 64:64 + FH], upto[:, :], lf[:, 0, :], start=True, stop=True)
            mm(psum[6][:, 64:64 + FH], ones[:, :], lf[:, 0, :], start=True, stop=False)
            mm(psum[6][:, 64:64 + FH], upto[:, :], lf[:, 1, :], start=False, stop=True)
            mm(psum[7][0:64, 64:64 + FH], upto8[:, :], lf[0:64, 2, :], start=True, stop=True).then_inc(signal("f_full"), 1)
            wait(pe, "f_ready", 1)
            for t in range(2):
                ins = pe.transpose(psum[7][0:FH, t * P:(t + 1) * P], f_p[:, t, :], ident[:, :])
            ins.then_inc(signal("fT_full"), 1)
            for h in range(FH):
                j, i = divmod(h, 4)
                unit = weights_landed(pe, ("w_q", j))
                job = ("w_q", h)
                lin.wait_free(pe, job)
                for c in range(KT):
                    ins = mm(psum[lin.bank(job)][:, 0:TOK], ring_pair(unit)[:, c, i * P:(i + 1) * P], uT[:, c, :],
                             start=(c == 0), stop=(c == KT - 1))
                ins.then_inc(lin.is_full(job), 1)
            lin.wait_drained(pe, ("w_q", 7))

            wait(pe, "fT_ready", 1)
            pe.wait_ge(sem("fox_cleared"), 1)
            turn.wait_drained(pe, ("kT", 1, 2))

            def prompt_scores(n):
                h, qt = divmod(n, 2)
                nk = P * (qt + 1)
                bank = psum[n % 4]
                if n >= 4:
                    wait(pe, "p_max_ready", n - 3)
                mm(bank[:, 0:nk], qT[:, h, qt * P:(qt + 1) * P], kTp[:, h, 0:nk], start=True, stop=False)
                mm(bank[:, 0:nk], selneg[:, h, :], fT[:, 0:nk], start=False, stop=True).then_inc(signal("ps_full"), 1)

            def prompt_turn(m):
                wait(pe, "p_exp_ready", m + 1)
                for a in range(m % 2 + 1):
                    ins = pe.transpose(psum[5 + m % 2][:, a * P:(a + 1) * P], p_sc[:, m % 4, a * P:(a + 1) * P], ident[:, :])
                ins.then_inc(signal("p_turned"), 1)

            def prompt_values(m):
                h, qt = divmod(m, 2)
                wait(pe, "p_T_ready", m + 1)
                if m >= 2:
                    wait(pe, "o_prompt_done", m - 1)
                for a in range(qt + 1):
                    ins = mm(psum[(7, 4)[m % 2]][:, 0:HD], p_T[:, m % 4, a, :], vp[:, a, h * HD:(h + 1) * HD],
                             start=(a == 0), stop=(a == qt))
                ins.then_inc(signal("po_full"), 1)

            for n in range(2 * FH + 3):
                if n < 2 * FH:
                    prompt_scores(n)
                if 2 <= n < 2 * FH + 2:
                    prompt_turn(n - 2)
                if n >= 3:
                    prompt_values(n - 3)
            wait(pe, "o_prompt_done", 2 * FH)

            k_loads = [wr.items[("fox_k", s)][1] for s in range(2)]
            v_loads = [wr.items[("fox_v", s)][1] for s in range(2)]

            def turn_keys(g, i, s, b):
                if i == 0:
                    pe.wait_ge(unit_full[4 * s], (b * PAGES + k_loads[s]) * 16)
                for n in range(2):
                    if isinstance(g, bass.RuntimeValue) or g or i:
                        pe.wait_ge(sem(("kt_act", "kt_dve")[n]), g * 4 + i)
                    for a in range(4):
                        ins = pe.transpose(psum[n][:, a * P:(a + 1) * P],
                                           ring_pair(4 * s)[:, 4 * n + a, i * P:(i + 1) * P], ident[:, :])
                    ins.then_inc(kt_full, 1)

            def head_scores(g, i, s):
                pe.wait_ge(sem("kt_act"), g * 4 + (i + 1))
                pe.wait_ge(sem("kt_dve"), g * 4 + (i + 1))
                if i == 0:
                    pe.wait_ge(sem("kn_ready"), g + 1)
                    if isinstance(g, bass.RuntimeValue) or g:
                        pe.wait_ge(sem("sc_ready"), g)
                for n in range(2):
                    mm(psum[2 + n][32 * i:32 * i + 32, :], qz[:, s, i, :], kt_sb[:, i % 2, n * 512:(n + 1) * 512],
                       start=True, stop=True, tile_position=(0, 32 * i))
                mm(psum[4][32 * i:32 * i + 32, 0:DT], qz[:, s, i, :], kn[:, s, i, :], start=True, stop=True,
                   tile_position=(0, 32 * i)).then_inc(sem("s_full"), 1)

            def turn_probs(g):
                pe.wait_ge(sem("exp_ready"), g + 1)
                for n in range(2):
                    for a in range(4):
                        ins = pe.transpose(psum[5 + n][:, a * P:(a + 1) * P],
                                           sc[:, (4 * n + a) * P:(4 * n + a + 1) * P], ident[:, :])
                    ins.then_inc(sem("pt_full"), 1)
                if isinstance(g, bass.RuntimeValue) or g:
                    pe.wait_ge(sem("og_ready"), g)
                pe.transpose(psum[7][0:DT, 0:P], sc[:, PAST:CTX], ident[:, :]).then_inc(sem("pt_full"), 1)

            def values(g, s, b):
                pe.wait_ge(unit_full[4 * s + 2], (b * PAGES + v_loads[s]) * 16)
                pe.wait_ge(sem("pt_act"), g + 1)
                pe.wait_ge(sem("pt_dve"), g + 1)
                for a in range(PAGES):
                    for i in range(4):
                        mm(psum[7][32 * i:32 * i + 32, 256:256 + HD], pT[:, a, 32 * i:32 * i + 32],
                           ring_pair(4 * s + 2)[:, a, i * P:(i + 1) * P], start=(a == 0), stop=False,
                           tile_position=(0, 32 * i), skip_group_check=True)
                for i in range(4):
                    ins = mm(psum[7][32 * i:32 * i + 32, 256:256 + HD], pTn[0:DT, 32 * i:32 * i + 32],
                             vn[0:DT, s, i * P:(i + 1) * P], start=False, stop=True,
                             tile_position=(0, 32 * i), skip_group_check=True)
                ins.then_inc(fo_full, 1)

            def fox_group(g, s, b, b0, first=False):
                turn_keys(g, 0, s, b)
                turn_keys(g, 1, s, b)
                head_scores(g, 0, s)
                turn_keys(g, 2, s, b)
                if not first:
                    turn_probs(g - 1)
                head_scores(g, 1, s)
                turn_keys(g, 3, s, b)
                if not first:
                    values(g - 1, 1 - s, b0)
                head_scores(g, 2, s)
                head_scores(g, 3, s)

            fox_group(0, 0, 0, 0, first=True)
            fox_group(1, 1, 0, 0)
            with pe.Fori(1, DB) as b:
                for s in range(2):
                    fox_group(b * 2 + s, s, b, b + (s - 1))
            turn_probs(2 * DB - 1)
            values(2 * DB - 1, 1, DB - 1)

            turn_stage("fox_o")
            projection("fox_wo")
            moe_front(1)
            experts(1)
            overflow(1)
            combine(1)


def kernel(**inputs):
    import concourse.bacc as bacc
    from concourse.bass_utils import run_bass_kernel_spmd

    nc = bacc.Bacc("TRN2", target_bir_lowering=False, num_devices=1)
    arrays, w, o = {}, {}, {}
    for name in INPUTS:
        a = np.ascontiguousarray(inputs[name])
        arrays[f"in_{name}"] = a
        w[name] = nc.dram_tensor(f"in_{name}", a.shape, mybir.dt.from_np(a.dtype), kind="ExternalInput").ap()
    for name, shape in OUTPUTS:
        o[name] = nc.dram_tensor(f"out_{name}", shape, F32, kind="ExternalOutput").ap()
    hybrid_trunk_step(nc, w, o)
    r = run_bass_kernel_spmd(nc, [arrays], core_ids=[0])
    return tuple(r.results[0][f"out_{name}"] for name, _ in OUTPUTS)
```
